# Optimizing a Trainium2 kernel written in Bass

```python
import jax, jax.numpy as jnp
from jax import lax
import numpy as np

D_MODEL = 1024
BATCH = 1
SEQ = 256
DEPTH = 2

N_A_LAYERS = DEPTH // 2
N_B_LAYERS = DEPTH - N_A_LAYERS
LRU_WIDTH = D_MODEL
LRU_HEADS = 8
LRU_BLOCK = LRU_WIDTH // LRU_HEADS
CONV_WIDTH = 4
LRU_C = 8.0
HEAD_DIM = 64
N_HEADS = D_MODEL // HEAD_DIM
N_KV_GROUPS = 4
HEADS_PER_GROUP = N_HEADS // N_KV_GROUPS
CMP_BLOCK = 32
CMP_STRIDE = 16
CMP_HIDDEN = 256
SLC_BLOCK = 64
SLC_TOPK = 16
N_LOCAL_BLOCKS = 2
WINDOW = 512
Q_BLOCK = 128
ROPE_THETA = 10000.0
FFN_HIDDEN = ((8 * D_MODEL // 3 + 255) // 256) * 256
EPS = 1e-6
NEG = -1e30
FORCE = 1e30


def rmsnorm(x, g):
    xf = x.astype(jnp.float32)
    y = xf * lax.rsqrt(jnp.mean(xf * xf, axis=-1, keepdims=True) + EPS)
    return (y * g.astype(jnp.float32)).astype(x.dtype)

def rope(x, pos):
    half = HEAD_DIM // 2
    freqs = jnp.power(ROPE_THETA, -jnp.arange(half, dtype=jnp.float32) / half)
    ang = pos.astype(jnp.float32)[:, None] * freqs[None, :]
    cos = jnp.cos(ang)[:, None, :]
    sin = jnp.sin(ang)[:, None, :]
    xf = x.astype(jnp.float32)
    x1, x2 = xf[..., :half], xf[..., half:]
    return jnp.concatenate([x1 * cos - x2 * sin, x1 * sin + x2 * cos], axis=-1).astype(x.dtype)

def masked_softmax(s, mask):
    s = jnp.where(mask, s, NEG)
    return jax.nn.softmax(s, axis=-1) * mask

def causal_conv(x, w, b):
    S = x.shape[1]
    xp = jnp.pad(x, ((0, 0), (CONV_WIDTH - 1, 0), (0, 0)))
    out = b
    for k in range(CONV_WIDTH):
        out = out + xp[:, k:k + S] * w[k]
    return out

def rg_lru(x, gate_w, gate_b, lam):
    B, S, R = x.shape
    xf = x.astype(jnp.float32)
    xh = xf.reshape(B, S, LRU_HEADS, LRU_BLOCK)
    gates = jnp.einsum('bshi,khij->kbshj', xh, gate_w.astype(jnp.float32)).reshape(2, B, S, R)
    gates = gates + gate_b.astype(jnp.float32)[:, None, None, :]
    r = jax.nn.sigmoid(gates[0])
    i = jax.nn.sigmoid(gates[1])
    log_a = -LRU_C * jax.nn.softplus(-lam.astype(jnp.float32)) * r
    a = jnp.exp(log_a)
    bterm = jnp.sqrt(-jnp.expm1(2.0 * log_a)) * (i * xf)

    def combine(e1, e2):
        a1, b1 = e1
        a2, b2 = e2
        return a1 * a2, a2 * b1 + b2

    _, h = lax.associative_scan(combine, (a, bterm), axis=1)
    return h.astype(x.dtype)

def recurrent_block(h, norm_g, w_in, conv_w, conv_b, gate_w, gate_b, lam, w_out):
    u = rmsnorm(h, norm_g)
    z = u @ w_in
    y = jax.nn.gelu(z[..., :LRU_WIDTH])
    xr = causal_conv(z[..., LRU_WIDTH:], conv_w, conv_b)
    hr = rg_lru(xr, gate_w, gate_b, lam)
    return (y * hr) @ w_out

def swiglu(h, norm_g, w_in, w_out):
    u = rmsnorm(h, norm_g)
    gu = u @ w_in
    return (jax.nn.silu(gu[..., :FFN_HIDDEN]) * gu[..., FFN_HIDDEN:]) @ w_out

def compress(t, pos_emb, w1, b1, w2, b2):
    B, S = t.shape[0], t.shape[1]
    n_cmp = (S - CMP_BLOCK) // CMP_STRIDE + 1
    idx = jnp.arange(n_cmp)[:, None] * CMP_STRIDE + jnp.arange(CMP_BLOCK)[None, :]
    blocks = t[:, idx] + pos_emb[:, None, :]
    blocks = blocks.transpose(0, 1, 3, 2, 4).reshape(B, n_cmp, N_KV_GROUPS, CMP_BLOCK * HEAD_DIM)
    return jax.nn.gelu(blocks @ w1 + b1) @ w2 + b2

def shared_kv(h, kv_norm, kv_w, k_norm, cmp_pos, cmp_w1, cmp_b1, cmp_w2, cmp_b2):
    B, S, _ = h.shape
    u = rmsnorm(h, kv_norm)
    kv = (u @ kv_w).reshape(B, S, 6, N_KV_GROUPS, HEAD_DIM)
    k_c, v_c, k_s, v_s, k_w, v_w = [kv[:, :, j] for j in range(6)]
    pos = jnp.arange(S)
    k_s = rope(rmsnorm(k_s, k_norm[1]), pos)
    k_w = rope(rmsnorm(k_w, k_norm[2]), pos)
    n_cmp = (S - CMP_BLOCK) // CMP_STRIDE + 1
    cmp_last = jnp.arange(n_cmp) * CMP_STRIDE + CMP_BLOCK - 1
    k_cmp = compress(k_c, cmp_pos[0], cmp_w1[0], cmp_b1[0], cmp_w2[0], cmp_b2[0])
    k_cmp = rope(rmsnorm(k_cmp, k_norm[0]), cmp_last)
    v_cmp = compress(v_c, cmp_pos[1], cmp_w1[1], cmp_b1[1], cmp_w2[1], cmp_b2[1])
    return (k_cmp, v_cmp, k_s, v_s, k_w, v_w)

def nsa_single(args):
    q, gate, k_cmp, v_cmp, k_slc, v_slc, k_win, v_win = args
    S = q.shape[0]
    G, Hg, dk = N_KV_GROUPS, HEADS_PER_GROUP, HEAD_DIM
    n_cmp = k_cmp.shape[0]
    n_slc = S // SLC_BLOCK
    top_n = min(SLC_TOPK, n_slc)
    scale = HEAD_DIM ** -0.5
    cmp_start = jnp.arange(n_cmp) * CMP_STRIDE
    cmp_last = cmp_start + CMP_BLOCK - 1
    slc_start = jnp.arange(n_slc) * SLC_BLOCK
    overlap = jnp.clip(jnp.minimum(cmp_start[:, None] + CMP_BLOCK, slc_start[None, :] + SLC_BLOCK)
                       - jnp.maximum(cmp_start[:, None], slc_start[None, :]), 0).astype(jnp.float32) / CMP_BLOCK
    kb = k_slc.reshape(n_slc, SLC_BLOCK, G, dk).transpose(2, 0, 1, 3)
    vb = v_slc.reshape(n_slc, SLC_BLOCK, G, dk).transpose(2, 0, 1, 3)
    kw_p = jnp.pad(k_win, ((WINDOW, 0), (0, 0), (0, 0)))
    vw_p = jnp.pad(v_win, ((WINDOW, 0), (0, 0), (0, 0)))
    qg = q.reshape(S, G, Hg, dk)
    blk = jnp.arange(n_slc)
    grp = jnp.arange(G)[None, :, None]

    def block(qb):
        s0 = qb * Q_BLOCK
        qt = lax.dynamic_slice_in_dim(qg, s0, Q_BLOCK, 0)
        gt = lax.dynamic_slice_in_dim(gate, s0, Q_BLOCK, 0).reshape(Q_BLOCK, 3, G, Hg)
        t = s0 + jnp.arange(Q_BLOCK)
        s = jnp.einsum('tghd,cgd->tghc', qt, k_cmp).astype(jnp.float32) * scale
        p_cmp = masked_softmax(s, (cmp_last[None, :] <= t[:, None])[:, None, None, :])
        o_cmp = jnp.einsum('tghc,cgd->tghd', p_cmp.astype(v_cmp.dtype), v_cmp)
        imp = jnp.einsum('tgc,cj->tgj', p_cmp.sum(axis=2), overlap)
        cur = (t // SLC_BLOCK)[:, None]
        causal_blk = blk[None, :] <= cur
        forced = (blk[None, :] == 0) | (causal_blk & (cur - blk[None, :] < N_LOCAL_BLOCKS))
        score = jnp.where(forced[:, None, :], FORCE, jnp.where(causal_blk[:, None, :], imp, NEG))
        _, idx = lax.top_k(score, top_n)
        ksel = kb[grp, idx].reshape(Q_BLOCK, G, top_n * SLC_BLOCK, dk)
        vsel = vb[grp, idx].reshape(Q_BLOCK, G, top_n * SLC_BLOCK, dk)
        kpos = (idx[..., None] * SLC_BLOCK + jnp.arange(SLC_BLOCK)).reshape(Q_BLOCK, G, top_n * SLC_BLOCK)
        s = jnp.einsum('tghd,tgkd->tghk', qt, ksel).astype(jnp.float32) * scale
        p = masked_softmax(s, (kpos <= t[:, None, None])[:, :, None, :])
        o_slc = jnp.einsum('tghk,tgkd->tghd', p.astype(vsel.dtype), vsel)
        kw = lax.dynamic_slice_in_dim(kw_p, s0, WINDOW + Q_BLOCK, 0)
        vw = lax.dynamic_slice_in_dim(vw_p, s0, WINDOW + Q_BLOCK, 0)
        kp = s0 - WINDOW + jnp.arange(WINDOW + Q_BLOCK)
        mw = (kp[None, :] <= t[:, None]) & (kp[None, :] > t[:, None] - WINDOW) & (kp[None, :] >= 0)
        s = jnp.einsum('tghd,kgd->tghk', qt, kw).astype(jnp.float32) * scale
        p = masked_softmax(s, mw[:, None, None, :])
        o_win = jnp.einsum('tghk,kgd->tghd', p.astype(vw.dtype), vw)
        o = gt[:, 0][..., None] * o_cmp + gt[:, 1][..., None] * o_slc + gt[:, 2][..., None] * o_win
        return o.reshape(Q_BLOCK, N_HEADS, dk)

    out = lax.map(block, jnp.arange(S // Q_BLOCK))
    return out.reshape(S, N_HEADS, dk)

def nsa_layer(h, norm_g, w_in, gate_b, q_norm_g, w_out, k_cmp, v_cmp, k_s, v_s, k_w, v_w):
    B, S, _ = h.shape
    u = rmsnorm(h, norm_g)
    z = u @ w_in
    q = z[..., :N_HEADS * HEAD_DIM].reshape(B, S, N_HEADS, HEAD_DIM)
    q = rope(rmsnorm(q, q_norm_g), jnp.arange(S))
    gates = jax.nn.sigmoid(z[..., N_HEADS * HEAD_DIM:] + gate_b).reshape(B, S, 3, N_HEADS)
    o = lax.map(nsa_single, (q, gates, k_cmp, v_cmp, k_s, v_s, k_w, v_w))
    return o.reshape(B, S, N_HEADS * HEAD_DIM) @ w_out

def first_inputs(seed: int = 0) -> dict:
    key = jax.random.key(seed)
    ks = jax.random.split(key, 26)

    def nrm(k, shape, scale):
        return jax.random.normal(k, shape, jnp.float32) * scale

    def gain(k, shape):
        return 1.0 + 0.02 * jax.random.normal(k, shape, jnp.float32)

    R, NA, NB = LRU_WIDTH, N_A_LAYERS, N_B_LAYERS
    u = jax.random.uniform(ks[7], (NA, R), jnp.float32, minval=0.9, maxval=0.999)
    s = u ** (1.0 / LRU_C)
    a_lambda = jnp.log(s) - jnp.log1p(-s)
    nq = N_HEADS * HEAD_DIM + 3 * N_HEADS
    return {
        "x": nrm(ks[0], (BATCH, SEQ, D_MODEL), 1.0),
        "a_norm": gain(ks[1], (NA, D_MODEL)),
        "a_w_in": nrm(ks[2], (NA, D_MODEL, 2 * R), D_MODEL ** -0.5),
        "a_conv_w": nrm(ks[3], (NA, CONV_WIDTH, R), CONV_WIDTH ** -0.5),
        "a_conv_b": nrm(ks[4], (NA, R), 0.01),
        "a_gate_w": nrm(ks[5], (NA, 2, LRU_HEADS, LRU_BLOCK, LRU_BLOCK), LRU_BLOCK ** -0.5),
        "a_gate_b": nrm(ks[6], (NA, 2, R), 0.01),
        "a_lambda": a_lambda,
        "a_w_out": nrm(ks[8], (NA, R, D_MODEL), R ** -0.5),
        "kv_norm": gain(ks[9], (D_MODEL,)),
        "kv_w": nrm(ks[10], (D_MODEL, 6 * N_KV_GROUPS * HEAD_DIM), D_MODEL ** -0.5),
        "k_norm": gain(ks[11], (3, HEAD_DIM)),
        "cmp_pos": nrm(ks[12], (2, CMP_BLOCK, HEAD_DIM), 0.02),
        "cmp_w1": nrm(ks[13], (2, CMP_BLOCK * HEAD_DIM, CMP_HIDDEN), (CMP_BLOCK * HEAD_DIM) ** -0.5),
        "cmp_b1": nrm(ks[14], (2, CMP_HIDDEN), 0.01),
        "cmp_w2": nrm(ks[15], (2, CMP_HIDDEN, HEAD_DIM), CMP_HIDDEN ** -0.5),
        "cmp_b2": nrm(ks[16], (2, HEAD_DIM), 0.01),
        "b_norm": gain(ks[17], (NB, D_MODEL)),
        "b_w_in": nrm(ks[18], (NB, D_MODEL, nq), D_MODEL ** -0.5),
        "b_gate_b": nrm(ks[19], (NB, 3 * N_HEADS), 0.01),
        "q_norm": gain(ks[20], (NB, HEAD_DIM)),
        "b_w_out": nrm(ks[21], (NB, N_HEADS * HEAD_DIM, D_MODEL), (N_HEADS * HEAD_DIM) ** -0.5),
        "f_norm": gain(ks[22], (DEPTH, D_MODEL)),
        "f_w_in": nrm(ks[23], (DEPTH, D_MODEL, 2 * FFN_HIDDEN), D_MODEL ** -0.5),
        "f_w_out": nrm(ks[24], (DEPTH, FFN_HIDDEN, D_MODEL), FFN_HIDDEN ** -0.5),
    }

def first_block(x, a_norm, a_w_in, a_conv_w, a_conv_b, a_gate_w, a_gate_b, a_lambda, a_w_out,
              kv_norm, kv_w, k_norm, cmp_pos, cmp_w1, cmp_b1, cmp_w2, cmp_b2,
              b_norm, b_w_in, b_gate_b, q_norm, b_w_out,
              f_norm, f_w_in, f_w_out):
    h = x
    shared = None
    for layer in range(DEPTH):
        if layer < N_A_LAYERS:
            i = layer
            h = h + recurrent_block(h, a_norm[i], a_w_in[i], a_conv_w[i], a_conv_b[i],
                                    a_gate_w[i], a_gate_b[i], a_lambda[i], a_w_out[i])
        else:
            if layer == N_A_LAYERS:
                shared = shared_kv(h, kv_norm, kv_w, k_norm, cmp_pos, cmp_w1, cmp_b1, cmp_w2, cmp_b2)
            j = layer - N_A_LAYERS
            h = h + nsa_layer(h, b_norm[j], b_w_in[j], b_gate_b[j], q_norm[j], b_w_out[j], *shared)
        h = h + swiglu(h, f_norm[layer], f_w_in[layer], f_w_out[layer])
    return h


HGRN_HEADS = 4
HGRN_HEAD_DIM = 128
HGRN_WIDTH = HGRN_HEADS * HGRN_HEAD_DIM
HGRN_CHUNK = 64
SB_HEADS = 8
SB_HEAD_DIM = 64
SB_WIDTH = SB_HEADS * SB_HEAD_DIM
SB_BLOCK = 128
FFN_DIM = 3584
N_EXPERTS = 8
TOP_K = 2
RMS_EPS = 1e-6
IN_WIDTH = 4 * HGRN_WIDTH + 3 * SB_WIDTH + 2 * D_MODEL


def _split_points():
    sizes = [HGRN_WIDTH] * 4 + [SB_WIDTH] * 3 + [D_MODEL] * 2
    pts, acc = [], 0
    for s in sizes[:-1]:
        acc += s
        pts.append(acc)
    return pts

def rms_norm(x, g):
    x32 = x.astype(jnp.float32)
    y = x32 * lax.rsqrt(jnp.mean(x32 * x32, axis=-1, keepdims=True) + RMS_EPS)
    return (y * g.astype(jnp.float32)).astype(x.dtype)

def hgrn2_chunkwise(q, k, v, log_f):
    B, S, H, Dk = q.shape
    Dv = v.shape[-1]
    n = S // HGRN_CHUNK

    def to_chunks(t):
        return t.reshape(B, n, HGRN_CHUNK, H, t.shape[-1]).transpose(1, 0, 3, 2, 4)

    causal = jnp.tril(jnp.ones((HGRN_CHUNK, HGRN_CHUNK), dtype=bool))[:, :, None]

    def step(s_prev, inp):
        qb, kb, vb, fb = inp
        b = jnp.cumsum(fb, axis=2)
        diff = b[:, :, :, None, :] - b[:, :, None, :, :]
        decay = jnp.exp(jnp.where(causal, diff, -jnp.inf))
        scores = jnp.einsum('bhtd,bhtsd,bhsd->bhts', qb, decay, kb)
        o = (jnp.einsum('bhts,bhsv->bhtv', scores, vb)
             + jnp.einsum('bhtd,bhdv->bhtv', qb * jnp.exp(b), s_prev))
        b_last = b[:, :, -1:, :]
        s_new = (jnp.exp(b_last[:, :, 0, :])[..., None] * s_prev
                 + jnp.einsum('bhsd,bhsv->bhdv', kb * jnp.exp(b_last - b), vb))
        return s_new, o

    s0 = jnp.zeros((B, H, Dk, Dv), jnp.float32)
    _, o = lax.scan(step, s0, (to_chunks(q), to_chunks(k), to_chunks(v), to_chunks(log_f)))
    return o.transpose(1, 0, 3, 2, 4).reshape(B, S, H, Dv)

def stick_breaking_attention(q, k, v):
    B, S, H, d = q.shape
    scale = d ** -0.5
    outs = []
    for blk in range(S // SB_BLOCK):
        t0 = blk * SB_BLOCK
        kl = t0 + SB_BLOCK
        z = jnp.einsum('bthd,bshd->bhts', q[:, t0:kl], k[:, :kl]).astype(jnp.float32) * scale
        t_idx = t0 + jnp.arange(SB_BLOCK)[:, None]
        s_idx = jnp.arange(kl)[None, :]
        strict = s_idx < t_idx
        log_keep = jnp.where(strict, jax.nn.log_sigmoid(-z), 0.0)
        after = lax.cumsum(log_keep, axis=3, reverse=True) - log_keep
        w = jnp.where(strict, jnp.exp(jax.nn.log_sigmoid(z) + after), 0.0)
        outs.append(jnp.einsum('bhts,bshd->bthd', w, v[:, :kl].astype(jnp.float32)))
    return jnp.concatenate(outs, axis=1)

def hybrid_mixer(h, w_in, lb, out_norm, w_branch_a, w_branch_b, w_out):
    B, S, _ = h.shape
    proj = jnp.einsum('bsd,dn->bsn', h, w_in)
    hq, hf, hi, hog, sq, sk, sv, ga, gb = jnp.split(proj, _split_points(), axis=-1)

    def hh(t):
        return t.reshape(B, S, HGRN_HEADS, HGRN_HEAD_DIM).astype(jnp.float32)
    lb = lb.reshape(HGRN_HEADS, HGRN_HEAD_DIM)
    zf = hh(hf)
    log_f = jnp.logaddexp(jnp.log(lb), jnp.log1p(-lb) + jax.nn.log_sigmoid(zf))
    k_in = (1.0 - lb) * jax.nn.sigmoid(-zf)
    o_a = hgrn2_chunkwise(jax.nn.silu(hh(hq)), k_in, hh(hi), log_f)
    o_a = rms_norm(o_a, out_norm) * jax.nn.silu(hh(hog))
    o_a = o_a.reshape(B, S, HGRN_WIDTH).astype(h.dtype)

    def sh(t):
        return t.reshape(B, S, SB_HEADS, SB_HEAD_DIM)
    o_b = stick_breaking_attention(sh(sq), sh(sk), sh(sv)).reshape(B, S, SB_WIDTH).astype(h.dtype)

    y = (jax.nn.sigmoid(ga) * jnp.einsum('bsn,nd->bsd', o_a, w_branch_a)
         + jax.nn.sigmoid(gb) * jnp.einsum('bsn,nd->bsd', o_b, w_branch_b))
    return jnp.einsum('bsd,de->bse', y, w_out)

def swiglu_2(h, w_gate, w_up, w_down):
    a = jnp.einsum('...d,df->...f', h, w_gate)
    u = jnp.einsum('...d,df->...f', h, w_up)
    return jnp.einsum('...f,fd->...d', jax.nn.silu(a) * u, w_down)

def moe_swiglu(h, w_router, w_gate, w_up, w_down):
    B, S, D = h.shape
    t = h.reshape(B * S, D)
    logits = jnp.einsum('td,de->te', t, w_router).astype(jnp.float32)
    top_val, top_idx = lax.top_k(logits, TOP_K)
    top_w = jax.nn.softmax(top_val, axis=-1)
    combine = jnp.einsum('tk,tke->te', top_w, jax.nn.one_hot(top_idx, N_EXPERTS, dtype=jnp.float32))
    y = jnp.zeros((B * S, D), jnp.float32)
    for e in range(N_EXPERTS):
        y = y + combine[:, e:e + 1] * swiglu_2(t, w_gate[e], w_up[e], w_down[e]).astype(jnp.float32)
    return y.astype(h.dtype).reshape(B, S, D)

def second_inputs(seed: int = 0) -> dict:
    key = jax.random.key(seed)
    ks = jax.random.split(key, 20)
    f32 = jnp.float32
    n_dense = (DEPTH + 1) // 2
    n_moe = DEPTH // 2
    res = (2 * DEPTH) ** -0.5

    def nrm(k, shape, fan_in, extra=1.0):
        return jax.random.normal(k, shape, f32) * (fan_in ** -0.5) * extra

    def gain(k, shape):
        return 1.0 + 0.02 * jax.random.normal(k, shape, f32)

    return {
        'x': jax.random.normal(ks[0], (BATCH, SEQ, D_MODEL), f32),
        'mix_norm': gain(ks[1], (DEPTH, D_MODEL)),
        'w_in': nrm(ks[2], (DEPTH, D_MODEL, IN_WIDTH), D_MODEL),
        'hgrn_lb_logits': 0.5 * jax.random.normal(ks[3], (DEPTH, HGRN_WIDTH), f32),
        'hgrn_out_norm': gain(ks[4], (DEPTH, HGRN_HEAD_DIM)),
        'w_branch_hgrn': nrm(ks[5], (DEPTH, HGRN_WIDTH, D_MODEL), HGRN_WIDTH),
        'w_branch_sb': nrm(ks[6], (DEPTH, SB_WIDTH, D_MODEL), SB_WIDTH),
        'w_out': nrm(ks[7], (DEPTH, D_MODEL, D_MODEL), D_MODEL, res),
        'ffn_norm': gain(ks[8], (DEPTH, D_MODEL)),
        'dense_w_gate': nrm(ks[9], (n_dense, D_MODEL, FFN_DIM), D_MODEL),
        'dense_w_up': nrm(ks[10], (n_dense, D_MODEL, FFN_DIM), D_MODEL),
        'dense_w_down': nrm(ks[11], (n_dense, FFN_DIM, D_MODEL), FFN_DIM, res),
        'moe_router': nrm(ks[12], (n_moe, D_MODEL, N_EXPERTS), D_MODEL),
        'moe_w_gate': nrm(ks[13], (n_moe, N_EXPERTS, D_MODEL, FFN_DIM), D_MODEL),
        'moe_w_up': nrm(ks[14], (n_moe, N_EXPERTS, D_MODEL, FFN_DIM), D_MODEL),
        'moe_w_down': nrm(ks[15], (n_moe, N_EXPERTS, FFN_DIM, D_MODEL), FFN_DIM, res),
        'final_norm': gain(ks[16], (D_MODEL,)),
    }

def second_block(x, mix_norm, w_in, hgrn_lb_logits, hgrn_out_norm, w_branch_hgrn, w_branch_sb, w_out,
              ffn_norm, dense_w_gate, dense_w_up, dense_w_down, moe_router, moe_w_gate, moe_w_up,
              moe_w_down, final_norm):
    lb_all = jnp.cumsum(jax.nn.softmax(hgrn_lb_logits.astype(jnp.float32), axis=0), axis=0)
    lb_all = lb_all - lb_all[0:1]
    for layer in range(DEPTH):
        h = rms_norm(x, mix_norm[layer])
        x = x + hybrid_mixer(h, w_in[layer], lb_all[layer], hgrn_out_norm[layer],
                             w_branch_hgrn[layer], w_branch_sb[layer], w_out[layer])
        h = rms_norm(x, ffn_norm[layer])
        j = layer // 2
        if layer % 2 == 0:
            x = x + swiglu_2(h, dense_w_gate[j], dense_w_up[j], dense_w_down[j])
        else:
            x = x + moe_swiglu(h, moe_router[j], moe_w_gate[j], moe_w_up[j], moe_w_down[j])
    return rms_norm(x, final_norm)


def setup_inputs(seed=0):
    out = dict(first_inputs(seed))
    for name, value in second_inputs(seed + 1).items():
        if name != "x":
            out[name + "_2"] = value
    return out


def reference(
    x, a_norm, a_w_in, a_conv_w, a_conv_b, a_gate_w, a_gate_b, a_lambda, a_w_out, kv_norm, kv_w,
    k_norm, cmp_pos, cmp_w1, cmp_b1, cmp_w2, cmp_b2, b_norm, b_w_in, b_gate_b, q_norm, b_w_out,
    f_norm, f_w_in, f_w_out, mix_norm_2, w_in_2, hgrn_lb_logits_2, hgrn_out_norm_2,
    w_branch_hgrn_2, w_branch_sb_2, w_out_2, ffn_norm_2, dense_w_gate_2, dense_w_up_2,
    dense_w_down_2, moe_router_2, moe_w_gate_2, moe_w_up_2, moe_w_down_2, final_norm_2,
):
    x = first_block(
        x, a_norm, a_w_in, a_conv_w, a_conv_b, a_gate_w, a_gate_b, a_lambda, a_w_out, kv_norm,
        kv_w, k_norm, cmp_pos, cmp_w1, cmp_b1, cmp_w2, cmp_b2, b_norm, b_w_in, b_gate_b, q_norm,
        b_w_out, f_norm, f_w_in, f_w_out,
    )
    return second_block(
        x, mix_norm_2, w_in_2, hgrn_lb_logits_2, hgrn_out_norm_2, w_branch_hgrn_2,
        w_branch_sb_2, w_out_2, ffn_norm_2, dense_w_gate_2, dense_w_up_2, dense_w_down_2,
        moe_router_2, moe_w_gate_2, moe_w_up_2, moe_w_down_2, final_norm_2,
    )


_drawn_inputs = setup_inputs


def setup_inputs(seed=0):
    import zlib

    import numpy as np

    out = dict(_drawn_inputs(seed))
    spreads = {}
    factors = {'a_norm': 3.064,
     'a_gate_b': 8.0,
     'kv_norm': 5.099,
     'k_norm': 5.017,
     'cmp_pos': 5.136,
     'cmp_b1': 6.709,
     'cmp_b2': 5.374,
     'b_norm': 6.486,
     'b_gate_b': 8.0,
     'q_norm': 6.794,
     'mix_norm_2': 5.081,
     'hgrn_lb_logits_2': 4.311,
     'hgrn_out_norm_2': 6.547,
     'ffn_norm_2': 9.887,
     'final_norm_2': 7.449}
    for name, (base, spread) in spreads.items():
        noise = np.random.default_rng([zlib.crc32(name.encode()), seed]).standard_normal(out[name].shape)
        drawn = base * np.exp(spread * noise) if base else spread * noise
        out[name] = __import__('jax').numpy.asarray(drawn.astype(out[name].dtype))
    for name, factor in factors.items():
        out[name] = (out[name] * factor).astype(out[name].dtype)
    return out
```

```python
from contextlib import ExitStack

import numpy as np
import concourse.bass as bass
from concourse import mybir

F32 = mybir.dt.float32
F32R = mybir.dt.float32r
I32 = mybir.dt.int32
U8 = mybir.dt.uint8
ACT = mybir.ActivationFunctionType
ALU = mybir.AluOpType
AX = mybir.AxisListType

P = 128
S = 256
M = S // P
D = 1024
KD = D // P
EPS = 1e-6
NEG = -1e30
SLOT = 4096

HD, NH, NG = 64, 16, 4
HPG = NH // NG
CB, CS, CH = 32, 16, 256
NCMP = (S - CB) // CS + 1
SCALE = HD ** -0.5
LRU_C = 8.0
CONV = 4
F_A = 2816
F_B = 3584
FB = 512
HH, HC = 4, 64
SH = 8
LEVELS = [1, 2, 4, 8, 16, 32]
E = 8
ITEMS = 12
NBB = F_B // FB

IN_ORDER = [1, 0, 5, 4, 2, 6, 3, 7, 8, 9, 10]


CONSTS = {}


def _const_arrays():
    cols, at = [], 0

    def put(name, a):
        nonlocal at
        a = np.broadcast_to(np.asarray(a, np.float32), (P, np.asarray(a).shape[-1]))
        CONSTS[name] = (at, a.shape[1])
        cols.append(a)
        at += a.shape[1]

    i = np.arange(P)
    put("ident", np.eye(P))
    put("neg_causal", np.where(i[None, :] > i[:, None], NEG, 0.0))
    put("before", (i[:, None] < i[None, :]) * 1.0)
    put("neg_not_before", np.where(i[:, None] < i[None, :], 0.0, NEG))
    put("minus_from", np.where(i[:, None] >= i[None, :], -1.0, 0.0))
    put("minus_one", -np.ones((P, P)))
    put("one", np.ones((P, P)))
    put("iota_slot", i[None, :])
    half = HD // 2
    freqs = np.power(np.float32(10000.0), -np.arange(half, dtype=np.float32) / np.float32(half)).astype(np.float32)

    def rope(pos):
        ang = (pos.astype(np.float32)[:, None] * freqs[None, :]).astype(np.float32)
        c, s = np.cos(ang).astype(np.float32), np.sin(ang).astype(np.float32)
        return np.concatenate([c, c], 1), np.concatenate([s, s], 1)

    for m in range(M):
        c, s = rope(m * P + i)
        put(f"cos{m}", c)
        put(f"sin{m}", s)
    c, s = rope(np.minimum(i, NCMP - 1) * CS + CB - 1)
    put("cosc", c)
    put("sinc", s)
    for m in range(M):
        last = np.arange(NCMP) * CS + CB - 1
        put(f"neg_cmp{m}", np.where(last[None, :] <= (m * P + i)[:, None], 0.0, NEG))
    put("row_valid", ((i >= CB - 1) * 1.0)[:, None])
    e = np.arange(E)
    put("lower_e", ((e[None, :] < e[:, None]) * 1.0).reshape(1, -1))
    put("iota_e", e[None, :])
    put("iota_i", np.arange(ITEMS)[None, :])
    base = np.concatenate(cols, 1)
    masks = [np.eye(P)]
    for lv in LEVELS + [64]:
        same = (i[:, None] // (2 * lv)) == (i[None, :] // (2 * lv))
        masks.append(same & (i[:, None] % (2 * lv) < lv) & (i[None, :] % (2 * lv) >= lv))
    masks = np.stack(masks, 1).astype(np.float32).reshape(P, -1)
    return np.ascontiguousarray(base), np.ascontiguousarray(masks)


CONST_F32, CONST_MASKS = _const_arrays()

ROWS = [
    [("a_norm", 8), ("a_conv_w", 32), ("a_conv_b", 8), ("a_gate_b", 16), ("a_lambda", 8),
     ("kv_norm", 8), ("b_norm", 8), ("f_norm", 16)],
    [("mix_norm_2", 16), ("ffn_norm_2", 16), ("hgrn_lb_logits_2", 8), ("cmp_b1", 4), ("cmp_pos", 32)],
]
COL = {}
for _g, _names in enumerate(ROWS):
    _at = _g * P
    for _n, _r in _names:
        COL[_n] = _at
        _at += _r
ROWS_USED = [sum(r for _, r in g) for g in ROWS]
BC = {"q_norm": (0, 64), "k_norm": (64, 192), "cmp_b2": (256, 128), "b_gate_b": (384, 48), "hgrn_out_norm_2": (432, 256)}
BC_W = 688


class Ring:

    def __init__(self, banks, filled, read):
        self.banks, self.filled, self.read, self.n = banks, filled, read, 0

    def claim(self, pe):
        if self.n >= len(self.banks):
            pe.wait_ge(self.read, self.n - len(self.banks) + 1)
        self.n += 1
        return self.banks[(self.n - 1) % len(self.banks)]

    def take(self, eng):
        self.n += 1
        eng.wait_ge(self.filled, self.n)
        return self.banks[(self.n - 1) % len(self.banks)]


def weight_plan():
    plan, fills = {}, [0, 0, 0]
    order, nxt = [], 0

    def tile(*key):
        nonlocal nxt
        s = nxt
        nxt = (nxt + 1) % 3
        plan[key] = (s, fills[s])
        fills[s] += 1
        order.append(key)

    def ffn(name, blocks):
        nonlocal nxt
        nxt = 0
        plan[name] = list(fills)
        for s in range(3):
            fills[s] += blocks
        order.append((name,))

    for t in (2, 3):
        tile("a_in", t)
    tile("a_gate")
    for t in (0, 1):
        tile("a_in", t)
    for t in (0, 1):
        tile("a_out", t)
    ffn("ffn0", 6)
    for t in range(3):
        tile("kv", t)
    for t in range(3):
        tile("b_in", t)
    for t in range(2):
        tile("cmp", t)
    for t in range(2):
        tile("b_out", t)
    ffn("ffn1", 6)
    for layer in range(2):
        for t in IN_ORDER:
            tile("mix_in", layer, t)
        tile("branch", layer, 0)
        tile("branch", layer, 1)
        for t in range(2):
            tile("mix_out", layer, t)
        if layer == 0:
            ffn("ffn2", NBB)
        else:
            ffn("moe", 0)
    return plan, order


def build(nc, A, out, dbg=None):
    plan, order = weight_plan()
    ctx = ExitStack()
    with ctx:
        def sbuf(name, shape, dt=F32, stack=ctx):
            return stack.enter_context(nc.sbuf_tensor(name, shape, dt))

        def sem(name):
            return ctx.enter_context(nc.semaphore(name))

        x = sbuf("x", [P, M, D])
        xn = sbuf("xn", [P, M, D])
        uT = sbuf("uT", [P, KD, S])
        raw = sbuf("raw", [P, 3, SLOT])
        const = sbuf("const", [P, CONST_F32.shape[1]])
        cols = sbuf("cols", [P, 2 * P])
        bc = sbuf("bc", [P, BC_W])
        small = sbuf("small", [P, 64])

        def C(name, rows=P):
            a, w = CONSTS[name]
            return const[0:rows, a:a + w]

        def col(name, i=0, n=1):
            return cols[:, COL[name] + i:COL[name] + i + n]

        with ExitStack() as st:
            rowbuf = sbuf("rowbuf", [P, 2, P], stack=st)
            zp = sbuf("zp", [P, KD, S + CONV - 1], stack=st)
            xr = sbuf("xr", [P, KD, S], stack=st)
            rg = sbuf("rg", [P, KD, S], stack=st)
            ig = sbuf("ig", [P, KD, S], stack=st)
            aa = sbuf("aa", [P, KD, S], stack=st)
            th = sbuf("th", [P, KD, S], stack=st)
            yg = sbuf("yg", [P, KD, S], stack=st)
            lam = sbuf("lam", [P, 8, KD], stack=st)
        with ExitStack() as st:
            wh = sbuf("wh", [P, 3, SLOT], F32R, stack=st)
            wl = sbuf("wl", [P, 3, SLOT], F32R, stack=st)
            xh = sbuf("xh", [P, KD, S], F32R, stack=st)
            xl = sbuf("xl", [P, KD, S], F32R, stack=st)
            sg = sbuf("sg", [P, FB], stack=st)
            hb = sbuf("hb", [P, FB], stack=st)
            hh = sbuf("hh", [P, FB], F32R, stack=st)
            hl = sbuf("hl", [P, FB], F32R, stack=st)
            ye = sbuf("ye", [P, D], stack=st)
            rti = sbuf("rti", [1, 16], I32, stack=st)
            wr = sbuf("wr", [P, KD * E], stack=st)
        with ExitStack() as st:
            ubT = sbuf("ubT", [P, KD, S], stack=st)
            kvn = sbuf("kvn", [P, M, 6 * NG * HD], stack=st)
            qn = sbuf("qn", [P, M, D], stack=st)
            tmp_a = sbuf("tmp_a", [P, D], stack=st)
            tmp_b = sbuf("tmp_b", [P, D], stack=st)
            xc = sbuf("xc", [P, CB * HD], stack=st)
            xcT = sbuf("xcT", [P, 2, 16, NG * NCMP], stack=st)
            h1T = sbuf("h1T", [P, 4, 64], stack=st)
            w2 = sbuf("w2", [P, 2, 2, HD], stack=st)
            cmpn = sbuf("cmpn", [P, 2, NG, HD], stack=st)
            kdup = sbuf("kdup", [P, M, 2, NG, 2, HD], stack=st)
            kcdup = sbuf("kcdup", [P, NG, 2, HD], stack=st)
            rope_g = sbuf("rope_g", [P, 5, 2, HD], stack=st)
            rope_k = sbuf("rope_k", [P, M, 2, 2, HD], stack=st)
            kT = sbuf("kT", [P, 2, NG, S], stack=st)
            kcT = sbuf("kcT", [P, NG, 16], stack=st)
            qT = sbuf("qT", [P, NH // 2, S], stack=st)
            gate = sbuf("gate", [P, M, 3, NH], stack=st)
            pr = sbuf("pr", [P, 2, 528], stack=st)
            pT = sbuf("pT", [P, 512], stack=st)
            pcT = sbuf("pcT", [P, P], stack=st)
            stat = sbuf("stat", [P, 2, 16], stack=st)
            oT = qT
        with ExitStack() as st:
            zf = sbuf("zf", [P, HH, S], stack=st)
            qh = sbuf("qh", [P, HH, S], stack=st)
            t1 = sbuf("t1", [P, HH, S], stack=st)
            t2 = sbuf("t2", [P, HH, S], stack=st)
            t3 = sbuf("t3", [P, HH, S], stack=st)
            kk = sbuf("kk", [P, HH, S], stack=st)
            bb = sbuf("bb", [P, HH, S], stack=st)
            keep = sbuf("keep", [P, HH, S], stack=st)
            sd = sbuf("sd", [P, HH, M, P], stack=st)
            sx = sbuf("sx", [P, HH, P], stack=st)
            skT = sbuf("skT", [P, 4, S], stack=st)
            sqT = sbuf("sqT", [P, 4, S], stack=st)
            hv = sbuf("hv", [P, M, 512], stack=st)
            sv = sbuf("sv", [P, M, 512], stack=st)
            hog = sbuf("hog", [P, M, 512], stack=st)
            sga = sbuf("sga", [P, M, D], stack=st)
            sgb = sbuf("sgb", [P, M, D], stack=st)
            oa = sbuf("oa", [P, M, 512], stack=st)
            oaT = sbuf("oaT", [P, 4, S], stack=st)
            obT = sbuf("obT", [P, 4, S], stack=st)
            e1 = sbuf("e1", [P, 2, 384], stack=st)
            sp = sbuf("sp", [P, 2, 384], stack=st)
            wt = sbuf("wt", [P, 2, 384], stack=st)
            lbt = sbuf("lbt", [P, 8, HH], stack=st)
            lmask = sbuf("lmask", [P, 8 * P], U8, stack=st)

        rt = uT[:, 3:6, :].rearrange("p a b -> p (a b)")
        R_, at = {}, 0
        for name, w in [("exp", M * E), ("logit", M * E), ("neg_max", M), ("sum", M), ("a64", E * E), ("b64", E * E),
                        ("rank", E), ("weight", M * E), ("pos", 3 * E), ("tiles", E), ("upto", E), ("before", E), ("ones", E),
                        ("owner", ITEMS * E), ("tmp", ITEMS * E), ("expert", ITEMS), ("first", ITEMS), ("there", ITEMS),
                        ("slot_of", M * ITEMS), ("weight_of", M * ITEMS), ("sel", M * E)]:
            R_[name] = rt[:, at:at + w]
            at += w
        slot_of, weight_of = (R_[k].rearrange("p (m i) -> p m i", m=M) for k in ("slot_of", "weight_of"))
        sel = R_["sel"].rearrange("p (m e) -> p m e", m=M)
        pick, pickw = uT[:, 0:1, :].rearrange("p a (m t) -> p (a m) t", m=M), uT[:, 1:2, :].rearrange("p a (m t) -> p (a m) t", m=M)
        pickT = uT[:, 2, :]

        ps = ctx.enter_context(nc.psum_tensor("ps", [P, 8, 512], F32))
        kv_scratch = nc.dram_tensor("kv_scratch", [S, 512], F32, kind="Internal").ap()

        slot_full = [sem(f"slot_full{s}") for s in range(3)]
        const_in = sem("const_in")
        rows_in = [sem(f"rows_in{i}") for i in range(2)]
        bc_in = sem("bc_in")
        x_in = sem("x_in")
        w2_in, masks_in, wr_in, ye_in, final_in = sem("w2_in"), sem("masks_in"), sem("wr_in"), sem("ye_in"), sem("final_in")
        kvc_out, kvc_in = sem("kvc_out"), sem("kvc_in")
        stage = sem("stage")
        dve_order, act_order = sem("dve_order"), sem("act_order")
        v_filled, v_read = sem("v_filled"), sem("v_read")
        a_filled, a_read = sem("a_filled"), sem("a_read")
        s_filled, s_read = sem("s_filled"), sem("s_read")
        norm_sq, norm_ms, norm_rt, norm_xn = sem("norm_sq"), sem("norm_ms"), sem("norm_rt"), sem("norm_xn")
        norm_h = sem("norm_h")
        xr_ready, ri_ready, la_ready, a_ready = sem("xr_ready"), sem("ri_ready"), sem("la_ready"), sem("a_ready")
        lam_abs, lam_exp = sem("lam_abs"), sem("lam_exp")
        th_ready, t2_ready, sq_ready, yg_ready, yh_ready = (
            sem("th_ready"), sem("t2_ready"), sem("sq_ready"), sem("yg_ready"), sem("yh_ready"))
        kvn_ready, qn_ready, gate_ready, gated = sem("kvn_ready"), sem("qn_ready"), sem("gate_ready"), sem("gated")
        ms_ready, root_ready = sem("ms_ready"), sem("root_ready")
        k_ready, q_ready, kc_ready = sem("k_ready"), sem("q_ready"), sem("kc_ready")
        max_ready, p_ready = sem("max_ready"), sem("p_ready")
        lb_max, lb_exp, lb_clamped, lb_ln = sem("lb_max"), sem("lb_exp"), sem("lb_clamped"), sem("lb_ln")
        zabs_ready, zln_ready, zdif_ready, kk_ready = sem("zabs_ready"), sem("zln_ready"), sem("zdif_ready"), sem("kk_ready")
        fabs_ready, fln_ready, qh_ready = sem("fabs_ready"), sem("fln_ready"), sem("qh_ready")
        decay_ready, decay_exp, level_ready = sem("decay_ready"), sem("decay_exp"), sem("level_ready")
        oms_ready, ort_ready, oa_ready = sem("oms_ready"), sem("ort_ready"), sem("oa_ready")
        ln_ready, sp_ready, y_ready = sem("ln_ready"), sem("sp_ready"), sem("y_ready")
        sel_ready, lmax_ready, lexp_ready, ye_zeroed = sem("sel_ready"), sem("lmax_ready"), sem("lexp_ready"), sem("ye_zeroed")
        wh_full = [sem(f"wh_full{s}") for s in range(3)]
        wl_full = [sem(f"wl_full{s}") for s in range(3)]
        g_done, u_done, t_done, d_done = sem("g_done"), sem("u_done"), sem("t_done"), sem("d_done")
        sg_ready, h_ready, hh_ready, hl_ready, d_added = (
            sem("sg_ready"), sem("h_ready"), sem("hh_ready"), sem("hl_ready"), sem("d_added"))
        pick_ready, picked, xh_ready, xl_ready = sem("pick_ready"), sem("picked"), sem("xh_ready"), sem("xl_ready")
        pickT_done, pickT_ready, put_done = sem("pickT_done"), sem("pickT_ready"), sem("put_done")
        items_ready = sem("items_ready")
        out_ready, out_sent = sem("out_ready"), sem("out_sent")

        block = ctx.enter_context(nc.Block())

        marks = {}
        freed = {}

        class Side:

            def __init__(self, eng):
                self.eng, self.n, self.counts, self.norms = eng, 0, {}, 0
                self.v = Ring([0, 1, 2], v_filled, v_read)
                self.a = Ring([3, 4, 5], a_filled, a_read)
                self.s = Ring([6, 7], s_filled, s_read)

            def barrier(self, name):
                self.n += 1
                marks[name] = self.n
                self.eng.drain().then_inc(stage, 1)
                self.eng.wait_ge(stage, 3 * self.n)

            def see(self, s, by=1):
                self.counts[s.name] = self.counts.get(s.name, 0) + by
                self.eng.wait_ge(s, self.counts[s.name])

            def link(self, ins, order):
                self.counts["order"] = self.counts.get("order", 0) + 1
                ins.then_inc(order, 1)
                self.eng.wait_ge(order, self.counts["order"])

        def tile_view(key, k, w):
            return raw[:, plan[key][0], 0:k * w].rearrange("p (k n) -> p k n", k=k)

        def arrived(eng, key):
            s, f = plan[key]
            eng.wait_ge(slot_full[s], 16 * (f + 1))

        FFN = {"ffn0": (6, 256, 0, 0), "ffn1": (6, 256, 6, 12), "ffn2": (NBB, FB, 12, 24)}
        MOE_B, MOE_U = 12 + NBB, 24 + 2 * NBB

        @block.tensor
        def _(pe):
            me = Side(pe)
            mm, tr = nc.tensor.matmul, nc.tensor.transpose
            pe.wait_ge(const_in, 16)
            ident = C("ident")

            for g in range(2):
                pe.wait_ge(rows_in[g], 16 * len(ROWS[g]))
                b = me.v.claim(pe)
                r = ROWS_USED[g]
                tr(ps[:, b, 0:r], rowbuf[0:r, g, :], const[0:r, 0:r]).then_inc(v_filled, 1)

            def drained(ring):
                pe.wait_ge(ring.read, ring.n)

            def norm(split=False):
                me.see(norm_xn, M)
                for j in range(4):
                    ring = me.s if split else (me.v, me.a)[j % 2]
                    b = ring.claim(pe)
                    for kk in range(2):
                        for m in range(M):
                            t = tr(ps[:, b, (kk * M + m) * P:(kk * M + m + 1) * P],
                                   xn[:, m, (2 * j + kk) * P:(2 * j + kk + 1) * P], ident)
                    t.then_inc(ring.filled, 1)
                for ring in ((me.s,) if split else (me.v, me.a)):
                    drained(ring)

            def released(key, ring):
                freed[key] = (ring.filled, ring.n)

            def product_T(ring, key, c, src):
                w = tile_view(key, KD, 512)
                b = ring.claim(pe)
                for k in range(KD):
                    t = mm(ps[:, b, 0:S], w[:, k, c * P:(c + 1) * P], src[:, k, :], start=(k == 0), stop=(k == KD - 1))
                t.then_inc(ring.filled, 1)

            def product(ring, key, m, src, w=512, kc=KD, c0=0):
                wv = tile_view(key, kc, max(w, D) if kc == 4 else w)
                b = ring.claim(pe)
                for k in range(kc):
                    t = mm(ps[:, b, 0:w], src[:, k, m * P:(m + 1) * P], wv[:, k, c0:c0 + w], start=(k == 0), stop=(k == kc - 1))
                t.then_inc(ring.filled, 1)

            me.barrier("start")
            norm()
            for t in (2, 3):
                arrived(pe, ("a_in", t))
                for c in range(4):
                    product_T(me.v, ("a_in", t), c, uT)
                released(("a_in", t), me.v)
            arrived(pe, ("a_gate",))
            gw = tile_view(("a_gate",), 16, P)
            for f in range(KD):
                me.see(xr_ready)
                b = me.a.claim(pe)
                for i in range(2):
                    t = mm(ps[:, b, i * S:(i + 1) * S], gw[:, i * KD + f, :], xr[:, f, :], start=True, stop=True)
                t.then_inc(a_filled, 1)
            released(("a_gate",), me.a)
            for t in (0, 1):
                arrived(pe, ("a_in", t))
                for c in range(4):
                    product_T(me.a, ("a_in", t), c, uT)
                released(("a_in", t), me.a)
            me.see(yh_ready)
            for t in range(2):
                arrived(pe, ("a_out", t))
                for m in range(M):
                    product(me.v, ("a_out", t), m, rg)
                released(("a_out", t), me.v)
            drained(me.v)

            def ffn_steps(ns):
                def wait(s, v):
                    if not (isinstance(v, int) and v <= 0):
                        pe.wait_ge(s, v)

                def split_product(bank, kind, xa, xb, k, B, w, last, c0=0, n=None):
                    a = wh[:, kind, k * w + c0:k * w + c0 + n]
                    l = wl[:, kind, k * w + c0:k * w + c0 + n]
                    mm(ps[:, bank, 0:n], xa, a, start=(k == 0), stop=False)
                    mm(ps[:, bank, 0:n], xa, l, start=False, stop=False)
                    return mm(ps[:, bank, 0:n], xb, a, start=False, stop=(k == last))

                def gate_up(kind, B, u, m, w):
                    pe.wait_ge(wh_full[kind], B + 1)
                    pe.wait_ge(wl_full[kind], B + 1)
                    wait(sg_ready if kind == 0 else h_ready, u)
                    for k in range(KD):
                        t = split_product(kind, kind, xh[:, k, m * P:(m + 1) * P], xl[:, k, m * P:(m + 1) * P],
                                          k, B, w, KD - 1, 0, w)
                    t.then_inc(g_done if kind == 0 else u_done, 1)

                def turn(u, w):
                    pe.wait_ge(h_ready, u + 1)
                    wait(hl_ready, u)
                    for c in range(w // P):
                        t = tr(ps[:, 2, c * P:(c + 1) * P], hb[:, c * P:(c + 1) * P], ident)
                    t.then_inc(t_done, 1)

                def down(B, u, w):
                    pe.wait_ge(wh_full[2], B + 1)
                    pe.wait_ge(wl_full[2], B + 1)
                    pe.wait_ge(hh_ready, u + 1)
                    pe.wait_ge(hl_ready, u + 1)
                    wait(d_added, u)
                    for half in range(2):
                        for c in range(w // P):
                            t = split_product(3 + half, 2, hh[:, c * P:(c + 1) * P], hl[:, c * P:(c + 1) * P],
                                              c, B, D, w // P - 1, half * FB, FB)
                    t.then_inc(d_done, 1)
                return gate_up, turn, down

            gate_up, turn, down = ffn_steps(None)

            def ffn(name):
                nb, wlast, B0, U0 = FFN[name]
                norm(split=True)

                def body(b, w, first=False):
                    for m in range(M):
                        u = b * M + (U0 + m)
                        gate_up(0, b + B0, u, m, w)
                        if not (first and m == 0):
                            turn(u - 1, w if m else FB)
                        gate_up(1, b + B0, u, m, w)
                        if not (first and m == 0):
                            down(b + (B0 if m else B0 - 1), u - 1, w if m else FB)

                body(0, FB, first=True)
                with pe.Fori(1, nb - 1) as b:
                    body(b, FB)
                body(nb - 1, wlast)
                u = U0 + nb * M - 1
                turn(u, wlast)
                down(B0 + nb - 1, u, wlast)
                pe.wait_ge(d_added, u + 1)

            me.barrier("ffn0")
            ffn("ffn0")

            me.barrier("nsa")
            norm()
            for t in range(3):
                arrived(pe, ("kv", t))
                product(me.v, ("kv", t), 0, uT)
                product(me.a, ("kv", t), 1, uT)
                released(("kv", t), me.a)
            for t in range(2):
                arrived(pe, ("b_in", t))
                product(me.v, ("b_in", t), 0, ubT)
                product(me.a, ("b_in", t), 1, ubT)
                released(("b_in", t), me.a)
            arrived(pe, ("b_in", 2))
            for m in range(M):
                product(me.v, ("b_in", 2), m, ubT, w=3 * NH)
            released(("b_in", 2), me.v)
            me.see(k_ready)
            for m in range(M):
                for w in range(2):
                    b = me.a.claim(pe)
                    for g in range(NG):
                        t = tr(ps[:, b, g * P:(g + 1) * P], kdup[:, m, w, g, :, :].rearrange("p a d -> p (a d)"), ident)
                    t.then_inc(a_filled, 1)
            for m in range(M):
                me.see(q_ready)
                for j in range(2):
                    b = me.a.claim(pe)
                    for i in range(4):
                        t = tr(ps[:, b, i * P:(i + 1) * P], qn[:, m, (4 * j + i) * P:(4 * j + i + 1) * P], ident)
                    t.then_inc(a_filled, 1)
            pe.wait_ge(kvc_in, 16 * 2 * 2 * NG)
            R = 2 * NG * NCMP
            for j in range(4):
                b = me.v.claim(pe)
                for i in range(4):
                    t = tr(ps[:, b, i * R:(i + 1) * R], xc[0:R, (4 * j + i) * P:(4 * j + i + 1) * P], const[0:R, 0:R])
                t.then_inc(v_filled, 1)
            drained(me.v)
            b = me.a.claim(pe)
            for kv in range(2):
                arrived(pe, ("cmp", kv))
                w1 = tile_view(("cmp", kv), 16, CH)
                for hc in range(2):
                    for l in range(16):
                        t = mm(ps[:, b, (kv * 2 + hc) * 64:(kv * 2 + hc) * 64 + NG * NCMP], w1[:, l, hc * P:(hc + 1) * P],
                               xcT[:, kv, l, :], start=(l == 0), stop=(l == 15))
            t.then_inc(a_filled, 1)
            released(("cmp", 0), me.a)
            released(("cmp", 1), me.a)
            drained(me.a)
            pe.wait_ge(w2_in, 16)
            b = me.v.claim(pe)
            for kv in range(2):
                for g in range(NG):
                    for hc in range(2):
                        t = mm(ps[0:NCMP, b, (kv * NG + g) * HD:(kv * NG + g + 1) * HD],
                               h1T[:, kv * 2 + hc, g * NCMP:(g + 1) * NCMP], w2[:, kv, hc, :], start=(hc == 0), stop=(hc == 1))
            t.then_inc(v_filled, 1)
            me.see(kc_ready)
            b = me.v.claim(pe)
            for g in range(NG):
                t = tr(ps[:, b, g * 16:g * 16 + NCMP], kcdup[0:NCMP, g, :, :].rearrange("p a d -> p (a d)"),
                       const[0:NCMP, 0:NCMP])
            t.then_inc(v_filled, 1)
            drained(me.v)

            def scores(m, h):
                g, p0, nk = h // HPG, HD * (h % 2), P * (m + 1)
                q = qT[p0:p0 + HD, h // 2, m * P:(m + 1) * P]
                b = me.s.claim(pe)
                for w in range(2):
                    mm(ps[:, b, w * S:w * S + nk], q, kT[p0:p0 + HD, w, g, 0:nk], start=True, stop=False)
                    t = mm(ps[:, b, w * S + m * P:w * S + nk], ident, C("neg_causal"), start=False, stop=True)
                t.then_inc(s_filled, 1)
                b = me.v.claim(pe)
                mm(ps[:, b, 0:NCMP], q, kcT[p0:p0 + HD, g, 0:NCMP], start=True, stop=False)
                mm(ps[:, b, 0:NCMP], ident, C(f"neg_cmp{m}"), start=False, stop=True).then_inc(v_filled, 1)

            def attend(i, m, h):
                g, nb = h // HPG, m + 1
                me.see(p_ready)
                b = me.a.claim(pe)
                for w in range(2):
                    for kb in range(nb):
                        t = tr(ps[:, b, (w * nb + kb) * P:(w * nb + kb + 1) * P],
                               pr[:, i % 2, w * S + kb * P:w * S + (kb + 1) * P], ident)
                t.then_inc(a_filled, 1)
                b = me.a.claim(pe)
                tr(ps[0:NCMP, b, 0:P], pr[:, i % 2, 512:512 + NCMP], ident).then_inc(a_filled, 1)
                drained(me.a)
                b = me.v.claim(pe)
                for w in range(2):
                    for kb in range(nb):
                        mm(ps[:, b, w * HD:(w + 1) * HD], pT[:, (w * nb + kb) * P:(w * nb + kb + 1) * P],
                           kvn[:, kb, (2 * w + 3) * 256 + g * HD:(2 * w + 3) * 256 + (g + 1) * HD],
                           start=(kb == 0), stop=(kb == nb - 1))
                mm(ps[:, b, 2 * HD:3 * HD], pcT[0:NCMP, :], cmpn[0:NCMP, 1, g, :], start=True, stop=True).then_inc(v_filled, 1)

            pairs = [(m, h) for m in range(M) for h in range(NH)]
            scores(*pairs[0])
            for i, (m, h) in enumerate(pairs):
                if i + 1 < len(pairs):
                    scores(*pairs[i + 1])
                attend(i, m, h)
            drained(me.v)
            for m in range(M):
                for j in range(2):
                    b = me.a.claim(pe)
                    for i in range(4):
                        t = tr(ps[:, b, i * P:(i + 1) * P], qn[:, m, (4 * j + i) * P:(4 * j + i + 1) * P], ident)
                    t.then_inc(a_filled, 1)
            drained(me.a)
            for t in range(2):
                arrived(pe, ("b_out", t))
                for m in range(M):
                    product(me.v, ("b_out", t), m, oT)
                released(("b_out", t), me.v)
            drained(me.v)

            me.barrier("ffn1")
            ffn("ffn1")

            def level_product(lv):
                me.see(level_ready)
                if lv == 128:
                    b = me.v.claim(pe)
                    for h in range(HH):
                        t = mm(ps[:, b, h * P:(h + 1) * P], t2[:, h, 0:P], t2[:, h, P:S], start=True, stop=True)
                    t.then_inc(v_filled, 1)
                    return
                ks, qs = (kk, qh) if lv == 0 else (t2, t2)
                for hp in range(2):
                    b = me.v.claim(pe)
                    for a in range(2):
                        for m in range(M):
                            t = mm(ps[:, b, (a * M + m) * P:(a * M + m + 1) * P], ks[:, 2 * hp + a, m * P:(m + 1) * P],
                                   qs[:, 2 * hp + a, m * P:(m + 1) * P], start=True, stop=True)
                    t.then_inc(v_filled, 1)

            def sb_z(b, h, stop=True):
                p0, hp = HD * (h % 2), h // 2
                mm(ps[:, b, 0:S], skT[p0:p0 + HD, hp, 0:P], sqT[p0:p0 + HD, hp, :], start=True, stop=stop)

            def sb_z1(b, h, stop=True):
                p0, hp = HD * (h % 2), h // 2
                return mm(ps[:, b, S:S + P], skT[p0:p0 + HD, hp, P:S], sqT[p0:p0 + HD, hp, P:S], start=True, stop=stop)

            def mixer(layer):
                norm()
                tiles = {t: ("mix_in", layer, t) for t in range(11)}
                for t, ring in ((1, me.v), (0, me.a), (5, me.v), (4, me.a)):
                    arrived(pe, tiles[t])
                    for c in range(4):
                        product_T(ring, tiles[t], c, uT)
                    released(tiles[t], ring)
                rest = [2, 6, 3, 7, 8, 9, 10]
                for j, lv in enumerate([0] + LEVELS + [64, 128]):
                    if j < len(rest):
                        arrived(pe, tiles[rest[j]])
                        for m in range(M):
                            product(me.a, tiles[rest[j]], m, uT)
                        released(tiles[rest[j]], me.a)
                    level_product(lv)
                drained(me.v)
                drained(me.a)
                for m in range(M):
                    b = me.v.claim(pe)
                    for h in range(HH):
                        o = ps[:, b, h * P:(h + 1) * P]
                        t = mm(o, sd[:, h, m, :], hv[:, m, h * P:(h + 1) * P], start=True, stop=(m == 0))
                        if m:
                            t = mm(o, sx[:, h, :], hv[:, 0, h * P:(h + 1) * P], start=False, stop=True)
                    t.then_inc(v_filled, 1)
                def sb_scores(h):
                    b = me.s.claim(pe)
                    sb_z(b, h)
                    sb_z1(b, h).then_inc(s_filled, 1)

                sb_scores(0)
                for h in range(SH):
                    if h + 1 < SH:
                        sb_scores(h + 1)
                    me.see(sp_ready)
                    spb = sp[:, h % 2, :]
                    b = me.a.claim(pe)
                    sb_z(b, h, stop=False)
                    mm(ps[:, b, 0:S], C("minus_from"), spb[:, 0:S], start=False, stop=False)
                    mm(ps[:, b, P:S], C("minus_one"), spb[:, S:S + P], start=False, stop=False)
                    mm(ps[:, b, 0:P], ident, C("neg_not_before"), start=False, stop=True)
                    sb_z1(b, h, stop=False)
                    mm(ps[:, b, S:S + P], C("minus_from"), spb[:, S:S + P], start=False, stop=False)
                    mm(ps[:, b, S:S + P], ident, C("neg_not_before"), start=False, stop=True).then_inc(a_filled, 1)
                    drained(me.a)
                    if h % 2 == 0:
                        bo = me.v.claim(pe)
                    p0 = HD * (h % 2)
                    mm(ps[p0:p0 + HD, bo, 0:S], sv[:, 0, h * HD:(h + 1) * HD], wt[:, h % 2, 0:S], start=True, stop=False)
                    t = mm(ps[p0:p0 + HD, bo, P:S], sv[:, 1, h * HD:(h + 1) * HD], wt[:, h % 2, S:S + P], start=False, stop=True)
                    if h % 2:
                        t.then_inc(v_filled, 1)
                me.see(oa_ready)
                for m in range(M):
                    b = me.a.claim(pe)
                    for k in range(4):
                        t = tr(ps[:, b, k * P:(k + 1) * P], oa[:, m, k * P:(k + 1) * P], ident)
                    t.then_inc(a_filled, 1)
                drained(me.a)
                drained(me.v)
                arrived(pe, ("branch", layer, 0))
                arrived(pe, ("branch", layer, 1))
                for m in range(M):
                    for half in range(2):
                        product(me.v, ("branch", layer, 0), m, oaT, w=512, kc=4, c0=half * 512)
                        if m == 1 and half == 1:
                            released(("branch", layer, 0), me.v)
                        product(me.v, ("branch", layer, 1), m, obT, w=512, kc=4, c0=half * 512)
                released(("branch", layer, 1), me.v)
                me.see(y_ready)
                for j in range(4):
                    b = me.a.claim(pe)
                    for kk_ in range(2):
                        for m in range(M):
                            k = 2 * j + kk_
                            t = tr(ps[:, b, (kk_ * M + m) * P:(kk_ * M + m + 1) * P], sga[:, m, k * P:(k + 1) * P], ident)
                    t.then_inc(a_filled, 1)
                drained(me.a)
                for t in range(2):
                    arrived(pe, ("mix_out", layer, t))
                    for m in range(M):
                        product(me.v, ("mix_out", layer, t), m, uT)
                    released(("mix_out", layer, t), me.v)
                drained(me.v)

            me.barrier("mix0")
            mixer(0)
            me.barrier("ffn2")
            ffn("ffn2")
            me.barrier("mix1")
            mixer(1)

            me.barrier("moe")
            norm()
            pe.wait_ge(wr_in, 16)
            b = me.v.claim(pe)
            for m in range(M):
                for k in range(KD):
                    t = mm(ps[:, b, m * E:(m + 1) * E], uT[:, k, m * P:(m + 1) * P], wr[:, k * E:(k + 1) * E],
                           start=(k == 0), stop=(k == KD - 1))
            t.then_inc(v_filled, 1)
            me.see(sel_ready)
            b = me.v.claim(pe)
            mm(ps[:, b, 0:E], C("before"), sel[:, 0, :], start=True, stop=True)
            mm(ps[:, b, E:2 * E], C("before"), sel[:, 1, :], start=True, stop=False)
            mm(ps[:, b, E:2 * E], C("one"), sel[:, 0, :], start=False, stop=True)
            mm(ps[:, b, 2 * E:3 * E], C("one"), sel[:, 0, :], start=True, stop=False)
            mm(ps[:, b, 2 * E:3 * E], C("one"), sel[:, 1, :], start=False, stop=True).then_inc(v_filled, 1)
            pe.wait_ge(items_ready, 1)
            n = pe.value_load(rti[0:1, 0:1], min_val=1, max_val=ITEMS)
            with pe.Fori(0, n) as it:
                B, U = it * NBB + MOE_B, it * NBB + MOE_U
                pe.wait_ge(pick_ready, it + 1)
                for k in range(KD):
                    o = ps[:, 5 + k // 4, (k % 4) * P:(k % 4 + 1) * P]
                    mm(o, xn[:, 0, k * P:(k + 1) * P], pick[:, 0, :], start=True, stop=False)
                    t = mm(o, xn[:, 1, k * P:(k + 1) * P], pick[:, 1, :], start=False, stop=True)
                t.then_inc(picked, 1)
                for m in range(M):
                    t = tr(ps[:, 7, m * P:(m + 1) * P], pickw[:, m, :], ident)
                t.then_inc(pickT_done, 1)
                pe.wait_ge(xh_ready, it + 1)
                pe.wait_ge(xl_ready, it + 1)
                gate_up(0, B, U, 0, FB)
                gate_up(1, B, U, 0, FB)
                with pe.Fori(1, NBB) as b:
                    gate_up(0, B + b, U + b, 0, FB)
                    turn(U + b - 1, FB)
                    gate_up(1, B + b, U + b, 0, FB)
                    down(B + b - 1, U + b - 1, FB)
                turn(U + (NBB - 1), FB)
                down(B + (NBB - 1), U + (NBB - 1), FB)
                pe.wait_ge(pickT_ready, it + 1)
                pe.wait_ge(d_added, U + NBB)
                for m in range(M):
                    for half in range(2):
                        t = mm(ps[:, 3 + 2 * m + half, :], pickT[:, m * P:(m + 1) * P], ye[:, half * FB:(half + 1) * FB],
                               start=True, stop=True)
                t.then_inc(put_done, 1)
            me.barrier("final")

        @block.scalar
        def _(act):
            me = Side(act)
            fn = nc.scalar.activation
            link = lambda ins: me.link(ins, act_order)
            act.wait_ge(x_in, 16)

            def norm(g=None, split=None):
                for m in range(M):
                    fn(xn[:, m, :], x[:, m, :], ACT.Square, accum_out=small[:, m:m + 1]).then_inc(norm_sq, 1)
                me.see(norm_ms)
                fn(small[:, 4:6], small[:, 2:4], ACT.Sqrt).then_inc(norm_rt, 1)
                if g is None:
                    return
                if split is not None:
                    for j in range(4):
                        b = me.s.take(act)
                        for kk_ in range(2):
                            k = 2 * j + kk_
                            t = fn(xh[:, k, :], ps[:, b, kk_ * S:(kk_ + 1) * S], ACT.Copy, scale=col(g, split + k))
                        t.then_inc(norm_h, 1)
                    return
                for j in (1, 3):
                    b = me.a.take(act)
                    for kk_ in range(2):
                        k = 2 * j + kk_
                        for dst, name, off in g:
                            t = fn(dst[:, k, :], ps[:, b, kk_ * S:(kk_ + 1) * S], ACT.Copy, scale=col(name, off + k))
                    t.then_inc(a_read, 1)

            me.barrier("start")
            norm([(uT, "a_norm", 0)])
            me.see(lam_abs)
            fn(lam[:, 1, :], lam[:, 0, :], ACT.Exp, scale=-1.0).then_inc(lam_exp, 1)
            for f in range(KD):
                b = me.a.take(act)
                fn(rg[:, f, :], ps[:, b, 0:S], ACT.Sigmoid, bias=col("a_gate_b", f))
                link(fn(ig[:, f, :], ps[:, b, S:2 * S], ACT.Sigmoid, bias=col("a_gate_b", KD + f)))
                act.nop().then_inc(a_read, 1)
            act.nop().then_inc(ri_ready, 1)
            me.see(la_ready)
            fn(aa[:], rg[:], ACT.Exp).then_inc(a_ready, 1)
            fn(th[:], rg[:], ACT.Tanh).then_inc(th_ready, 1)
            me.see(t2_ready)
            fn(th[:], th[:], ACT.Sqrt, scale=-1.0).then_inc(sq_ready, 1)
            for f in range(KD):
                b = me.a.take(act)
                fn(yg[:, f, :], ps[:, b, 0:S], ACT.Gelu_apprx_tanh).then_inc(a_read, 1)
            act.wait_ge(a_read, me.a.n)
            act.nop().then_inc(yg_ready, 1)

            def wait(s, v):
                if not (isinstance(v, int) and v <= 0):
                    act.wait_ge(s, v)

            users = [g_done, u_done, d_done]

            def high(kind, fills, U, n):
                act.wait_ge(slot_full[kind], fills * 16)
                wait(users[kind], U)
                fn(wh[:, kind, 0:n], raw[:, kind, 0:n], ACT.Copy).then_inc(wh_full[kind], 1)

            def silu(u, w):
                act.wait_ge(g_done, u + 1)
                wait(h_ready, u)
                fn(sg[:, 0:w], ps[:, 0, 0:w], ACT.Silu).then_inc(sg_ready, 1)

            def high_h(u, w):
                act.wait_ge(t_done, u + 1)
                wait(d_done, u)
                fn(hh[:, 0:w], ps[:, 2, 0:w], ACT.Copy).then_inc(hh_ready, 1)

            def ffn(name, g, off):
                nb, wlast, B0, U0 = FFN[name]
                f0 = plan[name]
                high(0, f0[0] + 1, U0, SLOT)
                high(1, f0[1] + 1, U0, SLOT)
                norm(g, split=off)

                def body(b, w, first=False, last=False, wn=FB):
                    u = b * M + U0
                    silu(u, w)
                    if not first:
                        high_h(u - 1, FB)
                    high(2, b + (f0[2] + 1), u, w // P * D)
                    silu(u + 1, w)
                    high_h(u, w)
                    if not last:
                        high(0, b + (f0[0] + 2), u + 2, KD * wn)
                        high(1, b + (f0[1] + 2), u + 2, KD * wn)

                body(0, FB, first=True)
                with act.Fori(1, nb - 2) as b:
                    body(b, FB)
                body(nb - 2, FB, wn=wlast)
                body(nb - 1, wlast, last=True)
                high_h(U0 + nb * M - 1, wlast)

            me.barrier("ffn0")
            ffn("ffn0", "f_norm", 0)

            me.barrier("nsa")
            norm([(uT, "kv_norm", 0), (ubT, "b_norm", 0)])
            for t in range(3):
                b = me.a.take(act)
                fn(kvn[:, 1, t * 512:(t + 1) * 512], ps[:, b, :], ACT.Copy).then_inc(a_read, 1)
                if t == 0:
                    marks["kvc_a"] = me.a.n
                if t == 2:
                    act.wait_ge(a_read, me.a.n)
                    act.nop().then_inc(kvn_ready, 1)
            for t in range(2):
                b = me.a.take(act)
                fn(qn[:, 1, t * 512:(t + 1) * 512], ps[:, b, :], ACT.Copy).then_inc(a_read, 1)
            act.wait_ge(a_read, me.a.n)
            act.nop().then_inc(qn_ready, 1)
            def root(n, rows=P):
                me.see(ms_ready)
                fn(stat[0:rows, 1, 0:n], stat[0:rows, 0, 0:n], ACT.Sqrt).then_inc(root_ready, 1)
            for _ in range(2 * M):
                root(NG)
            for m in range(M):
                b = me.a.take(act)
                fn(kT[:, 0, :, m * P:(m + 1) * P], ps[:, b, :].rearrange("p (g t) -> p g t", g=NG), ACT.Copy).then_inc(a_read, 1)
                b = me.a.take(act)
                fn(kT[:, 1, :, m * P:(m + 1) * P], ps[:, b, :].rearrange("p (g t) -> p g t", g=NG), ACT.Copy).then_inc(a_read, 1)
            for m in range(M):
                root(NH)
            for m in range(M):
                for j in range(2):
                    b = me.a.take(act)
                    fn(qT[:, 4 * j:4 * j + 4, m * P:(m + 1) * P], ps[:, b, :].rearrange("p (g t) -> p g t", g=4),
                       ACT.Copy).then_inc(a_read, 1)
            me.see(gate_ready)
            fn(gate[:], gate[:], ACT.Sigmoid).then_inc(gated, 1)
            b = me.a.take(act)
            for j in range(4):
                t = fn(h1T[:, j, 0:NG * NCMP], ps[:, b, j * 64:j * 64 + NG * NCMP], ACT.Gelu_apprx_tanh, bias=col("cmp_b1", j))
            t.then_inc(a_read, 1)
            root(NG, NCMP)

            def probs(i, m, h):
                nk, st_ = P * (m + 1), stat[:, i % 2, :]
                b = me.s.take(act)
                me.see(max_ready)
                for w in range(2):
                    t = fn(pr[:, i % 2, w * S:w * S + nk], ps[:, b, w * S:w * S + nk], ACT.Exp,
                           bias=st_[:, 4 + w:5 + w], scale=SCALE, accum_out=st_[:, 7 + w:8 + w])
                t.then_inc(s_read, 1)
                fn(pr[:, i % 2, 512:512 + NCMP], pr[:, i % 2, 512:512 + NCMP], ACT.Exp, bias=st_[:, 3:4], scale=SCALE,
                   accum_out=st_[:, 6:7]).then_inc(p_ready, 1)

            def turned(m):
                b = me.a.take(act)
                n = 2 * (m + 1) * P
                fn(pT[:, 0:n], ps[:, b, 0:n], ACT.Copy).then_inc(a_read, 1)
                b = me.a.take(act)
                fn(pcT[0:NCMP, :], ps[0:NCMP, b, 0:P], ACT.Copy).then_inc(a_read, 1)

            pairs = [(m, h) for m in range(M) for h in range(NH)]
            probs(0, *pairs[0])
            for i, (m, h) in enumerate(pairs):
                if i + 1 < len(pairs):
                    probs(i + 1, *pairs[i + 1])
                turned(m)
            for m in range(M):
                for j in range(2):
                    b = me.a.take(act)
                    fn(oT[:, 4 * j:4 * j + 4, m * P:(m + 1) * P], ps[:, b, :].rearrange("p (g t) -> p g t", g=4),
                       ACT.Copy).then_inc(a_read, 1)

            me.barrier("ffn1")
            ffn("ffn1", "f_norm", KD)

            def mixer(layer):
                norm([(uT, "mix_norm_2", layer * KD)])
                me.see(lb_max)
                fn(lbt[:, 1:3, :], lbt[:, 1:3, :], ACT.Exp).then_inc(lb_exp, 1)
                me.see(lb_clamped)
                fn(lbt[:, 5:7, :], lbt[:, 5:7, :], ACT.Ln).then_inc(lb_ln, 1)
                for c in range(4):
                    b = me.a.take(act)
                    fn(qh[:, c, :], ps[:, b, 0:S], ACT.Silu).then_inc(a_read, 1)
                act.wait_ge(a_read, me.a.n)
                act.nop().then_inc(qh_ready, 1)
                me.see(zabs_ready)
                link(fn(t1[:], t1[:], ACT.Exp))
                fn(t2[:], t1[:], ACT.Ln, bias=1.0).then_inc(zln_ready, 1)
                me.see(zdif_ready)
                fn(kk[:], t1[:], ACT.Exp).then_inc(kk_ready, 1)
                me.see(fabs_ready)
                link(fn(t2[:], t2[:], ACT.Exp))
                fn(t2[:], t2[:], ACT.Ln, bias=1.0).then_inc(fln_ready, 1)
                for c in range(4):
                    b = me.a.take(act)
                    fn(sqT[:, c, :], ps[:, b, 0:S], ACT.Copy, scale=HD ** -0.5).then_inc(a_read, 1)
                dests = [(hv, 0, ACT.Copy), (sv, 0, ACT.Copy), (hog, 0, ACT.Silu), (sga, 0, ACT.Sigmoid),
                         (sga, 512, ACT.Sigmoid), (sgb, 0, ACT.Sigmoid), (sgb, 512, ACT.Sigmoid)]
                for j, lv in enumerate([0] + LEVELS + [64, 128]):
                    if j < len(dests):
                        dst, c0, f = dests[j]
                        for m in range(M):
                            b = me.a.take(act)
                            fn(dst[:, m, c0:c0 + 512], ps[:, b, :], f).then_inc(a_read, 1)
                    if lv:
                        me.see(decay_ready)
                        fn(t1[:], t1[:], ACT.Exp).then_inc(decay_exp, 1)
                me.see(oms_ready)
                fn(small[:, 24:32], small[:, 16:24], ACT.Sqrt).then_inc(ort_ready, 1)

                def soft(h):
                    b = me.s.take(act)
                    link(fn(e1[:, h % 2, :], ps[:, b, 0:384], ACT.Abs))
                    link(fn(e1[:, h % 2, :], e1[:, h % 2, :], ACT.Exp, scale=-1.0))
                    fn(e1[:, h % 2, :], e1[:, h % 2, :], ACT.Ln, bias=1.0).then_inc(ln_ready, 1)

                soft(0)
                for h in range(SH):
                    if h + 1 < SH:
                        soft(h + 1)
                    b = me.a.take(act)
                    fn(wt[:, h % 2, :], ps[:, b, 0:384], ACT.Exp).then_inc(a_read, 1)
                for m in range(M):
                    b = me.a.take(act)
                    fn(oaT[:, :, m * P:(m + 1) * P], ps[:, b, :].rearrange("p (k t) -> p k t", k=4), ACT.Copy).then_inc(a_read, 1)
                for j in range(4):
                    b = me.a.take(act)
                    fn(uT[:, 2 * j:2 * j + 2, :].rearrange("p k t -> p (k t)"), ps[:, b, :], ACT.Copy).then_inc(a_read, 1)

            me.barrier("mix0")
            mixer(0)
            me.barrier("ffn2")
            ffn("ffn2", "ffn_norm_2", 0)
            me.barrier("mix1")
            mixer(1)

            me.barrier("moe")
            norm([(uT, "ffn_norm_2", KD)])
            me.see(lmax_ready)
            for m in range(M):
                t = fn(R_["exp"][:, m * E:(m + 1) * E], R_["logit"][:, m * E:(m + 1) * E], ACT.Exp, bias=R_["neg_max"][:, m:m + 1])
            t.then_inc(lexp_ready, 1)
            act.wait_ge(items_ready, 1)
            f0 = plan["moe"]
            n = act.value_load(rti[0:1, 0:1], min_val=1, max_val=ITEMS)
            with act.Fori(0, n) as it:
                U = it * NBB + MOE_U
                F = [it * NBB + (f0[s] + 1) for s in range(3)]
                high(0, F[0], U, SLOT)
                high(1, F[1], U, SLOT)
                act.wait_ge(picked, it + 1)
                act.wait_ge(u_done, U)
                for j in range(2):
                    t = fn(xh[:, 4 * j:4 * j + 4, 0:P], ps[:, 5 + j, :].rearrange("p (k t) -> p k t", k=4), ACT.Copy)
                t.then_inc(xh_ready, 1)
                act.wait_ge(pickT_done, it + 1)
                fn(pickT, ps[:, 7, 0:S], ACT.Copy).then_inc(pickT_ready, 1)
                silu(U, FB)
                high(0, F[0] + 1, U + 1, SLOT)
                high(1, F[1] + 1, U + 1, SLOT)
                high(2, F[2], U, SLOT)
                with act.Fori(1, NBB - 1) as b:
                    silu(U + b, FB)
                    high_h(U + b - 1, FB)
                    high(0, F[0] + b + 1, U + b + 1, SLOT)
                    high(1, F[1] + b + 1, U + b + 1, SLOT)
                    high(2, F[2] + b, U + b, SLOT)
                silu(U + (NBB - 1), FB)
                high_h(U + (NBB - 2), FB)
                high(2, F[2] + (NBB - 1), U + (NBB - 1), SLOT)
                high_h(U + (NBB - 1), FB)
            me.barrier("final")
            norm()

        @block.vector
        def _(dve):
            me = Side(dve)
            v = nc.vector
            link = lambda ins: me.link(ins, dve_order)

            def norm(g=None, split=None):
                me.norms += 1
                me.see(norm_sq, M)
                v.tensor_scalar(small[:, 2:4], small[:, 0:2], 1.0 / D, EPS, ALU.mult, ALU.add).then_inc(norm_ms, 1)
                me.see(norm_rt)
                link(v.reciprocal(small[:, 6:8], small[:, 4:6]))
                for m in range(M):
                    v.tensor_scalar(xn[:, m, :], x[:, m, :], small[:, 6 + m:7 + m], None, ALU.mult).then_inc(norm_xn, 1)
                if g is None:
                    return
                if split is not None:
                    for j in range(4):
                        b = me.s.take(dve)
                        me.see(norm_h)
                        for kk_ in range(2):
                            k = 2 * j + kk_
                            t = v.scalar_tensor_tensor(xl[:, k, :], ps[:, b, kk_ * S:(kk_ + 1) * S], col(g, split + k),
                                                       xh[:, k, :].bitcast(F32), ALU.mult, ALU.subtract)
                        t.then_inc(s_read, 1)
                    return
                for j in (0, 2):
                    b = me.v.take(dve)
                    for kk_ in range(2):
                        k = 2 * j + kk_
                        for dst, name, off in g:
                            t = v.tensor_scalar(dst[:, k, :], ps[:, b, kk_ * S:(kk_ + 1) * S], col(name, off + k), None, ALU.mult)
                    t.then_inc(v_read, 1)

            def residual(t, m):
                b = me.v.take(dve)
                xs = x[:, m, t * 512:(t + 1) * 512]
                v.tensor_tensor(xs, xs, ps[:, b, :], ALU.add).then_inc(v_read, 1)

            for g in range(2):
                b = me.v.take(dve)
                v.tensor_copy(cols[:, g * P:g * P + ROWS_USED[g]], ps[:, b, 0:ROWS_USED[g]]).then_inc(v_read, 1)
            dve.wait_ge(v_read, me.v.n)
            dve.wait_ge(bc_in, 16 * len(BC))
            dve.wait_ge(x_in, 16)

            me.barrier("start")
            norm([(uT, "a_norm", 0)])
            link(v.memset(zp[:, :, 0:CONV - 1], 0.0))
            la = col("a_lambda", 0, KD)
            link(v.tensor_scalar(lam[:, 2, :], la, -1.0, None, ALU.mult))
            v.tensor_tensor(lam[:, 0, :], lam[:, 2, :], la, ALU.max).then_inc(lam_abs, 1)
            me.see(lam_exp)
            link(v.tensor_scalar(lam[:, 3, :], lam[:, 1, :], 2.0, None, ALU.add))
            link(v.reciprocal(lam[:, 3, :], lam[:, 3, :]))
            link(v.tensor_tensor(lam[:, 3, :], lam[:, 1, :], lam[:, 3, :], ALU.mult))
            link(v.tensor_tensor(lam[:, 4, :], lam[:, 3, :], lam[:, 3, :], ALU.mult))
            link(v.tensor_scalar(lam[:, 5, :], lam[:, 4, :], 1.0 / 17, 1.0 / 15, ALU.mult, ALU.add))
            for d in (13, 11, 9, 7, 5, 3, 1):
                link(v.tensor_tensor(lam[:, 5, :], lam[:, 5, :], lam[:, 4, :], ALU.mult))
                link(v.tensor_scalar(lam[:, 5, :], lam[:, 5, :], 1.0 / d, None, ALU.add))
            link(v.tensor_tensor(lam[:, 5, :], lam[:, 5, :], lam[:, 3, :], ALU.mult))
            link(v.tensor_scalar(lam[:, 6, :], lam[:, 2, :], 0.0, None, ALU.max))
            link(v.scalar_tensor_tensor(lam[:, 6, :], lam[:, 5, :], 2.0, lam[:, 6, :], ALU.mult, ALU.add))
            link(v.tensor_scalar(lam[:, 7, :], lam[:, 6, :], -LRU_C, None, ALU.mult))
            for f in range(KD):
                b = me.v.take(dve)
                v.tensor_copy(zp[:, f, CONV - 1:], ps[:, b, 0:S]).then_inc(v_read, 1)
                dve.wait_ge(v_read, me.v.n)
                link(v.tensor_scalar(xr[:, f, :], zp[:, f, 0:S], col("a_conv_w", f), col("a_conv_b", f), ALU.mult, ALU.add))
                for k in range(1, CONV):
                    t = v.scalar_tensor_tensor(xr[:, f, :], zp[:, f, k:k + S], col("a_conv_w", k * KD + f), xr[:, f, :],
                                               ALU.mult, ALU.add)
                    if k < CONV - 1:
                        link(t)
                t.then_inc(xr_ready, 1)
            me.see(ri_ready)
            v.tensor_tensor(rg[:], rg[:], lam[:, 7, :].unsqueeze(2).to_broadcast([P, KD, S]), ALU.mult).then_inc(la_ready, 1)
            link(v.tensor_tensor(ig[:], ig[:], xr[:], ALU.mult))
            me.see(a_ready)
            link(v.tensor_tensor(xr[:], aa[:], aa[:], ALU.mult))
            link(v.memset(aa[:, :, 0:1], 0.0))
            me.see(th_ready)
            v.scalar_tensor_tensor(th[:], xr[:], 1.0, th[:], ALU.add, ALU.mult).then_inc(t2_ready, 1)
            me.see(sq_ready)
            link(v.tensor_tensor(ig[:], ig[:], th[:], ALU.mult))
            link(v.tensor_tensor_scan(rg[:].rearrange("p k t -> p (k t)"), aa[:].rearrange("p k t -> p (k t)"),
                                      ig[:].rearrange("p k t -> p (k t)"), 0.0, ALU.mult, ALU.add))
            me.see(yg_ready)
            v.tensor_tensor(rg[:], rg[:], yg[:], ALU.mult).then_inc(yh_ready, 1)
            for t in range(2):
                for m in range(M):
                    residual(t, m)

            def wait(s, val):
                if not (isinstance(val, int) and val <= 0):
                    dve.wait_ge(s, val)

            def low(kind, B, n):
                dve.wait_ge(wh_full[kind], B + 1)
                v.tensor_tensor(wl[:, kind, 0:n], raw[:, kind, 0:n], wh[:, kind, 0:n].bitcast(F32),
                                ALU.subtract).then_inc(wl_full[kind], 1)

            def hidden(u, w):
                dve.wait_ge(sg_ready, u + 1)
                dve.wait_ge(u_done, u + 1)
                wait(t_done, u)
                v.tensor_tensor(hb[:, 0:w], ps[:, 1, 0:w], sg[:, 0:w], ALU.mult).then_inc(h_ready, 1)

            def low_h(u, w):
                dve.wait_ge(hh_ready, u + 1)
                v.tensor_tensor(hl[:, 0:w], ps[:, 2, 0:w], hh[:, 0:w].bitcast(F32), ALU.subtract).then_inc(hl_ready, 1)

            def add_down(u, dst):
                dve.wait_ge(d_done, u + 1)
                for half in range(2):
                    o = dst[:, half * FB:(half + 1) * FB]
                    t = v.tensor_tensor(o, o, ps[:, 3 + half, :], ALU.add)
                t.then_inc(d_added, 1)

            def ffn(name, g, off):
                nb, wlast, B0, U0 = FFN[name]
                low(0, B0, SLOT)
                low(1, B0, SLOT)
                norm(g, split=off)

                def body(b, w, first=False, last=False, wn=FB):
                    u, B = b * M + U0, b + B0
                    if not first:
                        low_h(u - 1, FB)
                    hidden(u, w)
                    if not first:
                        add_down(u - 1, x[:, 1, :])
                    low(2, B, w // P * D)
                    low_h(u, w)
                    if not last:
                        low(0, B + 1, KD * wn)
                    hidden(u + 1, w)
                    if not last:
                        low(1, B + 1, KD * wn)
                    add_down(u, x[:, 0, :])

                body(0, FB, first=True)
                with dve.Fori(1, nb - 2) as b:
                    body(b, FB)
                body(nb - 2, FB, wn=wlast)
                body(nb - 1, wlast, last=True)
                low_h(U0 + nb * M - 1, wlast)
                add_down(U0 + nb * M - 1, x[:, 1, :])

            me.barrier("ffn0")
            ffn("ffn0", "f_norm", 0)

            me.barrier("nsa")
            norm([(uT, "kv_norm", 0), (ubT, "b_norm", 0)])
            for t in range(3):
                b = me.v.take(dve)
                v.tensor_copy(kvn[:, 0, t * 512:(t + 1) * 512], ps[:, b, :]).then_inc(v_read, 1)
                if t == 0:
                    marks["kvc_v"] = me.v.n
            def tables(dst, cos, sin, g, rows=P):
                v.tensor_tensor(dst[0:rows, 0, :], C(cos, rows), g[0:rows], ALU.mult)
                link(v.tensor_tensor(dst[0:rows, 1, :], C(sin, rows), g[0:rows], ALU.mult))

            gq, gk = bc[:, 0:HD], [bc[:, 64 + i * HD:64 + (i + 1) * HD] for i in range(3)]
            for m in range(M):
                tables(rope_g[:, m], f"cos{m}", f"sin{m}", gq)
                for w in range(2):
                    tables(rope_k[:, m, w], f"cos{m}", f"sin{m}", gk[1 + w])
            tables(rope_g[:, 2], "cosc", "sinc", gk[0], NCMP)

            def rope_norm(src, out, table, n, rows=P):
                a = tmp_a[0:rows, 0:n * HD].rearrange("p (h d) -> p h d", d=HD)
                b2 = tmp_b[0:rows, 0:n * HD].rearrange("p (h d) -> p h d", d=HD)
                link(v.tensor_tensor(a, src, src, ALU.mult))
                link(v.tensor_reduce(stat[0:rows, 0, 0:n], a, AX.X, ALU.add))
                link(v.tensor_scalar(stat[0:rows, 0, 0:n], stat[0:rows, 0, 0:n], 1.0 / HD, EPS, ALU.mult, ALU.add))
                dve.nop().then_inc(ms_ready, 1)
                me.see(root_ready)
                link(v.reciprocal(stat[0:rows, 1, 0:n], stat[0:rows, 1, 0:n]))
                link(v.tensor_tensor(a, src, stat[0:rows, 1, 0:n].unsqueeze(2).to_broadcast([rows, n, HD]), ALU.mult))
                link(v.tensor_tensor(b2, a, table[0:rows, 1, :].unsqueeze(1).to_broadcast([rows, n, HD]), ALU.mult))
                link(v.tensor_tensor(a, a, table[0:rows, 0, :].unsqueeze(1).to_broadcast([rows, n, HD]), ALU.mult))
                hf = HD // 2
                v.tensor_tensor(out[:, :, 0:hf], a[:, :, 0:hf], b2[:, :, hf:], ALU.subtract)
                link(v.tensor_tensor(out[:, :, hf:], a[:, :, hf:], b2[:, :, 0:hf], ALU.add))

            for t in range(2):
                b = me.v.take(dve)
                v.tensor_copy(qn[:, 0, t * 512:(t + 1) * 512], ps[:, b, :]).then_inc(v_read, 1)
            for m in range(M):
                b = me.v.take(dve)
                v.tensor_tensor(gate[:, m, :, :].rearrange("p b h -> p (b h)"), ps[:, b, 0:3 * NH], bc[:, 384:384 + 3 * NH],
                                ALU.add).then_inc(v_read, 1)
            dve.wait_ge(v_read, me.v.n)
            dve.nop().then_inc(gate_ready, 1)
            me.see(kvn_ready)
            for m in range(M):
                for w in range(2):
                    o = 512 + w * 512
                    kd = kdup[:, m, w]
                    rope_norm(kvn[:, m, o:o + NG * HD].rearrange("p (g d) -> p g d", d=HD), kd[:, :, 0, :],
                              rope_k[:, m, w], NG)
                    link(v.tensor_copy(kd[:, :, 1, :], kd[:, :, 0, :]))
            dve.nop().then_inc(k_ready, 1)
            me.see(qn_ready)
            for m in range(M):
                qh_ = qn[:, m, :].rearrange("p (h d) -> p h d", d=HD)
                rope_norm(qh_, qh_, rope_g[:, m], NH)
                dve.nop().then_inc(q_ready, 1)
            R = NG * NCMP
            for j in range(4):
                b = me.v.take(dve)
                src = ps[:, b, 0:8 * R].rearrange("p (i k c) -> p i k c", i=4, k=2)
                for kv in range(2):
                    t = v.tensor_tensor(xcT[:, kv, 4 * j:4 * j + 4, :], src[:, :, kv, :],
                                        col("cmp_pos", kv * 16 + 4 * j, 4).unsqueeze(2).to_broadcast([P, 4, R]), ALU.add)
                t.then_inc(v_read, 1)
            b = me.v.take(dve)
            b2v = bc[0:NCMP, 256:256 + 2 * HD].rearrange("p (k d) -> p k d", k=2)
            for kv in range(2):
                t = v.tensor_tensor(cmpn[0:NCMP, kv], ps[0:NCMP, b, kv * 256:(kv + 1) * 256].rearrange("p (g d) -> p g d", g=NG),
                                    b2v[:, kv, :].unsqueeze(1).to_broadcast([NCMP, NG, HD]), ALU.add)
            t.then_inc(v_read, 1)
            dve.wait_ge(v_read, me.v.n)
            rope_norm(cmpn[0:NCMP, 0], kcdup[0:NCMP, :, 0, :], rope_g[:, 2], NG, NCMP)
            link(v.tensor_copy(kcdup[0:NCMP, :, 1, :], kcdup[0:NCMP, :, 0, :]))
            dve.nop().then_inc(kc_ready, 1)
            b = me.v.take(dve)
            v.tensor_copy(kcT[:, :, 0:NCMP], ps[:, b, 0:64].rearrange("p (g c) -> p g c", g=NG)[:, :, 0:NCMP]).then_inc(v_read, 1)
            me.see(gated)
            link(v.tensor_scalar(gate[:, 0, 0, :], gate[:, 0, 0, :], C("row_valid"), None, ALU.mult))

            def maxima(i, m, h):
                nk, st_ = P * (m + 1), stat[:, i % 2, :]
                b = me.s.take(dve)
                v.tensor_reduce(st_[:, 1:3], ps[:, b, :].rearrange("p (w k) -> p w k", w=2)[:, :, 0:nk], AX.X, ALU.max)
                b = me.v.take(dve)
                v.tensor_copy(pr[:, i % 2, 512:512 + NCMP], ps[:, b, 0:NCMP]).then_inc(v_read, 1)
                dve.wait_ge(v_read, me.v.n)
                link(v.tensor_reduce(st_[:, 0:1], pr[:, i % 2, 512:512 + NCMP], AX.X, ALU.max))
                v.tensor_scalar(st_[:, 3:6], st_[:, 0:3], -SCALE, None, ALU.mult).then_inc(max_ready, 1)

            def combine(i, m, h):
                st_ = stat[:, i % 2, :]
                me.see(p_ready)
                link(v.reciprocal(st_[:, 9:12], st_[:, 6:9]))
                link(v.tensor_tensor(st_[:, 12:15], st_[:, 9:12], gate[:, m, :, h], ALU.mult))
                b = me.v.take(dve)
                o = qn[:, m, h * HD:(h + 1) * HD]
                link(v.tensor_scalar(o, ps[:, b, 0:HD], st_[:, 13:14], None, ALU.mult))
                link(v.scalar_tensor_tensor(o, ps[:, b, HD:2 * HD], st_[:, 14:15], o, ALU.mult, ALU.add))
                v.scalar_tensor_tensor(o, ps[:, b, 2 * HD:3 * HD], st_[:, 12:13], o, ALU.mult, ALU.add).then_inc(v_read, 1)

            pairs = [(m, h) for m in range(M) for h in range(NH)]
            maxima(0, *pairs[0])
            for i, (m, h) in enumerate(pairs):
                if i + 1 < len(pairs):
                    maxima(i + 1, *pairs[i + 1])
                combine(i, m, h)
            for t in range(2):
                for m in range(M):
                    residual(t, m)

            me.barrier("ffn1")
            ffn("ffn1", "f_norm", KD)

            def mixer(layer):
                norm([(uT, "mix_norm_2", layer * KD)])
                lg = [col("hgrn_lb_logits_2", i * HH, HH) for i in range(2)]
                link(v.tensor_copy(lbt[:, 7, :], lg[0]))
                link(v.tensor_tensor(lbt[:, 0, :], lbt[:, 7, :], lg[1], ALU.max))
                for i in range(2):
                    link(v.tensor_tensor(lbt[:, 1 + i, :], lg[i], lbt[:, 0, :], ALU.subtract))
                dve.nop().then_inc(lb_max, 1)
                me.see(lb_exp)
                link(v.tensor_tensor(lbt[:, 7, :], lbt[:, 1, :], lbt[:, 2, :], ALU.add))
                link(v.reciprocal(lbt[:, 7, :], lbt[:, 7, :]))
                for i in range(2):
                    link(v.tensor_tensor(lbt[:, 1 + i, :], lbt[:, 1 + i, :], lbt[:, 7, :], ALU.mult))
                link(v.tensor_copy(lbt[:, 3, :], lbt[:, 1, :]))
                if layer:
                    link(v.tensor_tensor(lbt[:, 3, :], lbt[:, 1, :], lbt[:, 2, :], ALU.add))
                link(v.tensor_tensor(lbt[:, 3, :], lbt[:, 3, :], lbt[:, 1, :], ALU.subtract))
                link(v.tensor_scalar(lbt[:, 4, :], lbt[:, 3, :], -1.0, 1.0, ALU.mult, ALU.add))
                link(v.tensor_scalar(lbt[:, 5:7, :], lbt[:, 3:5, :], 1e-12, None, ALU.max))
                dve.nop().then_inc(lb_clamped, 1)
                me.see(lb_ln)
                link(v.tensor_scalar(lbt[:, 1:3, :], lbt[:, 3:5, :], 1e-12, NEG, ALU.is_lt, ALU.mult))
                link(v.tensor_tensor(lbt[:, 5:7, :], lbt[:, 5:7, :], lbt[:, 1:3, :], ALU.add))

                def per_head(i):
                    return lbt[:, i, :].unsqueeze(2).to_broadcast([P, HH, S])

                for c in range(4):
                    b = me.v.take(dve)
                    v.tensor_copy(zf[:, c, :], ps[:, b, 0:S]).then_inc(v_read, 1)
                dve.wait_ge(v_read, me.v.n)
                link(v.scalar_tensor_tensor(t1[:], zf[:], -1.0, zf[:], ALU.mult, ALU.min))
                dve.nop().then_inc(zabs_ready, 1)
                link(v.memset(keep[:], 1.0))
                link(v.memset(keep[:].rearrange("p h (c s) -> p (h c) s", s=HC)[:, :, 0:1], 0.0))
                link(v.memset(sd[:], 0.0))
                dve.wait_ge(masks_in, 16 * (layer + 1))
                link(v.tensor_copy(lmask[:], t3[:].rearrange("p h t -> p (h t)")))
                me.see(zln_ready)
                link(v.scalar_tensor_tensor(t3[:], zf[:], 0.0, t2[:], ALU.min, ALU.subtract))
                link(v.tensor_tensor(t1[:], t3[:], zf[:], ALU.subtract))
                dve.nop().then_inc(zdif_ready, 1)
                link(v.tensor_tensor(t3[:], t3[:], per_head(6), ALU.add))
                link(v.tensor_tensor(t2[:], t3[:], per_head(5), ALU.subtract))
                link(v.scalar_tensor_tensor(t2[:], t2[:], -1.0, t2[:], ALU.mult, ALU.min))
                dve.nop().then_inc(fabs_ready, 1)
                link(v.tensor_tensor(t3[:], t3[:], per_head(5), ALU.max))
                me.see(kk_ready)
                link(v.tensor_tensor(kk[:], kk[:], per_head(4), ALU.mult))
                me.see(fln_ready)
                link(v.tensor_tensor(t3[:], t3[:], t2[:], ALU.add))
                flat = lambda a: a[:].rearrange("p h t -> p (h t)")
                link(v.tensor_tensor_scan(flat(bb), flat(keep), flat(t3), 0.0, ALU.mult, ALU.add))
                for c in range(4):
                    b = me.v.take(dve)
                    v.tensor_copy(skT[:, c, :], ps[:, b, 0:S]).then_inc(v_read, 1)
                me.see(qh_ready)

                def exponents(lv):
                    if lv <= 32:
                        bv = flat(bb).rearrange("p (n s) -> p n s", s=2 * lv)
                        tv = flat(t1).rearrange("p (n s) -> p n s", s=2 * lv)
                        mid = bv[:, :, lv - 1:lv].to_broadcast([P, HH * S // (2 * lv), lv])
                        v.tensor_tensor(tv[:, :, 0:lv], mid, bv[:, :, 0:lv], ALU.subtract)
                        link(v.tensor_tensor(tv[:, :, lv:], bv[:, :, lv:], mid, ALU.subtract))
                        return
                    chunk = lambda a, c: a[:, :, c * HC:(c + 1) * HC]
                    last = lambda c: bb[:, :, c * HC + HC - 1:c * HC + HC].to_broadcast([P, HH, HC])
                    if lv == 64:
                        for c in (0, 2):
                            v.tensor_tensor(chunk(t1, c), last(c), chunk(bb, c), ALU.subtract)
                        for c in (1, 3):
                            t = v.tensor_copy(chunk(t1, c), chunk(bb, c))
                        link(t)
                        return
                    v.tensor_tensor(chunk(t1, 1), last(1), chunk(bb, 1), ALU.subtract)
                    v.tensor_copy(chunk(t1, 2), chunk(bb, 2))
                    v.tensor_tensor(chunk(t1, 3), chunk(bb, 3), last(2), ALU.add)
                    link(v.tensor_tensor(chunk(t1, 0), last(0), chunk(bb, 0), ALU.subtract))
                    link(v.tensor_tensor(chunk(t1, 0), chunk(t1, 0), last(1), ALU.add))

                def factors(lv):
                    sz = 2 * lv
                    view = lambda a: flat(a).rearrange("p (n s) -> p n s", s=sz)
                    v.tensor_tensor(view(t2)[:, :, 0:lv], view(kk)[:, :, 0:lv], view(t1)[:, :, 0:lv], ALU.mult)
                    link(v.tensor_tensor(view(t2)[:, :, lv:], view(qh)[:, :, lv:], view(t1)[:, :, lv:], ALU.mult))

                def collect(j, lv):
                    if lv == 128:
                        b = me.v.take(dve)
                        v.tensor_copy(sx[:].rearrange("p h t -> p (h t)"), ps[:, b, :]).then_inc(v_read, 1)
                        dve.wait_ge(v_read, me.v.n)
                        return
                    mask = lmask[:, j * P:(j + 1) * P].unsqueeze(1).to_broadcast([P, 4, P])
                    for hp in range(2):
                        b = me.v.take(dve)
                        v.copy_predicated(sd[:, 2 * hp:2 * hp + 2].rearrange("p a m t -> p (a m) t"), mask,
                                          ps[:, b, :].rearrange("p (n t) -> p n t", n=4)).then_inc(v_read, 1)
                    dve.wait_ge(v_read, me.v.n)

                levels = [0] + LEVELS + [64, 128]
                for j, lv in enumerate(levels):
                    if lv:
                        exponents(lv)
                        dve.nop().then_inc(decay_ready, 1)
                        collect(j - 1, levels[j - 1])
                        me.see(decay_exp)
                        factors(lv)
                    dve.nop().then_inc(level_ready, 1)
                collect(len(levels) - 1, 128)
                for m in range(M):
                    b = me.v.take(dve)
                    v.tensor_copy(oa[:, m, :], ps[:, b, :]).then_inc(v_read, 1)
                dve.wait_ge(v_read, me.v.n)
                o8 = oa[:].rearrange("p m (h d) -> p (m h) d", d=P)
                t8 = flat(t1).rearrange("p (n d) -> p n d", d=P)
                link(v.tensor_tensor(t8, o8, o8, ALU.mult))
                link(v.tensor_reduce(small[:, 16:24], t8, AX.X, ALU.add))
                link(v.tensor_scalar(small[:, 16:24], small[:, 16:24], 1.0 / P, EPS, ALU.mult, ALU.add))
                dve.nop().then_inc(oms_ready, 1)
                me.see(ort_ready)
                link(v.reciprocal(small[:, 32:40], small[:, 24:32]))
                link(v.tensor_tensor(o8, o8, small[:, 32:40].unsqueeze(2).to_broadcast([P, 8, P]), ALU.mult))
                g = bc[:, 432 + layer * P:432 + (layer + 1) * P].unsqueeze(1).to_broadcast([P, 8, P])
                link(v.tensor_tensor(o8, o8, g, ALU.mult))
                link(v.tensor_tensor(oa[:], oa[:], hog[:], ALU.mult))
                dve.nop().then_inc(oa_ready, 1)

                for h in range(SH):
                    b = me.s.take(dve)
                    me.see(ln_ready)
                    s_ = sp[:, h % 2, :]
                    v.scalar_tensor_tensor(s_, ps[:, b, 0:384], 0.0, e1[:, h % 2, :], ALU.max, ALU.add).then_inc(s_read, 1)
                    dve.wait_ge(s_read, me.s.n)
                    diag = s_.rearrange("p (a t) -> p a t", t=P)[:, 0:3:2, :]
                    v.tensor_tensor(diag, diag, C("before").unsqueeze(1).to_broadcast([P, 2, P]), ALU.mult).then_inc(sp_ready, 1)
                    if h % 2:
                        b = me.v.take(dve)
                        v.tensor_copy(obT[:, h // 2, :], ps[:, b, 0:S]).then_inc(v_read, 1)
                for m in range(M):
                    for half in range(2):
                        cs = slice(half * 512, half * 512 + 512)
                        b = me.v.take(dve)
                        v.tensor_tensor(sga[:, m, cs], ps[:, b, :], sga[:, m, cs], ALU.mult).then_inc(v_read, 1)
                        b = me.v.take(dve)
                        v.tensor_tensor(sgb[:, m, cs], ps[:, b, :], sgb[:, m, cs], ALU.mult).then_inc(v_read, 1)
                dve.wait_ge(v_read, me.v.n)
                v.tensor_tensor(sga[:], sga[:], sgb[:], ALU.add).then_inc(y_ready, 1)
                for t in range(2):
                    for m in range(M):
                        residual(t, m)

            me.barrier("mix0")
            mixer(0)
            me.barrier("ffn2")
            ffn("ffn2", "ffn_norm_2", 0)
            me.barrier("mix1")
            mixer(1)

            me.barrier("moe")
            norm([(uT, "ffn_norm_2", KD)])
            dve.wait_ge(ye_in, 16)
            b = me.v.take(dve)
            v.tensor_copy(R_["logit"], ps[:, b, 0:M * E]).then_inc(v_read, 1)
            dve.wait_ge(v_read, me.v.n)
            for m in range(M):
                lm = R_["logit"][:, m * E:(m + 1) * E]
                ge8 = R_["a64"].rearrange("p (e f) -> p e f", e=E)
                eq8 = R_["b64"].rearrange("p (e f) -> p e f", e=E)
                mine, other = lm.unsqueeze(2).to_broadcast([P, E, E]), lm.unsqueeze(1).to_broadcast([P, E, E])
                link(v.tensor_tensor(ge8, other, mine, ALU.is_gt))
                link(v.tensor_tensor(eq8, other, mine, ALU.is_equal))
                link(v.tensor_tensor(R_["b64"], R_["b64"], C("lower_e"), ALU.mult))
                link(v.tensor_tensor(R_["a64"], R_["a64"], R_["b64"], ALU.add))
                link(v.tensor_reduce(R_["rank"], ge8, AX.X, ALU.add))
                link(v.tensor_scalar(sel[:, m, :], R_["rank"], 1.5, None, ALU.is_lt))
                link(v.tensor_reduce(R_["neg_max"][:, m:m + 1], lm, AX.X, ALU.max))
            link(v.tensor_scalar(R_["neg_max"], R_["neg_max"], -1.0, None, ALU.mult))
            dve.nop().then_inc(sel_ready, 1)
            dve.nop().then_inc(lmax_ready, 1)
            me.see(lexp_ready)
            for m in range(M):
                wm = R_["weight"][:, m * E:(m + 1) * E]
                link(v.tensor_tensor(wm, R_["exp"][:, m * E:(m + 1) * E], sel[:, m, :], ALU.mult))
                link(v.tensor_reduce(R_["sum"][:, m:m + 1], wm, AX.X, ALU.add))
                link(v.reciprocal(R_["sum"][:, m:m + 1], R_["sum"][:, m:m + 1]))
                link(v.tensor_scalar(wm, wm, R_["sum"][:, m:m + 1], None, ALU.mult))
            b = me.v.take(dve)
            v.tensor_copy(R_["pos"], ps[:, b, 0:3 * E]).then_inc(v_read, 1)
            dve.wait_ge(v_read, me.v.n)
            count = R_["pos"][:, 2 * E:3 * E]
            link(v.tensor_scalar(R_["tiles"], count, 0.5, None, ALU.is_gt))
            link(v.tensor_scalar(R_["ones"], count, P + 0.5, None, ALU.is_gt))
            link(v.tensor_tensor(R_["tiles"], R_["tiles"], R_["ones"], ALU.add))
            link(v.memset(R_["ones"], 1.0))
            link(v.tensor_tensor_scan(R_["upto"], R_["ones"], R_["tiles"], 0.0, ALU.mult, ALU.add))
            link(v.tensor_tensor(R_["before"], R_["upto"], R_["tiles"], ALU.subtract))
            shape = [P, ITEMS, E]
            own = R_["owner"].rearrange("p (i e) -> p i e", i=ITEMS)
            tmp = R_["tmp"].rearrange("p (i e) -> p i e", i=ITEMS)
            iota_i = C("iota_i").unsqueeze(2).to_broadcast(shape)
            over_e = lambda a: a.unsqueeze(1).to_broadcast(shape)
            link(v.tensor_tensor(own, iota_i, over_e(R_["before"]), ALU.is_ge))
            link(v.tensor_tensor(tmp, iota_i, over_e(R_["upto"]), ALU.is_lt))
            link(v.tensor_tensor(own, own, tmp, ALU.mult))

            def of_item(dst, a):
                link(v.tensor_tensor(tmp, own, over_e(a), ALU.mult))
                link(v.tensor_reduce(dst, tmp, AX.X, ALU.add))

            of_item(R_["expert"], C("iota_e"))
            of_item(R_["first"], R_["before"])
            link(v.tensor_tensor(R_["first"], C("iota_i"), R_["first"], ALU.subtract))
            link(v.tensor_scalar(R_["first"], R_["first"], float(P), None, ALU.mult))
            for m in range(M):
                sl, wi = slot_of[:, m, :], weight_of[:, m, :]
                of_item(wi, R_["weight"][:, m * E:(m + 1) * E])
                of_item(sl, R_["pos"][:, m * E:(m + 1) * E])
                of_item(R_["there"], sel[:, m, :])
                link(v.tensor_tensor(sl, sl, R_["first"], ALU.subtract))
                link(v.tensor_scalar(sl, sl, 1.0, None, ALU.add))
                link(v.tensor_tensor(sl, sl, R_["there"], ALU.mult))
                link(v.tensor_scalar(sl, sl, -1.0, None, ALU.add))
            link(v.tensor_copy(rti[0:1, 0:1], R_["upto"][0:1, E - 1:E]))
            link(v.tensor_copy(rti[0:1, 1:1 + ITEMS], R_["expert"][0:1, :]))
            dve.nop().then_inc(items_ready, 1)
            for m in range(M):
                link(v.tensor_tensor(xn[:, m, :], xn[:, m, :], ye[:], ALU.mult))
            n = dve.value_load(rti[0:1, 0:1], min_val=1, max_val=ITEMS)
            with dve.Fori(0, n) as it:
                B, U = it * NBB + MOE_B, it * NBB + MOE_U
                for m in range(M):
                    v.tensor_scalar(pick[:, m, :], C("iota_slot"), slot_of[:, m, bass.ds(it, 1)], None, ALU.is_equal)
                    t = v.tensor_scalar(pickw[:, m, :], C("iota_slot"), slot_of[:, m, bass.ds(it, 1)],
                                        weight_of[:, m, bass.ds(it, 1)], ALU.is_equal, ALU.mult)
                t.then_inc(pick_ready, 1)
                v.memset(ye[:], 0.0).then_inc(ye_zeroed, 1)
                low(0, B, SLOT)
                low(1, B, SLOT)
                dve.wait_ge(xh_ready, it + 1)
                for j in range(2):
                    t = v.tensor_tensor(xl[:, 4 * j:4 * j + 4, 0:P], ps[:, 5 + j, :].rearrange("p (k t) -> p k t", k=4),
                                        xh[:, 4 * j:4 * j + 4, 0:P].bitcast(F32), ALU.subtract)
                t.then_inc(xl_ready, 1)
                dve.wait_ge(ye_zeroed, it + 1)
                low(0, B + 1, SLOT)
                hidden(U, FB)
                low(1, B + 1, SLOT)
                low(2, B, SLOT)
                with dve.Fori(1, NBB - 1) as b:
                    low_h(U + b - 1, FB)
                    low(0, B + b + 1, SLOT)
                    hidden(U + b, FB)
                    low(1, B + b + 1, SLOT)
                    add_down(U + b - 1, ye)
                    low(2, B + b, SLOT)
                low_h(U + (NBB - 2), FB)
                hidden(U + (NBB - 1), FB)
                add_down(U + (NBB - 2), ye)
                low(2, B + (NBB - 1), SLOT)
                low_h(U + (NBB - 1), FB)
                add_down(U + (NBB - 1), ye)
                dve.wait_ge(put_done, it + 1)
                for m in range(M):
                    for half in range(2):
                        xs = x[:, m, half * FB:(half + 1) * FB]
                        v.tensor_tensor(xs, xs, ps[:, 3 + 2 * m + half, :], ALU.add)
            me.barrier("final")
            norm()
            dve.wait_ge(final_in, 16)
            for m in range(M):
                dve.wait_ge(norm_xn, M * me.norms)
                v.tensor_tensor(xn[:, m, :], xn[:, m, :], uT[:, 0:4, :].rearrange("p a b -> p (a b)"), ALU.mult).then_inc(out_ready, 1)

        @block.sync
        def _(sp_eng):
            sy = sp_eng
            sy.dma_start(x[:], A["x"].rearrange("a (m p) d -> p (a m) d", p=P)).then_inc(x_in, 16)

            def kp(w):
                return w.rearrange("(k p) n -> p k n", p=P)

            held = [None, None, None]

            def fill(s, src, k, w, free=None):
                if free or held[s]:
                    sy.wait_ge(*(free or held[s]))
                sy.dma_start(raw[:, s, 0:k * w].rearrange("p (k n) -> p k n", k=k), src).then_inc(slot_full[s], 16)

            def ffn_tiles(name, win_g, win_u, wdn):
                nb, wlast = FFN[name][:2]
                B0 = FFN[name][2]

                def gu(b, w=FB, st=False, free=True):
                    cs = slice(b * FB, b * FB + w) if st else bass.ds(b * FB, FB)
                    fill(0, kp(win_g)[:, :, cs], KD, w, (wl_full[0], b + B0) if free else None)
                    fill(1, kp(win_u)[:, :, cs], KD, w, (wl_full[1], b + B0) if free else None)

                def dn(b, w=FB, st=False, free=True):
                    cs = slice(b * 4, b * 4 + w // P) if st else bass.ds(b * 4, 4)
                    fill(2, kp(wdn)[:, cs, :], w // P, D, (wl_full[2], b + B0) if free else None)

                gu(0, FB, True, free=False)
                dn(0, FB, True, free=False)
                gu(1, FB, True)
                with sy.Fori(1, nb - 2) as b:
                    dn(b)
                    gu(b + 1)
                dn(nb - 2, FB, True)
                gu(nb - 1, wlast, True)
                dn(nb - 1, wlast, True)
                for s in range(3):
                    held[s] = (wl_full[s], B0 + nb)

            for key in order:
                if len(key) == 1 and key[0] in FFN:
                    if key[0] == "ffn2":
                        ffn_tiles("ffn2", A["dense_w_gate_2"][0], A["dense_w_up_2"][0], A["dense_w_down_2"][0])
                    else:
                        i = int(key[0][3])
                        ffn_tiles(key[0], A["f_w_in"][i, :, 0:F_A], A["f_w_in"][i, :, F_A:2 * F_A], A["f_w_out"][i])
                    continue
                if key == ("moe",):
                    continue
                s, f = plan[key]
                kind = key[0]
                t = key[-1]
                if kind == "a_in":
                    fill(s, kp(A["a_w_in"][0])[:, :, t * 512:t * 512 + 512], KD, 512)
                elif kind == "a_gate":
                    fill(s, A["a_gate_w"][0].rearrange("g h i j -> i (g h) j"), 16, P)
                elif kind == "a_out":
                    fill(s, kp(A["a_w_out"][0])[:, :, t * 512:t * 512 + 512], KD, 512)
                elif kind == "kv":
                    fill(s, kp(A["kv_w"])[:, :, t * 512:t * 512 + 512], KD, 512)
                elif kind == "cmp":
                    fill(s, kp(A["cmp_w1"][t]), 16, CH)
                elif kind == "b_in":
                    w = 512 if t < 2 else 3 * NH
                    fill(s, kp(A["b_w_in"][0])[:, :, t * 512:t * 512 + w], KD, w)
                elif kind == "b_out":
                    fill(s, kp(A["b_w_out"][0])[:, :, t * 512:t * 512 + 512], KD, 512)
                elif kind == "mix_in":
                    fill(s, kp(A["w_in_2"][key[1]])[:, :, t * 512:t * 512 + 512], KD, 512)
                elif kind == "branch":
                    w = A["w_branch_hgrn_2"] if t == 0 else A["w_branch_sb_2"]
                    fill(s, kp(w[key[1]]), 4, D)
                elif kind == "mix_out":
                    fill(s, kp(A["w_out_2"][key[1]])[:, :, t * 512:t * 512 + 512], KD, 512)
                held[s] = freed[key]

            for s in range(3):
                sy.wait_ge(*held[s])
            sy.wait_ge(items_ready, 1)
            n = sy.value_load(rti[0:1, 0:1], min_val=1, max_val=ITEMS)
            wg = A["moe_w_gate_2"][0].rearrange("e (k p) n -> e p k n", p=P)
            wu = A["moe_w_up_2"][0].rearrange("e (k p) n -> e p k n", p=P)
            wd = A["moe_w_down_2"][0].rearrange("e (k p) n -> e p k n", p=P)
            with sy.Fori(0, n) as it:
                e = sy.value_load(rti[0:1, bass.ds(it + 1, 1)], min_val=0, max_val=E - 1)

                def one(s, w, b, cs):
                    src = w[bass.ds(e, 1), :, cs, :] if s == 2 else w[bass.ds(e, 1), :, :, cs]
                    sy.wait_ge(wl_full[s], it * NBB + b + MOE_B)
                    k, wdt = (4, D) if s == 2 else (KD, FB)
                    sy.dma_start(raw[:, s, :].rearrange("p (k n) -> p k n", k=k),
                                 src.rearrange("e p k n -> (e p) k n")).then_inc(slot_full[s], 16)

                one(0, wg, 0, slice(0, FB))
                one(1, wu, 0, slice(0, FB))
                with sy.Fori(0, NBB - 1) as b:
                    one(0, wg, b + 1, bass.ds(b * FB + FB, FB))
                    one(1, wu, b + 1, bass.ds(b * FB + FB, FB))
                    one(2, wd, b, bass.ds(b * 4, 4))
                one(2, wd, NBB - 1, slice((NBB - 1) * 4, NBB * 4))
            sy.wait_ge(out_ready, 2)
            sy.dma_start(out.rearrange("a (m p) d -> p (a m) d", p=P), xn[:]).then_inc(out_sent, 16)
            sy.wait_ge(out_sent, 16)

        @block.gpsimd
        def _(po):
            po.dma_start(const[:], A["const_f32"]).then_inc(const_in, 16)
            for g in range(2):
                at = 0
                for name, r in ROWS[g]:
                    a = A[name]
                    n = 1
                    for d in a.shape:
                        n *= d
                    assert n == r * P, name
                    names = " ".join("abcd"[:len(a.shape)])
                    flat = a if len(a.shape) == 1 else a.rearrange(f"{names} -> ({names})")
                    po.dma_start(rowbuf[at:at + r, g, :], flat.rearrange("(r q) -> r q", q=P)).then_inc(rows_in[g], 16)
                    at += r
            for name, (at, w) in BC.items():
                a = A[name]
                names = " ".join("abcd"[:len(a.shape)])
                flat = a if len(a.shape) == 1 else a.rearrange(f"{names} -> ({names})")
                po.dma_start(bc[:, at:at + w], flat.partition_broadcast(P)).then_inc(bc_in, 16)
            po.wait_ge(stage, 3 * marks["nsa"])
            po.dma_start(w2[:].rearrange("p k c d -> p (k c) d"),
                         A["cmp_w2"].rearrange("k (c p) d -> p (k c) d", p=P)).then_inc(w2_in, 16)
            po.wait_ge(v_read, marks["kvc_v"])
            po.wait_ge(a_read, marks["kvc_a"])
            po.dma_start(kv_scratch.rearrange("(m p) n -> p m n", p=P), kvn[:, :, 0:512]).then_inc(kvc_out, 16)
            po.wait_ge(kvc_out, 16)
            for kv in range(2):
                for g in range(NG):
                    r = (kv * NG + g) * NCMP
                    for half in range(2):
                        src = kv_scratch[half * CS:half * CS + NCMP * CS, kv * 256 + g * HD:kv * 256 + g * HD + HD]
                        po.dma_start(xc[r:r + NCMP, half * CS * HD:(half + 1) * CS * HD].rearrange(
                            "c (l d) -> c l d", d=HD), src.rearrange("(c l) d -> c l d", l=CS)).then_inc(kvc_in, 16)
            for layer in range(2):
                po.wait_ge(stage, 3 * marks[f"mix{layer}"])
                po.dma_start(t3[:].rearrange("p h t -> p (h t)"), A["const_masks"]).then_inc(masks_in, 16)
            po.wait_ge(stage, 3 * marks["moe"])
            po.dma_start(ye[:], A["ffn_norm_2"][1, :].partition_broadcast(P)).then_inc(ye_in, 16)
            po.dma_start(wr[:].rearrange("p (k e) -> p k e", e=E),
                         A["moe_router_2"][0].rearrange("(k p) e -> p k e", p=P)).then_inc(wr_in, 16)
            po.wait_ge(stage, 3 * marks["final"])
            po.dma_start(uT[:, 0:4, :].rearrange("p a b -> p (a b)"), A["final_norm_2"].partition_broadcast(P)).then_inc(final_in, 16)


_INS = ["x", "a_norm", "a_w_in", "a_conv_w", "a_conv_b", "a_gate_w", "a_gate_b", "a_lambda", "a_w_out", "kv_norm",
        "kv_w", "k_norm", "cmp_pos", "cmp_w1", "cmp_b1", "cmp_w2", "cmp_b2", "b_norm", "b_w_in", "b_gate_b", "q_norm",
        "b_w_out", "f_norm", "f_w_in", "f_w_out", "mix_norm_2", "w_in_2", "hgrn_lb_logits_2", "hgrn_out_norm_2",
        "w_branch_hgrn_2", "w_branch_sb_2", "w_out_2", "ffn_norm_2", "dense_w_gate_2", "dense_w_up_2",
        "dense_w_down_2", "moe_router_2", "moe_w_gate_2", "moe_w_up_2", "moe_w_down_2", "final_norm_2"]


def kernel(**inputs):
    import concourse.bacc as bacc
    from concourse.bass_utils import run_bass_kernel_spmd

    nc = bacc.Bacc("TRN2", target_bir_lowering=False, num_devices=1)
    arrays = {name: np.ascontiguousarray(inputs[name]) for name in _INS}
    arrays["const_f32"], arrays["const_masks"] = CONST_F32, CONST_MASKS
    aps = {name: nc.dram_tensor(f"in_{name}", a.shape, mybir.dt.from_np(a.dtype), kind="ExternalInput").ap()
           for name, a in arrays.items()}
    out = nc.dram_tensor("out", (1, S, D), F32, kind="ExternalOutput").ap()
    build(nc, aps, out)
    r = run_bass_kernel_spmd(nc, [{f"in_{name}": a for name, a in arrays.items()}], core_ids=[0])
    return r.results[0]["out"]
```

```python
from contextlib import ExitStack

import numpy as np
import concourse.bass as bass
from concourse import mybir

F32 = mybir.dt.float32
F32R = mybir.dt.float32r
I32 = mybir.dt.int32
U8 = mybir.dt.uint8
ACT = mybir.ActivationFunctionType
ALU = mybir.AluOpType
AX = mybir.AxisListType

P = 128
S = 256
M = S // P
D = 1024
KD = D // P
EPS = 1e-6
NEG = -1e30
SLOT = 4096

HD, NH, NG = 64, 16, 4
HPG = NH // NG
CB, CS, CH = 32, 16, 256
NCMP = (S - CB) // CS + 1
SCALE = HD ** -0.5
KALL = NCMP + 2 * S
LRU_C = 8.0
CONV = 4
F_A = 2816
F_B = 3584
FB = 512
HH, HC = 4, 64
SH = 8
LEVELS = [1, 2, 4, 8, 16, 32]
E = 8
ITEMS = 12
MIN_ITEMS = 2 * S // P
NBB = F_B // FB

IN_ORDER = [1, 0, 5, 4, 2, 6, 3, 7, 8, 9, 10]


CONSTS = {}


def _const_arrays():
    cols, at = [], 0

    def put(name, a):
        nonlocal at
        a = np.broadcast_to(np.asarray(a, np.float32), (P, np.asarray(a).shape[-1]))
        CONSTS[name] = (at, a.shape[1])
        cols.append(a)
        at += a.shape[1]

    i = np.arange(P)
    put("ident", np.eye(P))
    put("neg_causal", np.where(i[None, :] > i[:, None], NEG, 0.0))
    put("before", (i[:, None] < i[None, :]) * 1.0)
    put("neg_not_before", np.where(i[:, None] < i[None, :], 0.0, NEG))
    put("minus_from", np.where(i[:, None] >= i[None, :], -1.0, 0.0))
    put("minus_one", -np.ones((P, P)))
    put("one", np.ones((P, P)))
    put("iota_slot", i[None, :])
    half = HD // 2
    freqs = np.power(np.float32(10000.0), -np.arange(half, dtype=np.float32) / np.float32(half)).astype(np.float32)

    def rope(pos):
        ang = (pos.astype(np.float32)[:, None] * freqs[None, :]).astype(np.float32)
        c, s = np.cos(ang).astype(np.float32), np.sin(ang).astype(np.float32)
        return np.concatenate([c, c], 1), np.concatenate([s, s], 1)

    for m in range(M):
        c, s = rope(m * P + i)
        put(f"cos{m}", c)
        put(f"sin{m}", s)
    c, s = rope(np.minimum(i, NCMP - 1) * CS + CB - 1)
    put("cosc", c)
    put("sinc", s)
    last = np.arange(NCMP) * CS + CB - 1
    for m in range(M):
        t = (m * P + i)[:, None]
        put(f"neg_keys{m}", np.concatenate([np.where(last[None, :] <= t, 0.0, NEG),
                                            np.where(np.arange((m + 1) * P)[None, :] <= t, 0.0, NEG)], 1))
    put("row_valid", ((i >= CB - 1) * 1.0)[:, None])
    e = np.arange(E)
    put("lower_e", ((e[None, :] < e[:, None]) * 1.0).reshape(1, -1))
    put("iota_e", e[None, :])
    put("iota_i", np.arange(ITEMS)[None, :])
    base = np.concatenate(cols, 1)
    masks = [np.eye(P)]
    for lv in LEVELS + [64]:
        same = (i[:, None] // (2 * lv)) == (i[None, :] // (2 * lv))
        masks.append(same & (i[:, None] % (2 * lv) < lv) & (i[None, :] % (2 * lv) >= lv))
    masks = np.stack(masks, 1).astype(np.float32).reshape(P, -1)
    return np.ascontiguousarray(base), np.ascontiguousarray(masks)


CONST_F32, CONST_MASKS = _const_arrays()

ROWS = [
    [("a_norm", 8), ("a_conv_w", 32), ("a_conv_b", 8), ("a_gate_b", 16), ("a_lambda", 8),
     ("kv_norm", 8), ("b_norm", 8), ("f_norm", 16)],
    [("mix_norm_2", 16), ("ffn_norm_2", 16), ("hgrn_lb_logits_2", 8), ("cmp_b1", 4), ("cmp_pos", 32)],
]
COL = {}
for _g, _names in enumerate(ROWS):
    _at = _g * P
    for _n, _r in _names:
        COL[_n] = _at
        _at += _r
ROWS_USED = [sum(r for _, r in g) for g in ROWS]
BC = {"q_norm": (0, 64), "k_norm": (64, 192), "cmp_b2": (256, 128), "b_gate_b": (384, 48), "hgrn_out_norm_2": (432, 256)}
BC_W = 688


class Ring:

    def __init__(self, banks, filled, read):
        self.banks, self.filled, self.read, self.n = banks, filled, read, 0

    def claim(self, pe):
        if self.n >= len(self.banks):
            pe.wait_ge(self.read, self.n - len(self.banks) + 1)
        self.n += 1
        return self.banks[(self.n - 1) % len(self.banks)]

    def take(self, eng):
        self.n += 1
        eng.wait_ge(self.filled, self.n)
        return self.banks[(self.n - 1) % len(self.banks)]


def weight_plan():
    plan, fills = {}, [0, 0, 0]
    order, nxt = [], 0

    def tile(*key):
        nonlocal nxt
        s = nxt
        nxt = (nxt + 1) % 3
        plan[key] = (s, fills[s])
        fills[s] += 1
        order.append(key)

    def ffn(name, blocks):
        nonlocal nxt
        plan[name] = [((nxt + kind) % 3, fills[(nxt + kind) % 3]) for kind in range(3)]
        for s in range(3):
            fills[s] += blocks
        order.append((name,))

    for t in (2, 3):
        tile("a_in", t)
    tile("a_gate")
    for t in (0, 1):
        tile("a_in", t)
    for t in (0, 1):
        tile("a_out", t)
    ffn("ffn0", 6)
    for t in range(3):
        tile("kv", t)
    for t in range(3):
        tile("b_in", t)
    for t in range(2):
        tile("cmp", t)
    for t in range(2):
        tile("b_out", t)
    ffn("ffn1", 6)
    for layer in range(2):
        for t in IN_ORDER:
            tile("mix_in", layer, t)
        tile("branch", layer, 0)
        tile("branch", layer, 1)
        for t in range(2):
            tile("mix_out", layer, t)
        if layer == 0:
            ffn("ffn2", NBB)
        else:
            ffn("moe", 0)
    return plan, order


def build(nc, A, out, dbg=None):
    plan, order = weight_plan()
    ctx = ExitStack()
    with ctx:
        def sbuf(name, shape, dt=F32, stack=ctx):
            return stack.enter_context(nc.sbuf_tensor(name, shape, dt))

        def sem(name):
            return ctx.enter_context(nc.semaphore(name))

        x = sbuf("x", [P, M, D])
        xn = sbuf("xn", [P, M, D])
        uT = sbuf("uT", [P, KD, S])
        raw = sbuf("raw", [P, 3, SLOT])
        const = sbuf("const", [P, CONST_F32.shape[1]])
        cols = sbuf("cols", [P, 2 * P])
        bc = sbuf("bc", [P, BC_W])
        small = sbuf("small", [P, 64])

        def C(name, rows=P):
            a, w = CONSTS[name]
            return const[0:rows, a:a + w]

        def col(name, i=0, n=1):
            return cols[:, COL[name] + i:COL[name] + i + n]

        with ExitStack() as st:
            rowbuf = sbuf("rowbuf", [P, 2, P], stack=st)
            zp = sbuf("zp", [P, KD, S + CONV - 1], stack=st)
            xr = sbuf("xr", [P, KD, S], stack=st)
            rg = sbuf("rg", [P, KD, S], stack=st)
            ig = sbuf("ig", [P, KD, S], stack=st)
            aa = sbuf("aa", [P, KD, S], stack=st)
            th = sbuf("th", [P, KD, S], stack=st)
            yg = sbuf("yg", [P, KD, S], stack=st)
            lam = sbuf("lam", [P, 8, KD], stack=st)
        with ExitStack() as st:
            wh = sbuf("wh", [P, 3, SLOT], F32R, stack=st)
            wl = sbuf("wl", [P, 3, SLOT], F32R, stack=st)
            xh = sbuf("xh", [P, KD, S], F32R, stack=st)
            xl = sbuf("xl", [P, KD, S], F32R, stack=st)
            sg = sbuf("sg", [P, FB], stack=st)
            hb = sbuf("hb", [P, FB], stack=st)
            hh = sbuf("hh", [P, FB], F32R, stack=st)
            hl = sbuf("hl", [P, FB], F32R, stack=st)
            ye = sbuf("ye", [P, D], stack=st)
            rti = sbuf("rti", [1, 16], I32, stack=st)
            wr = sbuf("wr", [P, KD * E], stack=st)
        with ExitStack() as st:
            ubT = sbuf("ubT", [P, KD, S], stack=st)
            kvn = sbuf("kvn", [P, M, 6 * NG * HD], stack=st)
            qn = sbuf("qn", [P, M, D], stack=st)
            tmp_a = sbuf("tmp_a", [P, D], stack=st)
            tmp_b = sbuf("tmp_b", [P, D], stack=st)
            xc = sbuf("xc", [P, CB * HD], stack=st)
            xcT = sbuf("xcT", [P, 2, 16, NG * NCMP], stack=st)
            h1T = sbuf("h1T", [P, 4, 64], stack=st)
            w2 = sbuf("w2", [P, 2, 2, HD], stack=st)
            cmpn = sbuf("cmpn", [P, 2, NG, HD], stack=st)
            kdup = sbuf("kdup", [P, M, 2, NG, 2, HD], stack=st)
            kcdup = sbuf("kcdup", [P, NG, 2, HD], stack=st)
            rope_g = sbuf("rope_g", [P, 5, 2, HD], stack=st)
            rope_k = sbuf("rope_k", [P, M, 2, 2, HD], stack=st)
            kT = sbuf("kT", [P, NG, KALL], stack=st)
            qT = sbuf("qT", [P, NH, S], stack=st)
            oT = sbuf("oT", [P, NH // 2, S], stack=st)
            diag = sbuf("diag", [P, 2, 3, P], stack=st)
            gate = sbuf("gate", [P, M, 3, NH], stack=st)
            pr = sbuf("pr", [P, 2, 528], stack=st)
            pT = sbuf("pT", [P, 2, 512], stack=st)
            pcT = sbuf("pcT", [P, 2, P], stack=st)
            stat = sbuf("stat", [P, 3, 16], stack=st)
        with ExitStack() as st:
            zf = sbuf("zf", [P, HH, S], stack=st)
            qh = sbuf("qh", [P, HH, S], stack=st)
            t1 = sbuf("t1", [P, HH, S], stack=st)
            t2 = sbuf("t2", [P, HH, S], stack=st)
            t3 = sbuf("t3", [P, HH, S], stack=st)
            kk = sbuf("kk", [P, HH, S], stack=st)
            bb = sbuf("bb", [P, HH, S], stack=st)
            keep = sbuf("keep", [P, HH, S], stack=st)
            sd = sbuf("sd", [P, HH, M, P], stack=st)
            sx = sbuf("sx", [P, HH, P], stack=st)
            skT = sbuf("skT", [P, 4, S], stack=st)
            sqT = sbuf("sqT", [P, 4, S], stack=st)
            hv = sbuf("hv", [P, M, 512], stack=st)
            sv = sbuf("sv", [P, M, 512], stack=st)
            hog = sbuf("hog", [P, M, 512], stack=st)
            sga = sbuf("sga", [P, M, D], stack=st)
            sgb = sbuf("sgb", [P, M, D], stack=st)
            oa = sbuf("oa", [P, M, 512], stack=st)
            oaT = sbuf("oaT", [P, 4, S], stack=st)
            obT = sbuf("obT", [P, 4, S], stack=st)
            e1 = sbuf("e1", [P, 2, 384], stack=st)
            sp = sbuf("sp", [P, 2, 384], stack=st)
            wt = sbuf("wt", [P, 2, 384], stack=st)
            lbt = sbuf("lbt", [P, 8, HH], stack=st)
            lmask = sbuf("lmask", [P, 8 * P], U8, stack=st)

        rt = uT[:, 3:6, :].rearrange("p a b -> p (a b)")
        R_, at = {}, 0
        for name, w in [("exp", M * E), ("logit", M * E), ("neg_max", M), ("sum", M), ("a64", E * E), ("b64", E * E),
                        ("rank", E), ("weight", M * E), ("pos", 3 * E), ("tiles", E), ("upto", E), ("before", E), ("ones", E),
                        ("owner", ITEMS * E), ("tmp", ITEMS * E), ("expert", ITEMS), ("first", ITEMS), ("there", ITEMS),
                        ("slot_of", M * ITEMS), ("weight_of", M * ITEMS), ("sel", M * E)]:
            R_[name] = rt[:, at:at + w]
            at += w
        slot_of, weight_of = (R_[k].rearrange("p (m i) -> p m i", m=M) for k in ("slot_of", "weight_of"))
        sel = R_["sel"].rearrange("p (m e) -> p m e", m=M)
        pick, pickw = uT[:, 0:1, :].rearrange("p a (m t) -> p (a m) t", m=M), uT[:, 1:2, :].rearrange("p a (m t) -> p (a m) t", m=M)
        pickT = uT[:, 2, :]

        ps = ctx.enter_context(nc.psum_tensor("ps", [P, 8, 512], F32))
        kv_scratch = nc.dram_tensor("kv_scratch", [S, 512], F32, kind="Internal").ap()

        slot_full = [sem(f"slot_full{s}") for s in range(3)]
        const_in = sem("const_in")
        rows_in = [sem(f"rows_in{i}") for i in range(2)]
        bc_in = sem("bc_in")
        x_in = sem("x_in")
        w2_in, masks_in, wr_in, ye_in, final_in = sem("w2_in"), sem("masks_in"), sem("wr_in"), sem("ye_in"), sem("final_in")
        q_zeroed, o_filled, o_read = sem("q_zeroed"), sem("o_filled"), sem("o_read")
        kvc_out, kvc_in = sem("kvc_out"), sem("kvc_in")
        stage = sem("stage")
        dve_order, act_order = sem("dve_order"), sem("act_order")
        v_filled, v_read = sem("v_filled"), sem("v_read")
        a_filled, a_read = sem("a_filled"), sem("a_read")
        s_filled, s_read = sem("s_filled"), sem("s_read")
        norm_sq, norm_ms, norm_rt, norm_xn = sem("norm_sq"), sem("norm_ms"), sem("norm_rt"), sem("norm_xn")
        norm_h, root_done = sem("norm_h"), sem("root_done")
        xr_ready, ri_ready, la_ready, a_ready = sem("xr_ready"), sem("ri_ready"), sem("la_ready"), sem("a_ready")
        lam_abs, lam_exp = sem("lam_abs"), sem("lam_exp")
        th_ready, t2_ready, sq_ready, yg_ready, yh_ready = (
            sem("th_ready"), sem("t2_ready"), sem("sq_ready"), sem("yg_ready"), sem("yh_ready"))
        kvn_ready, qn_ready, gate_ready, gated = sem("kvn_ready"), sem("qn_ready"), sem("gate_ready"), sem("gated")
        ms_ready, root_ready = sem("ms_ready"), sem("root_ready")
        k_ready, q_ready, kc_ready = sem("k_ready"), sem("q_ready"), sem("kc_ready")
        max_ready, diag_ready = sem("max_ready"), sem("diag_ready")
        lb_max, lb_exp, lb_clamped, lb_ln = sem("lb_max"), sem("lb_exp"), sem("lb_clamped"), sem("lb_ln")
        zabs_ready, zln_ready, zdif_ready, kk_ready = sem("zabs_ready"), sem("zln_ready"), sem("zdif_ready"), sem("kk_ready")
        fabs_ready, fln_ready, qh_ready = sem("fabs_ready"), sem("fln_ready"), sem("qh_ready")
        decay_ready, decay_exp, level_ready = sem("decay_ready"), sem("decay_exp"), sem("level_ready")
        oms_ready, ort_ready, oa_ready = sem("oms_ready"), sem("ort_ready"), sem("oa_ready")
        ln_ready, sp_ready, y_ready = sem("ln_ready"), sem("sp_ready"), sem("y_ready")
        sel_ready, lmax_ready, lexp_ready = sem("sel_ready"), sem("lmax_ready"), sem("lexp_ready")
        wh_full = [sem(f"wh_full{s}") for s in range(3)]
        wl_full = [sem(f"wl_full{s}") for s in range(3)]
        g_done, u_done, t_done, d_done = sem("g_done"), sem("u_done"), sem("t_done"), sem("d_done")
        sg_ready, h_ready, hh_ready, hl_ready, d_added = (
            sem("sg_ready"), sem("h_ready"), sem("hh_ready"), sem("hl_ready"), sem("d_added"))
        pick_ready, picked, xh_ready, xl_ready = sem("pick_ready"), sem("picked"), sem("xh_ready"), sem("xl_ready")
        pickT_done, pickT_ready, put_done, put_added = sem("pickT_done"), sem("pickT_ready"), sem("put_done"), sem("put_added")
        items_ready = sem("items_ready")
        out_ready, out_sent = sem("out_ready"), sem("out_sent")

        block = ctx.enter_context(nc.Block())

        marks = {}
        freed = {}

        class Side:

            def __init__(self, eng):
                self.eng, self.n, self.counts, self.norms = eng, 0, {}, 0
                self.v = Ring([0, 1, 2], v_filled, v_read)
                self.a = Ring([3, 4, 5], a_filled, a_read)
                self.s = Ring([6, 7], s_filled, s_read)
                self.sc = Ring([6, 0], s_filled, s_read)
                self.o = Ring([2], o_filled, o_read)

            def scores_begin(self):
                self.sc.n, self.sc.base = self.s.n, self.s.n

            def scores_end(self):
                self.s.n = self.sc.n

            def barrier(self, name):
                self.n += 1
                marks[name] = self.n
                self.eng.drain().then_inc(stage, 1)
                self.eng.wait_ge(stage, 3 * self.n)

            def see(self, s, by=1):
                self.counts[s.name] = self.counts.get(s.name, 0) + by
                self.eng.wait_ge(s, self.counts[s.name])

            def link(self, ins, order):
                self.counts["order"] = self.counts.get("order", 0) + 1
                ins.then_inc(order, 1)
                self.eng.wait_ge(order, self.counts["order"])

        def tile_view(key, k, w):
            return raw[:, plan[key][0], 0:k * w].rearrange("p (k n) -> p k n", k=k)

        def arrived(eng, key):
            s, f = plan[key]
            eng.wait_ge(slot_full[s], 16 * (f + 1))

        FFN = {"ffn0": (6, 256, 0, 0), "ffn1": (6, 256, 6, 12), "ffn2": (NBB, FB, 12, 24)}
        MOE_B, MOE_U = 12 + NBB, 24 + 2 * NBB

        @block.tensor
        def _(pe):
            me = Side(pe)
            mm, tr = nc.tensor.matmul, nc.tensor.transpose
            pe.wait_ge(const_in, 16)
            ident = C("ident")

            for g in range(2):
                pe.wait_ge(rows_in[g], 16 * len(ROWS[g]))
                b = me.v.claim(pe)
                r = ROWS_USED[g]
                tr(ps[:, b, 0:r], rowbuf[0:r, g, :], const[0:r, 0:r]).then_inc(v_filled, 1)

            def drained(ring):
                pe.wait_ge(ring.read, ring.n)

            def norm(split=False):
                src = x if split else xn
                if not split:
                    me.see(norm_xn, M)
                for j in range(4):
                    ring = me.s if split else (me.v, me.a)[j % 2]
                    b = ring.claim(pe)
                    for kk in range(2):
                        for m in range(M):
                            t = tr(ps[:, b, (kk * M + m) * P:(kk * M + m + 1) * P],
                                   src[:, m, (2 * j + kk) * P:(2 * j + kk + 1) * P], ident)
                    t.then_inc(ring.filled, 1)
                for ring in ((me.s,) if split else (me.v, me.a)):
                    drained(ring)

            def released(key, ring):
                freed[key] = (ring.filled, ring.n)

            def product_T(ring, key, c, src):
                w = tile_view(key, KD, 512)
                b = ring.claim(pe)
                for k in range(KD):
                    t = mm(ps[:, b, 0:S], w[:, k, c * P:(c + 1) * P], src[:, k, :], start=(k == 0), stop=(k == KD - 1))
                t.then_inc(ring.filled, 1)

            def product(ring, key, m, src, w=512, kc=KD, c0=0):
                wv = tile_view(key, kc, max(w, D) if kc == 4 else w)
                b = ring.claim(pe)
                for k in range(kc):
                    t = mm(ps[:, b, 0:w], src[:, k, m * P:(m + 1) * P], wv[:, k, c0:c0 + w], start=(k == 0), stop=(k == kc - 1))
                t.then_inc(ring.filled, 1)

            me.barrier("start")
            norm()
            for t in (2, 3):
                arrived(pe, ("a_in", t))
                for c in range(4):
                    product_T(me.v, ("a_in", t), c, uT)
                released(("a_in", t), me.v)
            arrived(pe, ("a_gate",))
            gw = tile_view(("a_gate",), 16, P)
            for f in range(KD):
                me.see(xr_ready)
                b = me.a.claim(pe)
                for i in range(2):
                    t = mm(ps[:, b, i * S:(i + 1) * S], gw[:, i * KD + f, :], xr[:, f, :], start=True, stop=True)
                t.then_inc(a_filled, 1)
            released(("a_gate",), me.a)
            for t in (0, 1):
                arrived(pe, ("a_in", t))
                for c in range(4):
                    product_T(me.a, ("a_in", t), c, uT)
                released(("a_in", t), me.a)
            me.see(yh_ready)
            for t in range(2):
                arrived(pe, ("a_out", t))
                for m in range(M):
                    product(me.v, ("a_out", t), m, rg)
                released(("a_out", t), me.v)
            drained(me.v)

            def ffn_steps(ns):
                def wait(s, v):
                    if not (isinstance(v, int) and v <= 0):
                        pe.wait_ge(s, v)

                def split_product(bank, kind, xa, xb, k, B, w, last, c0=0, n=None):
                    a = wh[:, kind, k * w + c0:k * w + c0 + n]
                    l = wl[:, kind, k * w + c0:k * w + c0 + n]
                    mm(ps[:, bank, 0:n], xa, a, start=(k == 0), stop=False)
                    mm(ps[:, bank, 0:n], xa, l, start=False, stop=False)
                    return mm(ps[:, bank, 0:n], xb, a, start=False, stop=(k == last))

                def gate_up(kind, B, u, m, w):
                    pe.wait_ge(wh_full[kind], B + 1)
                    pe.wait_ge(wl_full[kind], B + 1)
                    wait(sg_ready if kind == 0 else h_ready, u)
                    for k in range(KD):
                        t = split_product(kind, kind, xh[:, k, m * P:(m + 1) * P], xl[:, k, m * P:(m + 1) * P],
                                          k, B, w, KD - 1, 0, w)
                    t.then_inc(g_done if kind == 0 else u_done, 1)

                def turn(u, w):
                    pe.wait_ge(h_ready, u + 1)
                    wait(hl_ready, u)
                    for c in range(w // P):
                        t = tr(ps[:, 2, c * P:(c + 1) * P], hb[:, c * P:(c + 1) * P], ident)
                    t.then_inc(t_done, 1)

                def down(B, u, w):
                    pe.wait_ge(wh_full[2], B + 1)
                    pe.wait_ge(wl_full[2], B + 1)
                    pe.wait_ge(hh_ready, u + 1)
                    pe.wait_ge(hl_ready, u + 1)
                    wait(d_added, u)
                    for half in range(2):
                        for c in range(w // P):
                            t = split_product(3 + half, 2, hh[:, c * P:(c + 1) * P], hl[:, c * P:(c + 1) * P],
                                              c, B, D, w // P - 1, half * FB, FB)
                    t.then_inc(d_done, 1)
                return gate_up, turn, down

            gate_up, turn, down = ffn_steps(None)

            def ffn(name):
                nb, wlast, B0, U0 = FFN[name]
                norm(split=True)

                def body(b, w, first=False):
                    for m in range(M):
                        u = b * M + (U0 + m)
                        gate_up(0, b + B0, u, m, w)
                        if not (first and m == 0):
                            turn(u - 1, w if m else FB)
                        gate_up(1, b + B0, u, m, w)
                        if not (first and m == 0):
                            down(b + (B0 if m else B0 - 1), u - 1, w if m else FB)

                body(0, FB, first=True)
                with pe.Fori(1, nb - 1) as b:
                    body(b, FB)
                body(nb - 1, wlast)
                u = U0 + nb * M - 1
                turn(u, wlast)
                down(B0 + nb - 1, u, wlast)
                pe.wait_ge(d_added, u + 1)

            me.barrier("ffn0")
            ffn("ffn0")

            me.barrier("nsa")
            norm()
            for t in range(3):
                arrived(pe, ("kv", t))
                product(me.v, ("kv", t), 0, uT)
                product(me.a, ("kv", t), 1, uT)
                released(("kv", t), me.a)
            for t in range(2):
                arrived(pe, ("b_in", t))
                product(me.v, ("b_in", t), 0, ubT)
                product(me.a, ("b_in", t), 1, ubT)
                released(("b_in", t), me.a)
            arrived(pe, ("b_in", 2))
            for m in range(M):
                product(me.v, ("b_in", 2), m, ubT, w=3 * NH)
            released(("b_in", 2), me.v)
            pe.wait_ge(kvc_in, 16 * 2 * 2 * NG)
            R = 2 * NG * NCMP
            for j in range(4):
                b = me.v.claim(pe)
                for i in range(4):
                    t = tr(ps[:, b, i * R:(i + 1) * R], xc[0:R, (4 * j + i) * P:(4 * j + i + 1) * P], const[0:R, 0:R])
                t.then_inc(v_filled, 1)
            drained(me.v)
            b = me.a.claim(pe)
            for kv in range(2):
                arrived(pe, ("cmp", kv))
                w1 = tile_view(("cmp", kv), 16, CH)
                for hc in range(2):
                    for l in range(16):
                        t = mm(ps[:, b, (kv * 2 + hc) * 64:(kv * 2 + hc) * 64 + NG * NCMP], w1[:, l, hc * P:(hc + 1) * P],
                               xcT[:, kv, l, :], start=(l == 0), stop=(l == 15))
            t.then_inc(a_filled, 1)
            released(("cmp", 0), me.a)
            released(("cmp", 1), me.a)
            hidden_at = me.a.n
            me.see(k_ready)
            for m in range(M):
                for w in range(2):
                    b = me.a.claim(pe)
                    for g in range(NG):
                        t = tr(ps[:, b, g * P:(g + 1) * P], kdup[:, m, w, g, :, :].rearrange("p a d -> p (a d)"), ident)
                    t.then_inc(a_filled, 1)
            pe.wait_ge(a_read, hidden_at)
            pe.wait_ge(w2_in, 16)
            b = me.v.claim(pe)
            for kv in range(2):
                for g in range(NG):
                    for hc in range(2):
                        t = mm(ps[0:NCMP, b, (kv * NG + g) * HD:(kv * NG + g + 1) * HD],
                               h1T[:, kv * 2 + hc, g * NCMP:(g + 1) * NCMP], w2[:, kv, hc, :], start=(hc == 0), stop=(hc == 1))
            t.then_inc(v_filled, 1)
            for m in range(M):
                me.see(q_ready)
                for j in range(2):
                    b = me.a.claim(pe)
                    for i in range(4):
                        t = tr(ps[:, b, i * P:(i + 1) * P], qn[:, m, (4 * j + i) * P:(4 * j + i + 1) * P], ident)
                    t.then_inc(a_filled, 1)
            me.see(kc_ready)
            b = me.v.claim(pe)
            for g in range(NG):
                t = tr(ps[:, b, g * 16:g * 16 + NCMP], kcdup[0:NCMP, g, :, :].rearrange("p a d -> p (a d)"),
                       const[0:NCMP, 0:NCMP])
            t.then_inc(v_filled, 1)
            drained(me.v)
            drained(me.a)

            def scores(m, h):
                g, nk = h // HPG, P * (m + 1)
                q = qT[:, h, m * P:(m + 1) * P]
                b = me.sc.claim(pe)
                mm(ps[:, b, 0:NCMP + nk], q, kT[:, g, 0:NCMP + nk], start=True, stop=False)
                mm(ps[:, b, 0:NCMP + nk], ident, C(f"neg_keys{m}"), start=False, stop=True)
                mm(ps[:, b + 1, 0:nk], q, kT[:, g, NCMP + S:NCMP + S + nk], start=True, stop=False)
                mm(ps[:, b + 1, m * P:nk], ident, C("neg_causal"), start=False, stop=True).then_inc(s_filled, 1)

            turned_at = {}

            def turn_probs(i, m, h):
                nb = m + 1
                me.see(diag_ready)
                b = me.a.claim(pe)
                for w in range(2):
                    for kb in range(nb):
                        c0 = NCMP + w * S + kb * P
                        t = mm(ps[:, b, (w * nb + kb) * P:(w * nb + kb + 1) * P], pr[:, i % 2, c0:c0 + P],
                               diag[:, i % 2, 1 + w, :], start=True, stop=True)
                t.then_inc(a_filled, 1)
                b = me.a.claim(pe)
                mm(ps[0:NCMP, b, 0:P], pr[:, i % 2, 0:NCMP], diag[:, i % 2, 0, :], start=True, stop=True).then_inc(a_filled, 1)
                turned_at[i] = me.a.n

            def values(i, m, h):
                g, nb, p0 = h // HPG, m + 1, HD * (h % 2)
                pe.wait_ge(a_read, turned_at[i])
                b = me.o.claim(pe) if h % 2 == 0 else me.o.banks[0]
                o = ps[p0:p0 + HD, b, 0:P]
                for w in range(2):
                    for kb in range(nb):
                        mm(o, kvn[:, kb, (2 * w + 3) * 256 + g * HD:(2 * w + 3) * 256 + (g + 1) * HD],
                           pT[:, i % 2, (w * nb + kb) * P:(w * nb + kb + 1) * P], start=(w == 0 and kb == 0), stop=False)
                t = mm(o, cmpn[0:NCMP, 1, g, :], pcT[0:NCMP, i % 2, :], start=False, stop=True)
                if h % 2:
                    t.then_inc(o_filled, 1)

            me.scores_begin()
            pe.wait_ge(q_zeroed, 1)
            pairs = [(m, h) for m in range(M) for h in range(NH)]
            scores(*pairs[0])
            for i, pair in enumerate(pairs):
                if i + 1 < len(pairs):
                    scores(*pairs[i + 1])
                turn_probs(i, *pair)
                if i:
                    values(i - 1, *pairs[i - 1])
            values(i, *pair)
            drained(me.o)
            me.scores_end()
            for t in range(2):
                arrived(pe, ("b_out", t))
                for m in range(M):
                    product(me.v, ("b_out", t), m, oT)
                released(("b_out", t), me.v)
            drained(me.v)

            me.barrier("ffn1")
            ffn("ffn1")

            def level_product(lv):
                me.see(level_ready)
                if lv == 128:
                    b = me.v.claim(pe)
                    for h in range(HH):
                        t = mm(ps[:, b, h * P:(h + 1) * P], t2[:, h, 0:P], t2[:, h, P:S], start=True, stop=True)
                    t.then_inc(v_filled, 1)
                    return
                ks, qs = (kk, qh) if lv == 0 else (t2, t2)
                for hp in range(2):
                    b = me.v.claim(pe)
                    for a in range(2):
                        for m in range(M):
                            t = mm(ps[:, b, (a * M + m) * P:(a * M + m + 1) * P], ks[:, 2 * hp + a, m * P:(m + 1) * P],
                                   qs[:, 2 * hp + a, m * P:(m + 1) * P], start=True, stop=True)
                    t.then_inc(v_filled, 1)

            def sb_z(b, h, stop=True):
                p0, hp = HD * (h % 2), h // 2
                mm(ps[:, b, 0:S], skT[p0:p0 + HD, hp, 0:P], sqT[p0:p0 + HD, hp, :], start=True, stop=stop)

            def sb_z1(b, h, stop=True):
                p0, hp = HD * (h % 2), h // 2
                return mm(ps[:, b, S:S + P], skT[p0:p0 + HD, hp, P:S], sqT[p0:p0 + HD, hp, P:S], start=True, stop=stop)

            def mixer(layer):
                norm()
                tiles = {t: ("mix_in", layer, t) for t in range(11)}
                for t, ring in ((1, me.v), (0, me.a), (5, me.v), (4, me.a)):
                    arrived(pe, tiles[t])
                    for c in range(4):
                        product_T(ring, tiles[t], c, uT)
                    released(tiles[t], ring)
                rest = [2, 6, 3, 7, 8, 9, 10]
                for j, lv in enumerate([0] + LEVELS + [64, 128]):
                    if j < len(rest):
                        arrived(pe, tiles[rest[j]])
                        for m in range(M):
                            product(me.a, tiles[rest[j]], m, uT)
                        released(tiles[rest[j]], me.a)
                    level_product(lv)
                drained(me.v)
                drained(me.a)
                for m in range(M):
                    b = me.v.claim(pe)
                    for h in range(HH):
                        o = ps[:, b, h * P:(h + 1) * P]
                        t = mm(o, sd[:, h, m, :], hv[:, m, h * P:(h + 1) * P], start=True, stop=(m == 0))
                        if m:
                            t = mm(o, sx[:, h, :], hv[:, 0, h * P:(h + 1) * P], start=False, stop=True)
                    t.then_inc(v_filled, 1)
                def sb_scores(h):
                    b = me.s.claim(pe)
                    sb_z(b, h)
                    sb_z1(b, h).then_inc(s_filled, 1)

                sb_scores(0)
                for h in range(SH):
                    if h + 1 < SH:
                        sb_scores(h + 1)
                    me.see(sp_ready)
                    spb = sp[:, h % 2, :]
                    b = me.a.claim(pe)
                    sb_z(b, h, stop=False)
                    mm(ps[:, b, 0:S], C("minus_from"), spb[:, 0:S], start=False, stop=False)
                    mm(ps[:, b, P:S], C("minus_one"), spb[:, S:S + P], start=False, stop=False)
                    mm(ps[:, b, 0:P], ident, C("neg_not_before"), start=False, stop=True)
                    sb_z1(b, h, stop=False)
                    mm(ps[:, b, S:S + P], C("minus_from"), spb[:, S:S + P], start=False, stop=False)
                    mm(ps[:, b, S:S + P], ident, C("neg_not_before"), start=False, stop=True).then_inc(a_filled, 1)
                    drained(me.a)
                    if h % 2 == 0:
                        bo = me.v.claim(pe)
                    p0 = HD * (h % 2)
                    mm(ps[p0:p0 + HD, bo, 0:S], sv[:, 0, h * HD:(h + 1) * HD], wt[:, h % 2, 0:S], start=True, stop=False)
                    t = mm(ps[p0:p0 + HD, bo, P:S], sv[:, 1, h * HD:(h + 1) * HD], wt[:, h % 2, S:S + P], start=False, stop=True)
                    if h % 2:
                        t.then_inc(v_filled, 1)
                me.see(oa_ready)
                for m in range(M):
                    b = me.a.claim(pe)
                    for k in range(4):
                        t = tr(ps[:, b, k * P:(k + 1) * P], oa[:, m, k * P:(k + 1) * P], ident)
                    t.then_inc(a_filled, 1)
                drained(me.a)
                drained(me.v)
                arrived(pe, ("branch", layer, 0))
                arrived(pe, ("branch", layer, 1))
                for m in range(M):
                    for half in range(2):
                        product(me.v, ("branch", layer, 0), m, oaT, w=512, kc=4, c0=half * 512)
                        if m == 1 and half == 1:
                            released(("branch", layer, 0), me.v)
                        product(me.v, ("branch", layer, 1), m, obT, w=512, kc=4, c0=half * 512)
                released(("branch", layer, 1), me.v)
                me.see(y_ready)
                for j in range(4):
                    b = me.a.claim(pe)
                    for kk_ in range(2):
                        for m in range(M):
                            k = 2 * j + kk_
                            t = tr(ps[:, b, (kk_ * M + m) * P:(kk_ * M + m + 1) * P], sga[:, m, k * P:(k + 1) * P], ident)
                    t.then_inc(a_filled, 1)
                drained(me.a)
                for t in range(2):
                    arrived(pe, ("mix_out", layer, t))
                    for m in range(M):
                        product(me.v, ("mix_out", layer, t), m, uT)
                    released(("mix_out", layer, t), me.v)
                drained(me.v)

            me.barrier("mix0")
            mixer(0)
            me.barrier("ffn2")
            ffn("ffn2")
            me.barrier("mix1")
            mixer(1)

            me.barrier("moe")
            norm()
            pe.wait_ge(wr_in, 16)
            b = me.v.claim(pe)
            for m in range(M):
                for k in range(KD):
                    t = mm(ps[:, b, m * E:(m + 1) * E], uT[:, k, m * P:(m + 1) * P], wr[:, k * E:(k + 1) * E],
                           start=(k == 0), stop=(k == KD - 1))
            t.then_inc(v_filled, 1)
            me.see(sel_ready)
            b = me.v.claim(pe)
            mm(ps[:, b, 0:E], C("before"), sel[:, 0, :], start=True, stop=True)
            mm(ps[:, b, E:2 * E], C("before"), sel[:, 1, :], start=True, stop=False)
            mm(ps[:, b, E:2 * E], C("one"), sel[:, 0, :], start=False, stop=True)
            mm(ps[:, b, 2 * E:3 * E], C("one"), sel[:, 0, :], start=True, stop=False)
            mm(ps[:, b, 2 * E:3 * E], C("one"), sel[:, 1, :], start=False, stop=True).then_inc(v_filled, 1)
            pe.wait_ge(items_ready, 1)
            n = pe.value_load(rti[0:1, 0:1], min_val=MIN_ITEMS, max_val=ITEMS)

            def gather():
                for k in range(KD):
                    o = ps[:, 5 + k // 4, (k % 4) * P:(k % 4 + 1) * P]
                    mm(o, xn[:, 0, k * P:(k + 1) * P], pick[:, 0, :], start=True, stop=False)
                    t = mm(o, xn[:, 1, k * P:(k + 1) * P], pick[:, 1, :], start=False, stop=True)
                t.then_inc(picked, 1)

            def turn_weighted():
                for m in range(M):
                    t = tr(ps[:, 7, m * P:(m + 1) * P], pickw[:, m, :], ident)
                t.then_inc(pickT_done, 1)

            def give_back(it, u):
                pe.wait_ge(pickT_ready, it + 1)
                pe.wait_ge(d_added, u + 1)
                for m in range(M):
                    for half in range(2):
                        t = mm(ps[:, 3 + 2 * m + half, :], pickT[:, m * P:(m + 1) * P], ye[:, half * FB:(half + 1) * FB],
                               start=True, stop=True)
                t.then_inc(put_done, 1)

            def step(B, u, mid=None, before_down=None):
                gate_up(0, B, u, 0, FB)
                turn(u - 1, FB)
                if mid:
                    mid()
                gate_up(1, B, u, 0, FB)
                if before_down:
                    before_down()
                down(B - 1, u - 1, FB)

            def item(it, last=False):
                B, U = it * NBB + MOE_B, it * NBB + MOE_U
                step(B + 1, U + 1, before_down=lambda: pe.wait_ge(put_added, it + 1))
                with pe.Fori(2, NBB - 1) as b:
                    step(B + b, U + b)

                def pass_on():
                    pe.wait_ge(pick_ready, it + 2)
                    turn_weighted()
                    if not last:
                        gather()

                step(B + (NBB - 1), U + (NBB - 1), mid=pass_on)
                if last:
                    turn(U + (NBB - 1), FB)
                    down(B + (NBB - 1), U + (NBB - 1), FB)
                else:
                    pe.wait_ge(xh_ready, it + 2)
                    pe.wait_ge(xl_ready, it + 2)
                    step(B + NBB, U + NBB)
                give_back(it, U + (NBB - 1))

            pe.wait_ge(pick_ready, 1)
            gather()
            pe.wait_ge(xh_ready, 1)
            pe.wait_ge(xl_ready, 1)
            gate_up(0, MOE_B, MOE_U, 0, FB)
            gate_up(1, MOE_B, MOE_U, 0, FB)
            with pe.Fori(0, n - 1) as it:
                item(it)
            item(n - 1, last=True)
            me.barrier("final")

        @block.scalar
        def _(act):
            me = Side(act)
            fn = nc.scalar.activation
            link = lambda ins: me.link(ins, act_order)
            act.wait_ge(x_in, 16)

            def norm(g=None):
                for m in range(M):
                    fn(xn[:, m, :], x[:, m, :], ACT.Square, accum_out=small[:, m:m + 1]).then_inc(norm_sq, 1)
                me.see(norm_ms)
                fn(small[:, 4:6], small[:, 2:4], ACT.Sqrt).then_inc(norm_rt, 1)
                if g is None:
                    return
                for j in (1, 3):
                    b = me.a.take(act)
                    for kk_ in range(2):
                        k = 2 * j + kk_
                        for dst, name, off in g:
                            t = fn(dst[:, k, :], ps[:, b, kk_ * S:(kk_ + 1) * S], ACT.Copy, scale=col(name, off + k))
                    t.then_inc(a_read, 1)

            me.barrier("start")
            norm([(uT, "a_norm", 0)])
            me.see(lam_abs)
            fn(lam[:, 1, :], lam[:, 0, :], ACT.Exp, scale=-1.0).then_inc(lam_exp, 1)
            for f in range(KD):
                b = me.a.take(act)
                fn(rg[:, f, :], ps[:, b, 0:S], ACT.Sigmoid, bias=col("a_gate_b", f))
                link(fn(ig[:, f, :], ps[:, b, S:2 * S], ACT.Sigmoid, bias=col("a_gate_b", KD + f)))
                act.nop().then_inc(a_read, 1)
            act.nop().then_inc(ri_ready, 1)
            me.see(la_ready)
            fn(aa[:], rg[:], ACT.Exp).then_inc(a_ready, 1)
            fn(th[:], rg[:], ACT.Tanh).then_inc(th_ready, 1)
            me.see(t2_ready)
            fn(th[:], th[:], ACT.Sqrt, scale=-1.0).then_inc(sq_ready, 1)
            for f in range(KD):
                b = me.a.take(act)
                fn(yg[:, f, :], ps[:, b, 0:S], ACT.Gelu_apprx_tanh).then_inc(a_read, 1)
            act.wait_ge(a_read, me.a.n)
            act.nop().then_inc(yg_ready, 1)

            def wait(s, v):
                if not (isinstance(v, int) and v <= 0):
                    act.wait_ge(s, v)

            users = [g_done, u_done, d_done]

            def high(name, kind, b, U, n):
                s, f = plan[name][kind]
                act.wait_ge(slot_full[s], (b + (f + 1)) * 16)
                wait(users[kind], U)
                fn(wh[:, kind, 0:n], raw[:, s, 0:n], ACT.Copy).then_inc(wh_full[kind], 1)

            def silu(u, w, root=1.0):
                act.wait_ge(g_done, u + 1)
                wait(h_ready, u)
                fn(sg[:, 0:w], ps[:, 0, 0:w], ACT.Silu, scale=root).then_inc(sg_ready, 1)

            def high_h(u, w):
                act.wait_ge(t_done, u + 1)
                wait(d_done, u)
                fn(hh[:, 0:w], ps[:, 2, 0:w], ACT.Copy).then_inc(hh_ready, 1)

            def ffn(name, g, off):
                nb, wlast, B0, U0 = FFN[name]
                for j in range(4):
                    b = me.s.take(act)
                    for kk_ in range(2):
                        k = 2 * j + kk_
                        t = fn(xh[:, k, :], ps[:, b, kk_ * S:(kk_ + 1) * S], ACT.Copy, scale=col(g, off + k))
                    t.then_inc(norm_h, 1)
                high(name, 0, 0, U0, SLOT)
                high(name, 1, 0, U0, SLOT)
                for m in range(M):
                    fn(xn[:, m, :], x[:, m, :], ACT.Square, accum_out=small[:, m:m + 1]).then_inc(norm_sq, 1)
                me.see(norm_ms)
                fn(small[:, 4:6], small[:, 2:4], ACT.Sqrt).then_inc(norm_rt, 1)
                me.see(root_done)

                def body(b, w, first=False, last=False, wn=FB):
                    u = b * M + U0
                    silu(u, w, small[:, 6:7])
                    if not first:
                        high_h(u - 1, FB)
                    high(name, 2, b, u, w // P * D)
                    silu(u + 1, w, small[:, 7:8])
                    high_h(u, w)
                    if not last:
                        high(name, 0, b + 1, u + 2, KD * wn)
                        high(name, 1, b + 1, u + 2, KD * wn)

                body(0, FB, first=True)
                with act.Fori(1, nb - 2) as b:
                    body(b, FB)
                body(nb - 2, FB, wn=wlast)
                body(nb - 1, wlast, last=True)
                high_h(U0 + nb * M - 1, wlast)

            me.barrier("ffn0")
            ffn("ffn0", "f_norm", 0)

            me.barrier("nsa")
            norm([(uT, "kv_norm", 0), (ubT, "b_norm", 0)])
            for t in range(3):
                b = me.a.take(act)
                fn(kvn[:, 1, t * 512:(t + 1) * 512], ps[:, b, :], ACT.Copy).then_inc(a_read, 1)
                if t == 0:
                    marks["kvc_a"] = me.a.n
                if t == 2:
                    act.wait_ge(a_read, me.a.n)
                    act.nop().then_inc(kvn_ready, 1)
            def root(n, rows=P):
                me.see(ms_ready)
                fn(stat[0:rows, 1, 0:n], stat[0:rows, 0, 0:n], ACT.Sqrt).then_inc(root_ready, 1)
            for _ in range(2 * M):
                root(NG)
            for t in range(2):
                b = me.a.take(act)
                fn(qn[:, 1, t * 512:(t + 1) * 512], ps[:, b, :], ACT.Copy).then_inc(a_read, 1)
            act.wait_ge(a_read, me.a.n)
            act.nop().then_inc(qn_ready, 1)
            for m in range(M):
                root(NH)
            me.see(gate_ready)
            fn(gate[:], gate[:], ACT.Sigmoid).then_inc(gated, 1)
            b = me.a.take(act)
            for j in range(4):
                t = fn(h1T[:, j, 0:NG * NCMP], ps[:, b, j * 64:j * 64 + NG * NCMP], ACT.Gelu_apprx_tanh, bias=col("cmp_b1", j))
            t.then_inc(a_read, 1)
            act.wait_ge(q_zeroed, 1)
            for m in range(M):
                for w in range(2):
                    b = me.a.take(act)
                    c0 = NCMP + w * S + m * P
                    fn(kT[:, :, c0:c0 + P], ps[:, b, :].rearrange("p (g t) -> p g t", g=NG), ACT.Copy).then_inc(a_read, 1)
            for m in range(M):
                for j in range(2):
                    b = me.a.take(act)
                    for p0 in (0, HD):
                        heads = qT[p0:p0 + HD, 8 * j:8 * j + 8, m * P:(m + 1) * P].rearrange("p (c a) t -> p c a t", a=2)
                        t = fn(heads[:, :, p0 // HD, :], ps[p0:p0 + HD, b, :].rearrange("p (c t) -> p c t", c=4), ACT.Copy)
                    t.then_inc(a_read, 1)
            root(NG, NCMP)

            def probs(i, m, h):
                nk, st_ = P * (m + 1), stat[:, i % 3, :]
                b = me.sc.take(act)
                me.see(max_ready)
                for j, (bank, c0, n, d0) in enumerate([(b, 0, NCMP, 0), (b, NCMP, nk, NCMP), (b + 1, 0, nk, NCMP + S)]):
                    t = fn(pr[:, i % 2, d0:d0 + n], ps[:, bank, c0:c0 + n], ACT.Exp, bias=st_[:, 3 + j:4 + j], scale=SCALE,
                           accum_out=st_[:, 6 + j:7 + j])
                t.then_inc(s_read, 1)

            def turned(i, m):
                b = me.a.take(act)
                n = 2 * (m + 1) * P
                fn(pT[:, i % 2, 0:n], ps[:, b, 0:n], ACT.Copy).then_inc(a_read, 1)
                b = me.a.take(act)
                fn(pcT[0:NCMP, i % 2, :], ps[0:NCMP, b, 0:P], ACT.Copy).then_inc(a_read, 1)

            pairs = [(m, h) for m in range(M) for h in range(NH)]
            me.scores_begin()
            probs(0, *pairs[0])
            for i, (m, h) in enumerate(pairs):
                if i + 1 < len(pairs):
                    probs(i + 1, *pairs[i + 1])
                turned(i, m)
            me.scores_end()

            me.barrier("ffn1")
            ffn("ffn1", "f_norm", KD)

            def mixer(layer):
                norm([(uT, "mix_norm_2", layer * KD)])
                me.see(lb_max)
                fn(lbt[:, 1:3, :], lbt[:, 1:3, :], ACT.Exp).then_inc(lb_exp, 1)
                me.see(lb_clamped)
                fn(lbt[:, 5:7, :], lbt[:, 5:7, :], ACT.Ln).then_inc(lb_ln, 1)
                for c in range(4):
                    b = me.a.take(act)
                    fn(qh[:, c, :], ps[:, b, 0:S], ACT.Silu).then_inc(a_read, 1)
                act.wait_ge(a_read, me.a.n)
                act.nop().then_inc(qh_ready, 1)
                me.see(zabs_ready)
                link(fn(t1[:], t1[:], ACT.Exp))
                fn(t2[:], t1[:], ACT.Ln, bias=1.0).then_inc(zln_ready, 1)
                me.see(zdif_ready)
                fn(kk[:], t1[:], ACT.Exp).then_inc(kk_ready, 1)
                me.see(fabs_ready)
                link(fn(t2[:], t2[:], ACT.Exp))
                fn(t2[:], t2[:], ACT.Ln, bias=1.0).then_inc(fln_ready, 1)
                for c in range(4):
                    b = me.a.take(act)
                    fn(sqT[:, c, :], ps[:, b, 0:S], ACT.Copy, scale=HD ** -0.5).then_inc(a_read, 1)
                dests = [(hv, 0, ACT.Copy), (sv, 0, ACT.Copy), (hog, 0, ACT.Silu), (sga, 0, ACT.Sigmoid),
                         (sga, 512, ACT.Sigmoid), (sgb, 0, ACT.Sigmoid), (sgb, 512, ACT.Sigmoid)]
                for j, lv in enumerate([0] + LEVELS + [64, 128]):
                    if j < len(dests):
                        dst, c0, f = dests[j]
                        for m in range(M):
                            b = me.a.take(act)
                            fn(dst[:, m, c0:c0 + 512], ps[:, b, :], f).then_inc(a_read, 1)
                    if lv:
                        me.see(decay_ready)
                        fn(t1[:], t1[:], ACT.Exp).then_inc(decay_exp, 1)
                me.see(oms_ready)
                fn(small[:, 24:32], small[:, 16:24], ACT.Sqrt).then_inc(ort_ready, 1)

                def soft(h):
                    b = me.s.take(act)
                    link(fn(e1[:, h % 2, :], ps[:, b, 0:384], ACT.Abs))
                    link(fn(e1[:, h % 2, :], e1[:, h % 2, :], ACT.Exp, scale=-1.0))
                    fn(e1[:, h % 2, :], e1[:, h % 2, :], ACT.Ln, bias=1.0).then_inc(ln_ready, 1)

                soft(0)
                for h in range(SH):
                    if h + 1 < SH:
                        soft(h + 1)
                    b = me.a.take(act)
                    fn(wt[:, h % 2, :], ps[:, b, 0:384], ACT.Exp).then_inc(a_read, 1)
                for m in range(M):
                    b = me.a.take(act)
                    fn(oaT[:, :, m * P:(m + 1) * P], ps[:, b, :].rearrange("p (k t) -> p k t", k=4), ACT.Copy).then_inc(a_read, 1)
                for j in range(4):
                    b = me.a.take(act)
                    fn(uT[:, 2 * j:2 * j + 2, :].rearrange("p k t -> p (k t)"), ps[:, b, :], ACT.Copy).then_inc(a_read, 1)

            me.barrier("mix0")
            mixer(0)
            me.barrier("ffn2")
            ffn("ffn2", "ffn_norm_2", 0)
            me.barrier("mix1")
            mixer(1)

            me.barrier("moe")
            norm([(uT, "ffn_norm_2", KD)])
            me.see(lmax_ready)
            for m in range(M):
                t = fn(R_["exp"][:, m * E:(m + 1) * E], R_["logit"][:, m * E:(m + 1) * E], ACT.Exp, bias=R_["neg_max"][:, m:m + 1])
            t.then_inc(lexp_ready, 1)
            act.wait_ge(items_ready, 1)
            n = act.value_load(rti[0:1, 0:1], min_val=MIN_ITEMS, max_val=ITEMS)

            def take_tokens(count, u):
                act.wait_ge(picked, count)
                act.wait_ge(u_done, u)
                for j in range(2):
                    t = fn(xh[:, 4 * j:4 * j + 4, 0:P], ps[:, 5 + j, :].rearrange("p (k t) -> p k t", k=4), ACT.Copy)
                t.then_inc(xh_ready, 1)

            def item(it, last=False):
                U = it * NBB + MOE_U

                def step(b):
                    u = U + b
                    silu(u, FB)
                    high_h(u - 1, FB)
                    high("moe", 0, it * NBB + b + 1, u + 1, SLOT)
                    high("moe", 1, it * NBB + b + 1, u + 1, SLOT)
                    high("moe", 2, it * NBB + b, u, SLOT)

                with act.Fori(1, NBB - 1) as b:
                    step(b)
                u = U + (NBB - 1)
                silu(u, FB)
                high_h(u - 1, FB)
                if not last:
                    high("moe", 0, it * NBB + NBB, u + 1, SLOT)
                    take_tokens(it + 2, u + 1)
                    high("moe", 1, it * NBB + NBB, u + 1, SLOT)
                high("moe", 2, it * NBB + (NBB - 1), u, SLOT)
                act.wait_ge(pickT_done, it + 1)
                fn(pickT, ps[:, 7, 0:S], ACT.Copy).then_inc(pickT_ready, 1)
                if last:
                    high_h(u, FB)
                else:
                    step(NBB)

            high("moe", 0, 0, MOE_U, SLOT)
            take_tokens(1, MOE_U)
            high("moe", 1, 0, MOE_U, SLOT)
            silu(MOE_U, FB)
            high("moe", 0, 1, MOE_U + 1, SLOT)
            high("moe", 1, 1, MOE_U + 1, SLOT)
            high("moe", 2, 0, MOE_U, SLOT)
            with act.Fori(0, n - 1) as it:
                item(it)
            item(n - 1, last=True)
            me.barrier("final")
            norm()

        @block.vector
        def _(dve):
            me = Side(dve)
            v = nc.vector
            link = lambda ins: me.link(ins, dve_order)

            def norm(g=None):
                me.norms += 1
                me.see(norm_sq, M)
                v.tensor_scalar(small[:, 2:4], small[:, 0:2], 1.0 / D, EPS, ALU.mult, ALU.add).then_inc(norm_ms, 1)
                me.see(norm_rt)
                link(v.reciprocal(small[:, 6:8], small[:, 4:6]))
                for m in range(M):
                    v.tensor_scalar(xn[:, m, :], x[:, m, :], small[:, 6 + m:7 + m], None, ALU.mult).then_inc(norm_xn, 1)
                if g is None:
                    return
                for j in (0, 2):
                    b = me.v.take(dve)
                    for kk_ in range(2):
                        k = 2 * j + kk_
                        for dst, name, off in g:
                            t = v.tensor_scalar(dst[:, k, :], ps[:, b, kk_ * S:(kk_ + 1) * S], col(name, off + k), None, ALU.mult)
                    t.then_inc(v_read, 1)

            def residual(t, m):
                b = me.v.take(dve)
                xs = x[:, m, t * 512:(t + 1) * 512]
                v.tensor_tensor(xs, xs, ps[:, b, :], ALU.add).then_inc(v_read, 1)

            for g in range(2):
                b = me.v.take(dve)
                v.tensor_copy(cols[:, g * P:g * P + ROWS_USED[g]], ps[:, b, 0:ROWS_USED[g]]).then_inc(v_read, 1)
            dve.wait_ge(v_read, me.v.n)
            dve.wait_ge(bc_in, 16 * len(BC))
            dve.wait_ge(x_in, 16)

            me.barrier("start")
            norm([(uT, "a_norm", 0)])
            link(v.memset(zp[:, :, 0:CONV - 1], 0.0))
            la = col("a_lambda", 0, KD)
            link(v.tensor_scalar(lam[:, 2, :], la, -1.0, None, ALU.mult))
            v.tensor_tensor(lam[:, 0, :], lam[:, 2, :], la, ALU.max).then_inc(lam_abs, 1)
            me.see(lam_exp)
            link(v.tensor_scalar(lam[:, 3, :], lam[:, 1, :], 2.0, None, ALU.add))
            link(v.reciprocal(lam[:, 3, :], lam[:, 3, :]))
            link(v.tensor_tensor(lam[:, 3, :], lam[:, 1, :], lam[:, 3, :], ALU.mult))
            link(v.tensor_tensor(lam[:, 4, :], lam[:, 3, :], lam[:, 3, :], ALU.mult))
            link(v.tensor_scalar(lam[:, 5, :], lam[:, 4, :], 1.0 / 17, 1.0 / 15, ALU.mult, ALU.add))
            for d in (13, 11, 9, 7, 5, 3, 1):
                link(v.tensor_tensor(lam[:, 5, :], lam[:, 5, :], lam[:, 4, :], ALU.mult))
                link(v.tensor_scalar(lam[:, 5, :], lam[:, 5, :], 1.0 / d, None, ALU.add))
            link(v.tensor_tensor(lam[:, 5, :], lam[:, 5, :], lam[:, 3, :], ALU.mult))
            link(v.tensor_scalar(lam[:, 6, :], lam[:, 2, :], 0.0, None, ALU.max))
            link(v.scalar_tensor_tensor(lam[:, 6, :], lam[:, 5, :], 2.0, lam[:, 6, :], ALU.mult, ALU.add))
            link(v.tensor_scalar(lam[:, 7, :], lam[:, 6, :], -LRU_C, None, ALU.mult))
            for f in range(KD):
                b = me.v.take(dve)
                v.tensor_copy(zp[:, f, CONV - 1:], ps[:, b, 0:S]).then_inc(v_read, 1)
                dve.wait_ge(v_read, me.v.n)
                link(v.tensor_scalar(xr[:, f, :], zp[:, f, 0:S], col("a_conv_w", f), col("a_conv_b", f), ALU.mult, ALU.add))
                for k in range(1, CONV):
                    t = v.scalar_tensor_tensor(xr[:, f, :], zp[:, f, k:k + S], col("a_conv_w", k * KD + f), xr[:, f, :],
                                               ALU.mult, ALU.add)
                    if k < CONV - 1:
                        link(t)
                t.then_inc(xr_ready, 1)
            me.see(ri_ready)
            v.tensor_tensor(rg[:], rg[:], lam[:, 7, :].unsqueeze(2).to_broadcast([P, KD, S]), ALU.mult).then_inc(la_ready, 1)
            link(v.tensor_tensor(ig[:], ig[:], xr[:], ALU.mult))
            me.see(a_ready)
            link(v.tensor_tensor(xr[:], aa[:], aa[:], ALU.mult))
            link(v.memset(aa[:, :, 0:1], 0.0))
            me.see(th_ready)
            v.scalar_tensor_tensor(th[:], xr[:], 1.0, th[:], ALU.add, ALU.mult).then_inc(t2_ready, 1)
            me.see(sq_ready)
            link(v.tensor_tensor(ig[:], ig[:], th[:], ALU.mult))
            link(v.tensor_tensor_scan(rg[:].rearrange("p k t -> p (k t)"), aa[:].rearrange("p k t -> p (k t)"),
                                      ig[:].rearrange("p k t -> p (k t)"), 0.0, ALU.mult, ALU.add))
            me.see(yg_ready)
            v.tensor_tensor(rg[:], rg[:], yg[:], ALU.mult).then_inc(yh_ready, 1)
            for t in range(2):
                for m in range(M):
                    residual(t, m)

            def wait(s, val):
                if not (isinstance(val, int) and val <= 0):
                    dve.wait_ge(s, val)

            def low(name, kind, B, n):
                dve.wait_ge(wh_full[kind], B + 1)
                v.tensor_tensor(wl[:, kind, 0:n], raw[:, plan[name][kind][0], 0:n], wh[:, kind, 0:n].bitcast(F32),
                                ALU.subtract).then_inc(wl_full[kind], 1)

            def hidden(u, w, root=None):
                dve.wait_ge(sg_ready, u + 1)
                dve.wait_ge(u_done, u + 1)
                wait(t_done, u)
                if root is None:
                    t = v.tensor_tensor(hb[:, 0:w], ps[:, 1, 0:w], sg[:, 0:w], ALU.mult)
                else:
                    t = v.scalar_tensor_tensor(hb[:, 0:w], ps[:, 1, 0:w], root, sg[:, 0:w], ALU.mult, ALU.mult)
                t.then_inc(h_ready, 1)

            def low_h(u, w):
                dve.wait_ge(hh_ready, u + 1)
                v.tensor_tensor(hl[:, 0:w], ps[:, 2, 0:w], hh[:, 0:w].bitcast(F32), ALU.subtract).then_inc(hl_ready, 1)

            def add_down(u, dst):
                dve.wait_ge(d_done, u + 1)
                for half in range(2):
                    o = dst[:, half * FB:(half + 1) * FB]
                    t = v.tensor_tensor(o, o, ps[:, 3 + half, :], ALU.add)
                t.then_inc(d_added, 1)

            def ffn(name, g, off):
                nb, wlast, B0, U0 = FFN[name]
                for j in range(4):
                    b = me.s.take(dve)
                    me.see(norm_h)
                    for kk_ in range(2):
                        k = 2 * j + kk_
                        t = v.scalar_tensor_tensor(xl[:, k, :], ps[:, b, kk_ * S:(kk_ + 1) * S], col(g, off + k),
                                                   xh[:, k, :].bitcast(F32), ALU.mult, ALU.subtract)
                    t.then_inc(s_read, 1)
                low(name, 0, B0, SLOT)
                low(name, 1, B0, SLOT)
                me.see(norm_sq, M)
                v.tensor_scalar(small[:, 2:4], small[:, 0:2], 1.0 / D, EPS, ALU.mult, ALU.add).then_inc(norm_ms, 1)
                me.see(norm_rt)
                v.reciprocal(small[:, 6:8], small[:, 4:6]).then_inc(root_done, 1)
                me.see(root_done)

                def body(b, w, first=False, last=False, wn=FB):
                    u, B = b * M + U0, b + B0
                    if not first:
                        low_h(u - 1, FB)
                    hidden(u, w, small[:, 6:7])
                    if not first:
                        add_down(u - 1, x[:, 1, :])
                    low(name, 2, B, w // P * D)
                    low_h(u, w)
                    if not last:
                        low(name, 0, B + 1, KD * wn)
                    hidden(u + 1, w, small[:, 7:8])
                    if not last:
                        low(name, 1, B + 1, KD * wn)
                    add_down(u, x[:, 0, :])

                body(0, FB, first=True)
                with dve.Fori(1, nb - 2) as b:
                    body(b, FB)
                body(nb - 2, FB, wn=wlast)
                body(nb - 1, wlast, last=True)
                low_h(U0 + nb * M - 1, wlast)
                add_down(U0 + nb * M - 1, x[:, 1, :])

            me.barrier("ffn0")
            ffn("ffn0", "f_norm", 0)

            me.barrier("nsa")
            norm([(uT, "kv_norm", 0), (ubT, "b_norm", 0)])
            for t in range(3):
                b = me.v.take(dve)
                v.tensor_copy(kvn[:, 0, t * 512:(t + 1) * 512], ps[:, b, :]).then_inc(v_read, 1)
                if t == 0:
                    marks["kvc_v"] = me.v.n
            def tables(dst, cos, sin, g, rows=P):
                v.tensor_tensor(dst[0:rows, 0, :], C(cos, rows), g[0:rows], ALU.mult)
                link(v.tensor_tensor(dst[0:rows, 1, :], C(sin, rows), g[0:rows], ALU.mult))

            gq, gk = bc[:, 0:HD], [bc[:, 64 + i * HD:64 + (i + 1) * HD] for i in range(3)]
            for m in range(M):
                tables(rope_g[:, m], f"cos{m}", f"sin{m}", gq)
                for w in range(2):
                    tables(rope_k[:, m, w], f"cos{m}", f"sin{m}", gk[1 + w])
            tables(rope_g[:, 2], "cosc", "sinc", gk[0], NCMP)

            def rope_norm(src, out, table, n, rows=P):
                a = tmp_a[0:rows, 0:n * HD].rearrange("p (h d) -> p h d", d=HD)
                b2 = tmp_b[0:rows, 0:n * HD].rearrange("p (h d) -> p h d", d=HD)
                link(v.tensor_tensor(a, src, src, ALU.mult))
                link(v.tensor_reduce(stat[0:rows, 0, 0:n], a, AX.X, ALU.add))
                link(v.tensor_scalar(stat[0:rows, 0, 0:n], stat[0:rows, 0, 0:n], 1.0 / HD, EPS, ALU.mult, ALU.add))
                dve.nop().then_inc(ms_ready, 1)
                me.see(root_ready)
                link(v.reciprocal(stat[0:rows, 1, 0:n], stat[0:rows, 1, 0:n]))
                link(v.tensor_tensor(a, src, stat[0:rows, 1, 0:n].unsqueeze(2).to_broadcast([rows, n, HD]), ALU.mult))
                link(v.tensor_tensor(b2, a, table[0:rows, 1, :].unsqueeze(1).to_broadcast([rows, n, HD]), ALU.mult))
                link(v.tensor_tensor(a, a, table[0:rows, 0, :].unsqueeze(1).to_broadcast([rows, n, HD]), ALU.mult))
                hf = HD // 2
                v.tensor_tensor(out[:, :, 0:hf], a[:, :, 0:hf], b2[:, :, hf:], ALU.subtract)
                link(v.tensor_tensor(out[:, :, hf:], a[:, :, hf:], b2[:, :, 0:hf], ALU.add))

            me.see(kvn_ready)
            for m in range(M):
                for w in range(2):
                    o = 512 + w * 512
                    kd = kdup[:, m, w]
                    rope_norm(kvn[:, m, o:o + NG * HD].rearrange("p (g d) -> p g d", d=HD), kd[:, :, 0, :],
                              rope_k[:, m, w], NG)
                    link(v.tensor_copy(kd[:, :, 1, :], kd[:, :, 0, :]))
            dve.nop().then_inc(k_ready, 1)
            for t in range(2):
                b = me.v.take(dve)
                v.tensor_copy(qn[:, 0, t * 512:(t + 1) * 512], ps[:, b, :]).then_inc(v_read, 1)
            for m in range(M):
                b = me.v.take(dve)
                v.tensor_tensor(gate[:, m, :, :].rearrange("p b h -> p (b h)"), ps[:, b, 0:3 * NH], bc[:, 384:384 + 3 * NH],
                                ALU.add).then_inc(v_read, 1)
            dve.wait_ge(v_read, me.v.n)
            dve.nop().then_inc(gate_ready, 1)
            R = NG * NCMP
            for j in range(4):
                b = me.v.take(dve)
                src = ps[:, b, 0:8 * R].rearrange("p (i k c) -> p i k c", i=4, k=2)
                for kv in range(2):
                    t = v.tensor_tensor(xcT[:, kv, 4 * j:4 * j + 4, :], src[:, :, kv, :],
                                        col("cmp_pos", kv * 16 + 4 * j, 4).unsqueeze(2).to_broadcast([P, 4, R]), ALU.add)
                t.then_inc(v_read, 1)
            me.see(qn_ready)
            for m in range(M):
                qh_ = qn[:, m, :].rearrange("p (h d) -> p h d", d=HD)
                rope_norm(qh_, qh_, rope_g[:, m], NH)
                dve.nop().then_inc(q_ready, 1)
            b = me.v.take(dve)
            b2v = bc[0:NCMP, 256:256 + 2 * HD].rearrange("p (k d) -> p k d", k=2)
            for kv in range(2):
                t = v.tensor_tensor(cmpn[0:NCMP, kv], ps[0:NCMP, b, kv * 256:(kv + 1) * 256].rearrange("p (g d) -> p g d", g=NG),
                                    b2v[:, kv, :].unsqueeze(1).to_broadcast([NCMP, NG, HD]), ALU.add)
            t.then_inc(v_read, 1)
            dve.wait_ge(v_read, me.v.n)
            rope_norm(cmpn[0:NCMP, 0], kcdup[0:NCMP, :, 0, :], rope_g[:, 2], NG, NCMP)
            link(v.tensor_copy(kcdup[0:NCMP, :, 1, :], kcdup[0:NCMP, :, 0, :]))
            dve.nop().then_inc(kc_ready, 1)
            b = me.v.take(dve)
            v.tensor_copy(kT[:, :, 0:NCMP], ps[:, b, 0:64].rearrange("p (g c) -> p g c", g=NG)[:, :, 0:NCMP]).then_inc(v_read, 1)
            me.see(gated)
            link(v.tensor_scalar(gate[:, 0, 0, :], gate[:, 0, 0, :], C("row_valid"), None, ALU.mult))

            def maxima(i, m, h):
                nk, st_ = P * (m + 1), stat[:, i % 3, :]
                b = me.sc.take(dve)
                v.tensor_reduce(st_[:, 0:1], ps[:, b, 0:NCMP], AX.X, ALU.max)
                v.tensor_reduce(st_[:, 1:2], ps[:, b, NCMP:NCMP + nk], AX.X, ALU.max)
                link(v.tensor_reduce(st_[:, 2:3], ps[:, b + 1, 0:nk], AX.X, ALU.max))
                v.tensor_scalar(st_[:, 3:6], st_[:, 0:3], -SCALE, None, ALU.mult).then_inc(max_ready, 1)

            def diagonals(i, m, h):
                st_ = stat[:, i % 3, :]
                dve.wait_ge(s_read, me.sc.base + i + 1)
                link(v.reciprocal(st_[:, 9:12], st_[:, 6:9]))
                link(v.tensor_tensor(st_[:, 12:15], st_[:, 9:12], gate[:, m, :, h], ALU.mult))
                v.tensor_tensor(diag[:, i % 2], C("ident").unsqueeze(1).to_broadcast([P, 3, P]),
                                st_[:, 12:15].unsqueeze(2).to_broadcast([P, 3, P]), ALU.mult).then_inc(diag_ready, 1)

            def outputs(m, h):
                if h % 2:
                    b = me.o.take(dve)
                    v.tensor_copy(oT[:, h // 2, m * P:(m + 1) * P], ps[:, b, 0:P]).then_inc(o_read, 1)

            pairs = [(m, h) for m in range(M) for h in range(NH)]
            me.scores_begin()
            maxima(0, *pairs[0])
            for i, pair in enumerate(pairs):
                diagonals(i, *pair)
                if i + 1 < len(pairs):
                    maxima(i + 1, *pairs[i + 1])
                if i:
                    outputs(*pairs[i - 1])
            outputs(*pair)
            me.scores_end()
            for t in range(2):
                for m in range(M):
                    residual(t, m)

            me.barrier("ffn1")
            ffn("ffn1", "f_norm", KD)

            def mixer(layer):
                norm([(uT, "mix_norm_2", layer * KD)])
                lg = [col("hgrn_lb_logits_2", i * HH, HH) for i in range(2)]
                link(v.tensor_copy(lbt[:, 7, :], lg[0]))
                link(v.tensor_tensor(lbt[:, 0, :], lbt[:, 7, :], lg[1], ALU.max))
                for i in range(2):
                    link(v.tensor_tensor(lbt[:, 1 + i, :], lg[i], lbt[:, 0, :], ALU.subtract))
                dve.nop().then_inc(lb_max, 1)
                me.see(lb_exp)
                link(v.tensor_tensor(lbt[:, 7, :], lbt[:, 1, :], lbt[:, 2, :], ALU.add))
                link(v.reciprocal(lbt[:, 7, :], lbt[:, 7, :]))
                for i in range(2):
                    link(v.tensor_tensor(lbt[:, 1 + i, :], lbt[:, 1 + i, :], lbt[:, 7, :], ALU.mult))
                link(v.tensor_copy(lbt[:, 3, :], lbt[:, 1, :]))
                if layer:
                    link(v.tensor_tensor(lbt[:, 3, :], lbt[:, 1, :], lbt[:, 2, :], ALU.add))
                link(v.tensor_tensor(lbt[:, 3, :], lbt[:, 3, :], lbt[:, 1, :], ALU.subtract))
                link(v.tensor_scalar(lbt[:, 4, :], lbt[:, 3, :], -1.0, 1.0, ALU.mult, ALU.add))
                link(v.tensor_scalar(lbt[:, 5:7, :], lbt[:, 3:5, :], 1e-12, None, ALU.max))
                dve.nop().then_inc(lb_clamped, 1)
                me.see(lb_ln)
                link(v.tensor_scalar(lbt[:, 1:3, :], lbt[:, 3:5, :], 1e-12, NEG, ALU.is_lt, ALU.mult))
                link(v.tensor_tensor(lbt[:, 5:7, :], lbt[:, 5:7, :], lbt[:, 1:3, :], ALU.add))

                def per_head(i):
                    return lbt[:, i, :].unsqueeze(2).to_broadcast([P, HH, S])

                for c in range(4):
                    b = me.v.take(dve)
                    v.tensor_copy(zf[:, c, :], ps[:, b, 0:S]).then_inc(v_read, 1)
                dve.wait_ge(v_read, me.v.n)
                link(v.scalar_tensor_tensor(t1[:], zf[:], -1.0, zf[:], ALU.mult, ALU.min))
                dve.nop().then_inc(zabs_ready, 1)
                link(v.memset(keep[:], 1.0))
                link(v.memset(keep[:].rearrange("p h (c s) -> p (h c) s", s=HC)[:, :, 0:1], 0.0))
                link(v.memset(sd[:], 0.0))
                dve.wait_ge(masks_in, 16 * (layer + 1))
                link(v.tensor_copy(lmask[:], t3[:].rearrange("p h t -> p (h t)")))
                me.see(zln_ready)
                link(v.scalar_tensor_tensor(t3[:], zf[:], 0.0, t2[:], ALU.min, ALU.subtract))
                link(v.tensor_tensor(t1[:], t3[:], zf[:], ALU.subtract))
                dve.nop().then_inc(zdif_ready, 1)
                link(v.tensor_tensor(t3[:], t3[:], per_head(6), ALU.add))
                link(v.tensor_tensor(t2[:], t3[:], per_head(5), ALU.subtract))
                link(v.scalar_tensor_tensor(t2[:], t2[:], -1.0, t2[:], ALU.mult, ALU.min))
                dve.nop().then_inc(fabs_ready, 1)
                link(v.tensor_tensor(t3[:], t3[:], per_head(5), ALU.max))
                me.see(kk_ready)
                link(v.tensor_tensor(kk[:], kk[:], per_head(4), ALU.mult))
                me.see(fln_ready)
                link(v.tensor_tensor(t3[:], t3[:], t2[:], ALU.add))
                flat = lambda a: a[:].rearrange("p h t -> p (h t)")
                link(v.tensor_tensor_scan(flat(bb), flat(keep), flat(t3), 0.0, ALU.mult, ALU.add))
                for c in range(4):
                    b = me.v.take(dve)
                    v.tensor_copy(skT[:, c, :], ps[:, b, 0:S]).then_inc(v_read, 1)
                me.see(qh_ready)

                def exponents(lv):
                    if lv <= 32:
                        bv = flat(bb).rearrange("p (n s) -> p n s", s=2 * lv)
                        tv = flat(t1).rearrange("p (n s) -> p n s", s=2 * lv)
                        mid = bv[:, :, lv - 1:lv].to_broadcast([P, HH * S // (2 * lv), lv])
                        v.tensor_tensor(tv[:, :, 0:lv], mid, bv[:, :, 0:lv], ALU.subtract)
                        link(v.tensor_tensor(tv[:, :, lv:], bv[:, :, lv:], mid, ALU.subtract))
                        return
                    chunk = lambda a, c: a[:, :, c * HC:(c + 1) * HC]
                    last = lambda c: bb[:, :, c * HC + HC - 1:c * HC + HC].to_broadcast([P, HH, HC])
                    if lv == 64:
                        for c in (0, 2):
                            v.tensor_tensor(chunk(t1, c), last(c), chunk(bb, c), ALU.subtract)
                        for c in (1, 3):
                            t = v.tensor_copy(chunk(t1, c), chunk(bb, c))
                        link(t)
                        return
                    v.tensor_tensor(chunk(t1, 1), last(1), chunk(bb, 1), ALU.subtract)
                    v.tensor_copy(chunk(t1, 2), chunk(bb, 2))
                    v.tensor_tensor(chunk(t1, 3), chunk(bb, 3), last(2), ALU.add)
                    link(v.tensor_tensor(chunk(t1, 0), last(0), chunk(bb, 0), ALU.subtract))
                    link(v.tensor_tensor(chunk(t1, 0), chunk(t1, 0), last(1), ALU.add))

                def factors(lv):
                    sz = 2 * lv
                    view = lambda a: flat(a).rearrange("p (n s) -> p n s", s=sz)
                    v.tensor_tensor(view(t2)[:, :, 0:lv], view(kk)[:, :, 0:lv], view(t1)[:, :, 0:lv], ALU.mult)
                    link(v.tensor_tensor(view(t2)[:, :, lv:], view(qh)[:, :, lv:], view(t1)[:, :, lv:], ALU.mult))

                def collect(j, lv):
                    if lv == 128:
                        b = me.v.take(dve)
                        v.tensor_copy(sx[:].rearrange("p h t -> p (h t)"), ps[:, b, :]).then_inc(v_read, 1)
                        dve.wait_ge(v_read, me.v.n)
                        return
                    mask = lmask[:, j * P:(j + 1) * P].unsqueeze(1).to_broadcast([P, 4, P])
                    for hp in range(2):
                        b = me.v.take(dve)
                        v.copy_predicated(sd[:, 2 * hp:2 * hp + 2].rearrange("p a m t -> p (a m) t"), mask,
                                          ps[:, b, :].rearrange("p (n t) -> p n t", n=4)).then_inc(v_read, 1)
                    dve.wait_ge(v_read, me.v.n)

                levels = [0] + LEVELS + [64, 128]
                for j, lv in enumerate(levels):
                    if lv:
                        exponents(lv)
                        dve.nop().then_inc(decay_ready, 1)
                        collect(j - 1, levels[j - 1])
                        me.see(decay_exp)
                        factors(lv)
                    dve.nop().then_inc(level_ready, 1)
                collect(len(levels) - 1, 128)
                for m in range(M):
                    b = me.v.take(dve)
                    v.tensor_copy(oa[:, m, :], ps[:, b, :]).then_inc(v_read, 1)
                dve.wait_ge(v_read, me.v.n)
                o8 = oa[:].rearrange("p m (h d) -> p (m h) d", d=P)
                t8 = flat(t1).rearrange("p (n d) -> p n d", d=P)
                link(v.tensor_tensor(t8, o8, o8, ALU.mult))
                link(v.tensor_reduce(small[:, 16:24], t8, AX.X, ALU.add))
                link(v.tensor_scalar(small[:, 16:24], small[:, 16:24], 1.0 / P, EPS, ALU.mult, ALU.add))
                dve.nop().then_inc(oms_ready, 1)
                me.see(ort_ready)
                link(v.reciprocal(small[:, 32:40], small[:, 24:32]))
                link(v.tensor_tensor(o8, o8, small[:, 32:40].unsqueeze(2).to_broadcast([P, 8, P]), ALU.mult))
                g = bc[:, 432 + layer * P:432 + (layer + 1) * P].unsqueeze(1).to_broadcast([P, 8, P])
                link(v.tensor_tensor(o8, o8, g, ALU.mult))
                link(v.tensor_tensor(oa[:], oa[:], hog[:], ALU.mult))
                dve.nop().then_inc(oa_ready, 1)

                for h in range(SH):
                    b = me.s.take(dve)
                    me.see(ln_ready)
                    s_ = sp[:, h % 2, :]
                    v.scalar_tensor_tensor(s_, ps[:, b, 0:384], 0.0, e1[:, h % 2, :], ALU.max, ALU.add).then_inc(s_read, 1)
                    dve.wait_ge(s_read, me.s.n)
                    diag = s_.rearrange("p (a t) -> p a t", t=P)[:, 0:3:2, :]
                    v.tensor_tensor(diag, diag, C("before").unsqueeze(1).to_broadcast([P, 2, P]), ALU.mult).then_inc(sp_ready, 1)
                    if h % 2:
                        b = me.v.take(dve)
                        v.tensor_copy(obT[:, h // 2, :], ps[:, b, 0:S]).then_inc(v_read, 1)
                for m in range(M):
                    for half in range(2):
                        cs = slice(half * 512, half * 512 + 512)
                        b = me.v.take(dve)
                        v.tensor_tensor(sga[:, m, cs], ps[:, b, :], sga[:, m, cs], ALU.mult).then_inc(v_read, 1)
                        b = me.v.take(dve)
                        v.tensor_tensor(sgb[:, m, cs], ps[:, b, :], sgb[:, m, cs], ALU.mult).then_inc(v_read, 1)
                dve.wait_ge(v_read, me.v.n)
                v.tensor_tensor(sga[:], sga[:], sgb[:], ALU.add).then_inc(y_ready, 1)
                for t in range(2):
                    for m in range(M):
                        residual(t, m)

            me.barrier("mix0")
            mixer(0)
            me.barrier("ffn2")
            ffn("ffn2", "ffn_norm_2", 0)
            me.barrier("mix1")
            mixer(1)

            me.barrier("moe")
            norm([(uT, "ffn_norm_2", KD)])
            dve.wait_ge(ye_in, 16)
            b = me.v.take(dve)
            v.tensor_copy(R_["logit"], ps[:, b, 0:M * E]).then_inc(v_read, 1)
            dve.wait_ge(v_read, me.v.n)
            for m in range(M):
                lm = R_["logit"][:, m * E:(m + 1) * E]
                ge8 = R_["a64"].rearrange("p (e f) -> p e f", e=E)
                eq8 = R_["b64"].rearrange("p (e f) -> p e f", e=E)
                mine, other = lm.unsqueeze(2).to_broadcast([P, E, E]), lm.unsqueeze(1).to_broadcast([P, E, E])
                link(v.tensor_tensor(ge8, other, mine, ALU.is_gt))
                link(v.tensor_tensor(eq8, other, mine, ALU.is_equal))
                link(v.tensor_tensor(R_["b64"], R_["b64"], C("lower_e"), ALU.mult))
                link(v.tensor_tensor(R_["a64"], R_["a64"], R_["b64"], ALU.add))
                link(v.tensor_reduce(R_["rank"], ge8, AX.X, ALU.add))
                link(v.tensor_scalar(sel[:, m, :], R_["rank"], 1.5, None, ALU.is_lt))
                link(v.tensor_reduce(R_["neg_max"][:, m:m + 1], lm, AX.X, ALU.max))
            link(v.tensor_scalar(R_["neg_max"], R_["neg_max"], -1.0, None, ALU.mult))
            dve.nop().then_inc(sel_ready, 1)
            dve.nop().then_inc(lmax_ready, 1)
            me.see(lexp_ready)
            for m in range(M):
                wm = R_["weight"][:, m * E:(m + 1) * E]
                link(v.tensor_tensor(wm, R_["exp"][:, m * E:(m + 1) * E], sel[:, m, :], ALU.mult))
                link(v.tensor_reduce(R_["sum"][:, m:m + 1], wm, AX.X, ALU.add))
                link(v.reciprocal(R_["sum"][:, m:m + 1], R_["sum"][:, m:m + 1]))
                link(v.tensor_scalar(wm, wm, R_["sum"][:, m:m + 1], None, ALU.mult))
            b = me.v.take(dve)
            v.tensor_copy(R_["pos"], ps[:, b, 0:3 * E]).then_inc(v_read, 1)
            dve.wait_ge(v_read, me.v.n)
            count = R_["pos"][:, 2 * E:3 * E]
            link(v.tensor_scalar(R_["tiles"], count, 0.5, None, ALU.is_gt))
            link(v.tensor_scalar(R_["ones"], count, P + 0.5, None, ALU.is_gt))
            link(v.tensor_tensor(R_["tiles"], R_["tiles"], R_["ones"], ALU.add))
            link(v.memset(R_["ones"], 1.0))
            link(v.tensor_tensor_scan(R_["upto"], R_["ones"], R_["tiles"], 0.0, ALU.mult, ALU.add))
            link(v.tensor_tensor(R_["before"], R_["upto"], R_["tiles"], ALU.subtract))
            shape = [P, ITEMS, E]
            own = R_["owner"].rearrange("p (i e) -> p i e", i=ITEMS)
            tmp = R_["tmp"].rearrange("p (i e) -> p i e", i=ITEMS)
            iota_i = C("iota_i").unsqueeze(2).to_broadcast(shape)
            over_e = lambda a: a.unsqueeze(1).to_broadcast(shape)
            link(v.tensor_tensor(own, iota_i, over_e(R_["before"]), ALU.is_ge))
            link(v.tensor_tensor(tmp, iota_i, over_e(R_["upto"]), ALU.is_lt))
            link(v.tensor_tensor(own, own, tmp, ALU.mult))

            def of_item(dst, a):
                link(v.tensor_tensor(tmp, own, over_e(a), ALU.mult))
                link(v.tensor_reduce(dst, tmp, AX.X, ALU.add))

            of_item(R_["expert"], C("iota_e"))
            of_item(R_["first"], R_["before"])
            link(v.tensor_tensor(R_["first"], C("iota_i"), R_["first"], ALU.subtract))
            link(v.tensor_scalar(R_["first"], R_["first"], float(P), None, ALU.mult))
            for m in range(M):
                sl, wi = slot_of[:, m, :], weight_of[:, m, :]
                of_item(wi, R_["weight"][:, m * E:(m + 1) * E])
                of_item(sl, R_["pos"][:, m * E:(m + 1) * E])
                of_item(R_["there"], sel[:, m, :])
                link(v.tensor_tensor(sl, sl, R_["first"], ALU.subtract))
                link(v.tensor_scalar(sl, sl, 1.0, None, ALU.add))
                link(v.tensor_tensor(sl, sl, R_["there"], ALU.mult))
                link(v.tensor_scalar(sl, sl, -1.0, None, ALU.add))
            link(v.tensor_copy(rti[0:1, 0:1], R_["upto"][0:1, E - 1:E]))
            link(v.tensor_copy(rti[0:1, 1:1 + ITEMS], R_["expert"][0:1, :]))
            dve.nop().then_inc(items_ready, 1)
            for m in range(M):
                link(v.tensor_tensor(xn[:, m, :], xn[:, m, :], ye[:], ALU.mult))
            n = dve.value_load(rti[0:1, 0:1], min_val=MIN_ITEMS, max_val=ITEMS)

            def add_up(u, first=False):
                if not first:
                    return add_down(u, ye)
                dve.wait_ge(d_done, u + 1)
                for half in range(2):
                    t = v.tensor_copy(ye[:, half * FB:(half + 1) * FB], ps[:, 3 + half, :])
                t.then_inc(d_added, 1)

            def pick_tokens(i):
                for m in range(M):
                    t = v.tensor_scalar(pick[:, m, :], C("iota_slot"), slot_of[:, m, bass.ds(i, 1)], None, ALU.is_equal)
                return t

            def weigh_tokens(i):
                for m in range(M):
                    t = v.tensor_scalar(pickw[:, m, :], C("iota_slot"), slot_of[:, m, bass.ds(i, 1)],
                                        weight_of[:, m, bass.ds(i, 1)], ALU.is_equal, ALU.mult)
                return t

            def low_tokens(count):
                dve.wait_ge(xh_ready, count)
                for j in range(2):
                    t = v.tensor_tensor(xl[:, 4 * j:4 * j + 4, 0:P], ps[:, 5 + j, :].rearrange("p (k t) -> p k t", k=4),
                                        xh[:, 4 * j:4 * j + 4, 0:P].bitcast(F32), ALU.subtract)
                t.then_inc(xl_ready, 1)

            def item(it, last=False):
                B, U = it * NBB + MOE_B, it * NBB + MOE_U

                def step(b, first=False):
                    low_h(U + b - 1, FB)
                    low("moe", 0, B + b + 1, SLOT)
                    hidden(U + b, FB)
                    low("moe", 1, B + b + 1, SLOT)
                    add_up(U + b - 1, first)
                    low("moe", 2, B + b, SLOT)

                step(1, first=True)
                dve.wait_ge(picked, it + 1)
                t = weigh_tokens(it)
                if not last:
                    t = pick_tokens(it + 1)
                t.then_inc(pick_ready, 1)
                with dve.Fori(2, NBB - 1) as b:
                    step(b)
                u = U + (NBB - 1)
                low_h(u - 1, FB)
                if not last:
                    low("moe", 0, B + NBB, SLOT)
                hidden(u, FB)
                if not last:
                    low_tokens(it + 2)
                    low("moe", 1, B + NBB, SLOT)
                add_up(u - 1)
                low("moe", 2, B + (NBB - 1), SLOT)
                if last:
                    low_h(u, FB)
                    add_up(u)
                else:
                    step(NBB)
                dve.wait_ge(put_done, it + 1)
                for m in range(M):
                    for half in range(2):
                        xs = x[:, m, half * FB:(half + 1) * FB]
                        t = v.tensor_tensor(xs, xs, ps[:, 3 + 2 * m + half, :], ALU.add)
                t.then_inc(put_added, 1)

            dve.nop().then_inc(put_added, 1)
            pick_tokens(0).then_inc(pick_ready, 1)
            low("moe", 0, MOE_B, SLOT)
            low_tokens(1)
            low("moe", 1, MOE_B, SLOT)
            low("moe", 0, MOE_B + 1, SLOT)
            hidden(MOE_U, FB)
            low("moe", 1, MOE_B + 1, SLOT)
            low("moe", 2, MOE_B, SLOT)
            with dve.Fori(0, n - 1) as it:
                item(it)
            item(n - 1, last=True)
            me.barrier("final")
            norm()
            dve.wait_ge(final_in, 16)
            for m in range(M):
                dve.wait_ge(norm_xn, M * me.norms)
                v.tensor_tensor(xn[:, m, :], xn[:, m, :], uT[:, 0:4, :].rearrange("p a b -> p (a b)"), ALU.mult).then_inc(out_ready, 1)

        @block.sync
        def _(sp_eng):
            sy = sp_eng
            sy.dma_start(x[:], A["x"].rearrange("a (m p) d -> p (a m) d", p=P)).then_inc(x_in, 16)

            def kp(w):
                return w.rearrange("(k p) n -> p k n", p=P)

            held = [None, None, None]

            def fill(s, src, k, w, free=None):
                if free or held[s]:
                    sy.wait_ge(*(free or held[s]))
                sy.dma_start(raw[:, s, 0:k * w].rearrange("p (k n) -> p k n", k=k), src).then_inc(slot_full[s], 16)

            def ffn_tiles(name, win_g, win_u, wdn):
                nb, wlast = FFN[name][:2]
                B0 = FFN[name][2]

                slot = [s for s, _ in plan[name]]

                def gu(b, w=FB, st=False, free=True):
                    cs = slice(b * FB, b * FB + w) if st else bass.ds(b * FB, FB)
                    fill(slot[0], kp(win_g)[:, :, cs], KD, w, (wl_full[0], b + B0) if free else None)
                    fill(slot[1], kp(win_u)[:, :, cs], KD, w, (wl_full[1], b + B0) if free else None)

                def dn(b, w=FB, st=False, free=True):
                    cs = slice(b * 4, b * 4 + w // P) if st else bass.ds(b * 4, 4)
                    fill(slot[2], kp(wdn)[:, cs, :], w // P, D, (wl_full[2], b + B0) if free else None)

                gu(0, FB, True, free=False)
                dn(0, FB, True, free=False)
                gu(1, FB, True)
                with sy.Fori(1, nb - 2) as b:
                    dn(b)
                    gu(b + 1)
                dn(nb - 2, FB, True)
                gu(nb - 1, wlast, True)
                dn(nb - 1, wlast, True)
                for kind in range(3):
                    held[slot[kind]] = (wl_full[kind], B0 + nb)

            for key in order:
                if len(key) == 1 and key[0] in FFN:
                    if key[0] == "ffn2":
                        ffn_tiles("ffn2", A["dense_w_gate_2"][0], A["dense_w_up_2"][0], A["dense_w_down_2"][0])
                    else:
                        i = int(key[0][3])
                        ffn_tiles(key[0], A["f_w_in"][i, :, 0:F_A], A["f_w_in"][i, :, F_A:2 * F_A], A["f_w_out"][i])
                    continue
                if key == ("moe",):
                    continue
                s, f = plan[key]
                kind = key[0]
                t = key[-1]
                if kind == "a_in":
                    fill(s, kp(A["a_w_in"][0])[:, :, t * 512:t * 512 + 512], KD, 512)
                elif kind == "a_gate":
                    fill(s, A["a_gate_w"][0].rearrange("g h i j -> i (g h) j"), 16, P)
                elif kind == "a_out":
                    fill(s, kp(A["a_w_out"][0])[:, :, t * 512:t * 512 + 512], KD, 512)
                elif kind == "kv":
                    fill(s, kp(A["kv_w"])[:, :, t * 512:t * 512 + 512], KD, 512)
                elif kind == "cmp":
                    fill(s, kp(A["cmp_w1"][t]), 16, CH)
                elif kind == "b_in":
                    w = 512 if t < 2 else 3 * NH
                    fill(s, kp(A["b_w_in"][0])[:, :, t * 512:t * 512 + w], KD, w)
                elif kind == "b_out":
                    fill(s, kp(A["b_w_out"][0])[:, :, t * 512:t * 512 + 512], KD, 512)
                elif kind == "mix_in":
                    fill(s, kp(A["w_in_2"][key[1]])[:, :, t * 512:t * 512 + 512], KD, 512)
                elif kind == "branch":
                    w = A["w_branch_hgrn_2"] if t == 0 else A["w_branch_sb_2"]
                    fill(s, kp(w[key[1]]), 4, D)
                elif kind == "mix_out":
                    fill(s, kp(A["w_out_2"][key[1]])[:, :, t * 512:t * 512 + 512], KD, 512)
                held[s] = freed[key]

            for s in range(3):
                sy.wait_ge(*held[s])
            sy.wait_ge(items_ready, 1)
            n = sy.value_load(rti[0:1, 0:1], min_val=MIN_ITEMS, max_val=ITEMS)
            wg = A["moe_w_gate_2"][0].rearrange("e (k p) n -> e p k n", p=P)
            wu = A["moe_w_up_2"][0].rearrange("e (k p) n -> e p k n", p=P)
            wd = A["moe_w_down_2"][0].rearrange("e (k p) n -> e p k n", p=P)
            slot = [s for s, _ in plan["moe"]]

            def expert_of(it):
                return sy.value_load(rti[0:1, bass.ds(it + 1, 1)], min_val=0, max_val=E - 1)

            def one(kind, w, e, B, cs):
                src = w[bass.ds(e, 1), :, cs, :] if kind == 2 else w[bass.ds(e, 1), :, :, cs]
                sy.wait_ge(wl_full[kind], B)
                k = 4 if kind == 2 else KD
                sy.dma_start(raw[:, slot[kind], :].rearrange("p (k n) -> p k n", k=k),
                             src.rearrange("e p k n -> (e p) k n")).then_inc(slot_full[slot[kind]], 16)

            def item(it, last=False):
                B = it * NBB + MOE_B
                e = expert_of(it)
                with sy.Fori(0, NBB - 1) as b:
                    one(0, wg, e, B + b + 1, bass.ds(b * FB + FB, FB))
                    one(1, wu, e, B + b + 1, bass.ds(b * FB + FB, FB))
                    one(2, wd, e, B + b, bass.ds(b * 4, 4))
                if not last:
                    e_next = expert_of(it + 1)
                    one(0, wg, e_next, B + NBB, slice(0, FB))
                    one(1, wu, e_next, B + NBB, slice(0, FB))
                one(2, wd, e, B + (NBB - 1), slice((NBB - 1) * 4, NBB * 4))

            e = sy.value_load(rti[0:1, 1:2], min_val=0, max_val=E - 1)
            one(0, wg, e, MOE_B, slice(0, FB))
            one(1, wu, e, MOE_B, slice(0, FB))
            with sy.Fori(0, n - 1) as it:
                item(it)
            item(n - 1, last=True)
            sy.wait_ge(out_ready, 2)
            sy.dma_start(out.rearrange("a (m p) d -> p (a m) d", p=P), xn[:]).then_inc(out_sent, 16)
            sy.wait_ge(out_sent, 16)

        @block.gpsimd
        def _(po):
            po.dma_start(const[:], A["const_f32"]).then_inc(const_in, 16)
            for g in range(2):
                at = 0
                for name, r in ROWS[g]:
                    a = A[name]
                    n = 1
                    for d in a.shape:
                        n *= d
                    assert n == r * P, name
                    names = " ".join("abcd"[:len(a.shape)])
                    flat = a if len(a.shape) == 1 else a.rearrange(f"{names} -> ({names})")
                    po.dma_start(rowbuf[at:at + r, g, :], flat.rearrange("(r q) -> r q", q=P)).then_inc(rows_in[g], 16)
                    at += r
            for name, (at, w) in BC.items():
                a = A[name]
                names = " ".join("abcd"[:len(a.shape)])
                flat = a if len(a.shape) == 1 else a.rearrange(f"{names} -> ({names})")
                po.dma_start(bc[:, at:at + w], flat.partition_broadcast(P)).then_inc(bc_in, 16)
            po.wait_ge(stage, 3 * marks["nsa"])
            po.dma_start(w2[:].rearrange("p k c d -> p (k c) d"),
                         A["cmp_w2"].rearrange("k (c p) d -> p (k c) d", p=P)).then_inc(w2_in, 16)
            nc.gpsimd.memset(qT[:], 0.0).then_inc(q_zeroed, 1)
            po.wait_ge(v_read, marks["kvc_v"])
            po.wait_ge(a_read, marks["kvc_a"])
            po.dma_start(kv_scratch.rearrange("(m p) n -> p m n", p=P), kvn[:, :, 0:512]).then_inc(kvc_out, 16)
            po.wait_ge(kvc_out, 16)
            for kv in range(2):
                for g in range(NG):
                    r = (kv * NG + g) * NCMP
                    for half in range(2):
                        src = kv_scratch[half * CS:half * CS + NCMP * CS, kv * 256 + g * HD:kv * 256 + g * HD + HD]
                        po.dma_start(xc[r:r + NCMP, half * CS * HD:(half + 1) * CS * HD].rearrange(
                            "c (l d) -> c l d", d=HD), src.rearrange("(c l) d -> c l d", l=CS)).then_inc(kvc_in, 16)
            for layer in range(2):
                po.wait_ge(stage, 3 * marks[f"mix{layer}"])
                po.dma_start(t3[:].rearrange("p h t -> p (h t)"), A["const_masks"]).then_inc(masks_in, 16)
            po.wait_ge(stage, 3 * marks["moe"])
            po.dma_start(ye[:], A["ffn_norm_2"][1, :].partition_broadcast(P)).then_inc(ye_in, 16)
            po.dma_start(wr[:].rearrange("p (k e) -> p k e", e=E),
                         A["moe_router_2"][0].rearrange("(k p) e -> p k e", p=P)).then_inc(wr_in, 16)
            po.wait_ge(stage, 3 * marks["final"])
            po.dma_start(uT[:, 0:4, :].rearrange("p a b -> p (a b)"), A["final_norm_2"].partition_broadcast(P)).then_inc(final_in, 16)


_INS = ["x", "a_norm", "a_w_in", "a_conv_w", "a_conv_b", "a_gate_w", "a_gate_b", "a_lambda", "a_w_out", "kv_norm",
        "kv_w", "k_norm", "cmp_pos", "cmp_w1", "cmp_b1", "cmp_w2", "cmp_b2", "b_norm", "b_w_in", "b_gate_b", "q_norm",
        "b_w_out", "f_norm", "f_w_in", "f_w_out", "mix_norm_2", "w_in_2", "hgrn_lb_logits_2", "hgrn_out_norm_2",
        "w_branch_hgrn_2", "w_branch_sb_2", "w_out_2", "ffn_norm_2", "dense_w_gate_2", "dense_w_up_2",
        "dense_w_down_2", "moe_router_2", "moe_w_gate_2", "moe_w_up_2", "moe_w_down_2", "final_norm_2"]


def kernel(**inputs):
    import concourse.bacc as bacc
    from concourse.bass_utils import run_bass_kernel_spmd

    nc = bacc.Bacc("TRN2", target_bir_lowering=False, num_devices=1)
    arrays = {name: np.ascontiguousarray(inputs[name]) for name in _INS}
    arrays["const_f32"], arrays["const_masks"] = CONST_F32, CONST_MASKS
    aps = {name: nc.dram_tensor(f"in_{name}", a.shape, mybir.dt.from_np(a.dtype), kind="ExternalInput").ap()
           for name, a in arrays.items()}
    out = nc.dram_tensor("out", (1, S, D), F32, kind="ExternalOutput").ap()
    build(nc, aps, out)
    r = run_bass_kernel_spmd(nc, [{f"in_{name}": a for name, a in arrays.items()}], core_ids=[0])
    return r.results[0]["out"]
```

```python
from contextlib import ExitStack

import numpy as np
import concourse.bass as bass
from concourse import mybir

F32 = mybir.dt.float32
F32R = mybir.dt.float32r
I32 = mybir.dt.int32
U8 = mybir.dt.uint8
ACT = mybir.ActivationFunctionType
ALU = mybir.AluOpType
AX = mybir.AxisListType

P = 128
S = 256
M = S // P
D = 1024
KD = D // P
EPS = 1e-6
NEG = -1e30
SLOT = 4096

HD, NH, NG = 64, 16, 4
HPG = NH // NG
CB, CS, CH = 32, 16, 256
NCMP = (S - CB) // CS + 1
SCALE = HD ** -0.5
KALL = NCMP + 2 * S
LRU_C = 8.0
CONV = 4
F_A = 2816
F_B = 3584
FB = 512
HH, HC = 4, 64
SH = 8
LEVELS = [1, 2, 4, 8, 16, 32]
E = 8
GIVE_BANKS = [5, 6, 7, 2]
ITEMS = 12
MIN_ITEMS = 2 * S // P
NBB = F_B // FB

IN_ORDER = [1, 0, 5, 4, 2, 6, 3, 7, 8, 9, 10]
REST = IN_ORDER[4:]
HALVES = 2 * len(REST)
HW = 256
Q_OUT = 2 * len(IN_ORDER)
LEVEL_AT = {1: 0, 3: 1, 4: 2, 6: 4, 7: 8, 9: 16, 10: 32, 12: 64, 13: 128}
HEAD_AT = {i + 4: i for i in range(SH)}


CONSTS = {}


def _const_arrays():
    cols, at = [], 0

    def put(name, a):
        nonlocal at
        a = np.broadcast_to(np.asarray(a, np.float32), (P, np.asarray(a).shape[-1]))
        CONSTS[name] = (at, a.shape[1])
        cols.append(a)
        at += a.shape[1]

    i = np.arange(P)
    put("ident", np.eye(P))
    put("neg_causal", np.where(i[None, :] > i[:, None], NEG, 0.0))
    put("before", (i[:, None] < i[None, :]) * 1.0)
    put("neg_not_before", np.where(i[:, None] < i[None, :], 0.0, NEG))
    put("minus_from", np.where(i[:, None] >= i[None, :], -1.0, 0.0))
    put("minus_one", -np.ones((P, P)))
    put("one", np.ones((P, P)))
    put("iota_slot", i[None, :])
    half = HD // 2
    freqs = np.power(np.float32(10000.0), -np.arange(half, dtype=np.float32) / np.float32(half)).astype(np.float32)

    def rope(pos):
        ang = (pos.astype(np.float32)[:, None] * freqs[None, :]).astype(np.float32)
        c, s = np.cos(ang).astype(np.float32), np.sin(ang).astype(np.float32)
        return np.concatenate([c, c], 1), np.concatenate([s, s], 1)

    for m in range(M):
        c, s = rope(m * P + i)
        put(f"cos{m}", c)
        put(f"sin{m}", s)
    c, s = rope(np.minimum(i, NCMP - 1) * CS + CB - 1)
    put("cosc", c)
    put("sinc", s)
    last = np.arange(NCMP) * CS + CB - 1
    for m in range(M):
        t = (m * P + i)[:, None]
        put(f"neg_keys{m}", np.concatenate([np.where(last[None, :] <= t, 0.0, NEG),
                                            np.where(np.arange((m + 1) * P)[None, :] <= t, 0.0, NEG)], 1))
    put("row_valid", ((i >= CB - 1) * 1.0)[:, None])
    e = np.arange(E)
    put("lower_e", ((e[None, :] < e[:, None]) * 1.0).reshape(1, -1))
    put("iota_e", e[None, :])
    put("iota_i", np.arange(ITEMS)[None, :])
    base = np.concatenate(cols, 1)
    masks = [np.eye(P)]
    for lv in LEVELS + [64]:
        same = (i[:, None] // (2 * lv)) == (i[None, :] // (2 * lv))
        masks.append(same & (i[:, None] % (2 * lv) < lv) & (i[None, :] % (2 * lv) >= lv))
    masks = np.stack(masks, 1).astype(np.float32).reshape(P, -1)
    return np.ascontiguousarray(base), np.ascontiguousarray(masks)


CONST_F32, CONST_MASKS = _const_arrays()

ROWS = [
    [("a_norm", 8), ("a_conv_w", 32), ("a_conv_b", 8), ("a_gate_b", 16), ("a_lambda", 8),
     ("kv_norm", 8), ("b_norm", 8), ("f_norm", 16)],
    [("mix_norm_2", 16), ("ffn_norm_2", 16), ("hgrn_lb_logits_2", 8), ("cmp_b1", 4), ("cmp_pos", 32)],
]
COL = {}
for _g, _names in enumerate(ROWS):
    _at = _g * P
    for _n, _r in _names:
        COL[_n] = _at
        _at += _r
ROWS_USED = [sum(r for _, r in g) for g in ROWS]
BC = {"q_norm": (0, 64), "k_norm": (64, 192), "cmp_b2": (256, 128), "b_gate_b": (384, 48), "hgrn_out_norm_2": (432, 256)}
BC_W = 688


class Ring:

    def __init__(self, banks, filled, read):
        self.banks, self.filled, self.read, self.n = banks, filled, read, 0

    def claim(self, pe):
        if self.n >= len(self.banks):
            pe.wait_ge(self.read, self.n - len(self.banks) + 1)
        self.n += 1
        return self.banks[(self.n - 1) % len(self.banks)]

    def take(self, eng):
        self.n += 1
        eng.wait_ge(self.filled, self.n)
        return self.banks[(self.n - 1) % len(self.banks)]


def weight_plan():
    plan, fills = {}, [0, 0, 0]
    order, nxt = [], 0

    def tile(*key):
        nonlocal nxt
        s = nxt
        nxt = (nxt + 1) % 3
        plan[key] = (s, fills[s])
        fills[s] += 1
        order.append(key)

    def ffn(name, blocks):
        nonlocal nxt
        plan[name] = [((nxt + kind) % 3, fills[(nxt + kind) % 3]) for kind in range(3)]
        for s in range(3):
            fills[s] += blocks
        order.append((name,))

    for t in (2, 3):
        tile("a_in", t)
    tile("a_gate")
    for t in (0, 1):
        tile("a_in", t)
    for t in (0, 1):
        tile("a_out", t)
    ffn("ffn0", 6)
    for t in range(3):
        tile("kv", t)
    for t in range(3):
        tile("b_in", t)
    for t in range(2):
        tile("cmp", t)
    for t in range(2):
        tile("b_out", t)
    ffn("ffn1", 6)
    for layer in range(2):
        for t in IN_ORDER:
            tile("mix_in", layer, t)
        tile("branch", layer, 1)
        tile("branch", layer, 0)
        for t in range(2):
            tile("mix_out", layer, t)
        if layer == 0:
            ffn("ffn2", NBB)
        else:
            ffn("moe", 0)
    return plan, order


def build(nc, A, out, dbg=None):
    plan, order = weight_plan()
    ctx = ExitStack()
    with ctx:
        def sbuf(name, shape, dt=F32, stack=ctx):
            return stack.enter_context(nc.sbuf_tensor(name, shape, dt))

        def sem(name):
            return ctx.enter_context(nc.semaphore(name))

        x = sbuf("x", [P, M, D])
        xn = sbuf("xn", [P, M, D])
        with ExitStack() as st:
            uT = sbuf("uT", [P, KD, S], stack=st)
            raw = sbuf("raw", [P, 3, SLOT], stack=st)
        uh = sbuf("uh", [P, KD, S], F32R)
        raw_low = sbuf("raw_low", [P, 3, SLOT], F32R)
        const = sbuf("const", [P, CONST_F32.shape[1]])
        cols = sbuf("cols", [P, 2 * P])
        bc = sbuf("bc", [P, BC_W])
        small = sbuf("small", [P, 64])

        def C(name, rows=P):
            a, w = CONSTS[name]
            return const[0:rows, a:a + w]

        def col(name, i=0, n=1):
            return cols[:, COL[name] + i:COL[name] + i + n]

        with ExitStack() as st:
            rowbuf = sbuf("rowbuf", [P, 2, P], stack=st)
            zp = sbuf("zp", [P, KD, S + CONV - 1], stack=st)
            xr = sbuf("xr", [P, KD, S], stack=st)
            rg = sbuf("rg", [P, KD, S], stack=st)
            ig = sbuf("ig", [P, KD, S], stack=st)
            aa = sbuf("aa", [P, KD, S], stack=st)
            th = sbuf("th", [P, KD, S], stack=st)
            yg = sbuf("yg", [P, KD, S], stack=st)
            lam = sbuf("lam", [P, 8, KD], stack=st)
        with ExitStack() as st:
            wh = sbuf("wh", [P, 3, SLOT], F32R, stack=st)
            wl = sbuf("wl", [P, 3, SLOT], F32R, stack=st)
            xh = sbuf("xh", [P, KD, S], F32R, stack=st)
            xl = sbuf("xl", [P, KD, S], F32R, stack=st)
            sg = sbuf("sg", [P, FB], stack=st)
            hb = sbuf("hb", [P, FB], stack=st)
            hh = sbuf("hh", [P, FB], F32R, stack=st)
            hl = sbuf("hl", [P, FB], F32R, stack=st)
            ye = sbuf("ye", [P, D], stack=st)
            rti = sbuf("rti", [1, 16], I32, stack=st)
            wr = sbuf("wr", [P, KD * E], stack=st)
        with ExitStack() as st:
            ubT = sbuf("ubT", [P, KD, S], stack=st)
            kvn = sbuf("kvn", [P, M, 6 * NG * HD], stack=st)
            qn = sbuf("qn", [P, M, D], stack=st)
            tmp_a = sbuf("tmp_a", [P, D], stack=st)
            tmp_b = sbuf("tmp_b", [P, D], stack=st)
            xc = sbuf("xc", [P, CB * HD], stack=st)
            xcT = sbuf("xcT", [P, 2, 16, NG * NCMP], stack=st)
            h1T = sbuf("h1T", [P, 4, 64], stack=st)
            w2 = sbuf("w2", [P, 2, 2, HD], stack=st)
            cmpn = sbuf("cmpn", [P, 2, NG, HD], stack=st)
            kdup = sbuf("kdup", [P, M, 2, NG, 2, HD], stack=st)
            kcdup = sbuf("kcdup", [P, NG, 2, HD], stack=st)
            rope_g = sbuf("rope_g", [P, 5, 2, HD], stack=st)
            rope_k = sbuf("rope_k", [P, M, 2, 2, HD], stack=st)
            kT = sbuf("kT", [P, NG, KALL], stack=st)
            qT = sbuf("qT", [P, NH, S], stack=st)
            oT = sbuf("oT", [P, NH // 2, S], stack=st)
            diag = sbuf("diag", [P, 2, 3, P], stack=st)
            hidden_n = xc[0:NG * NCMP, 0:2 * CH]
            gate = sbuf("gate", [P, M, 3, NH], stack=st)
            pr = sbuf("pr", [P, 2, 528], stack=st)
            pT = sbuf("pT", [P, 2, 512], stack=st)
            pcT = sbuf("pcT", [P, 2, P], stack=st)
            stat = sbuf("stat", [P, 3, 16], stack=st)
        with ExitStack() as st:
            zf = sbuf("zf", [P, HH, S], stack=st)
            qh = sbuf("qh", [P, HH, S], stack=st)
            t1 = sbuf("t1", [P, HH, S], stack=st)
            t2 = sbuf("t2", [P, HH, S], stack=st)
            t3 = sbuf("t3", [P, HH, S], stack=st)
            kk = sbuf("kk", [P, HH, S], stack=st)
            bb = sbuf("bb", [P, HH, S], stack=st)
            keep = sbuf("keep", [P, HH, S], stack=st)
            sd = sbuf("sd", [P, HH, M, P], stack=st)
            sx = sbuf("sx", [P, HH, P], stack=st)
            skT = sbuf("skT", [P, 4, S], stack=st)
            sqT = sbuf("sqT", [P, 4, S], stack=st)
            hv = sbuf("hv", [P, M, 512], stack=st)
            sv = sbuf("sv", [P, M, 512], stack=st)
            hog = sbuf("hog", [P, M, 512], stack=st)
            sga = sbuf("sga", [P, M, D], stack=st)
            sgb = sbuf("sgb", [P, M, D], stack=st)
            oa = sbuf("oa", [P, M, 512], stack=st)
            oaT = sbuf("oaT", [P, 4, S], stack=st)
            obT = sbuf("obT", [P, 4, S], stack=st)
            e1 = sbuf("e1", [P, 2, 384], stack=st)
            sp = sbuf("sp", [P, 2, 384], stack=st)
            wt = sbuf("wt", [P, 2, 384], stack=st)
            lbt = sbuf("lbt", [P, 8, HH], stack=st)
            lmask = sbuf("lmask", [P, 8 * P], U8, stack=st)
            wmh = sbuf("wmh", [P, 2, KD, HW], F32R, stack=st)
            ul = sbuf("ul", [P, KD, S], F32R, stack=st)

        rt = uT[:, 3:6, :].rearrange("p a b -> p (a b)")
        R_, at = {}, 0
        for name, w in [("exp", M * E), ("logit", M * E), ("neg_max", M), ("sum", M), ("a64", E * E), ("b64", E * E),
                        ("rank", E), ("weight", M * E), ("pos", 3 * E), ("tiles", E), ("upto", E), ("before", E), ("ones", E),
                        ("owner", ITEMS * E), ("tmp", ITEMS * E), ("expert", ITEMS), ("first", ITEMS), ("there", ITEMS),
                        ("slot_of", M * ITEMS), ("weight_of", M * ITEMS), ("sel", M * E)]:
            R_[name] = rt[:, at:at + w]
            at += w
        slot_of, weight_of = (R_[k].rearrange("p (m i) -> p m i", m=M) for k in ("slot_of", "weight_of"))
        sel = R_["sel"].rearrange("p (m e) -> p m e", m=M)
        pick, pickw = uT[:, 0:1, :].rearrange("p a (m t) -> p (a m) t", m=M), uT[:, 1:2, :].rearrange("p a (m t) -> p (a m) t", m=M)
        pickT = uT[:, 2, :]

        ps = ctx.enter_context(nc.psum_tensor("ps", [P, 8, 512], F32))
        kv_scratch = nc.dram_tensor("kv_scratch", [S, 512], F32, kind="Internal").ap()

        slot_full = [sem(f"slot_full{s}") for s in range(3)]
        const_in = sem("const_in")
        rows_in = [sem(f"rows_in{i}") for i in range(2)]
        bc_in = sem("bc_in")
        x_in = sem("x_in")
        w2_in, masks_in, wr_in, ye_in, final_in = sem("w2_in"), sem("masks_in"), sem("wr_in"), sem("ye_in"), sem("final_in")
        q_zeroed, o_filled, o_read = sem("q_zeroed"), sem("o_filled"), sem("o_read")
        kvc_out, kvc_in = sem("kvc_out"), sem("kvc_in")
        stage = sem("stage")
        dve_order, act_order = sem("dve_order"), sem("act_order")
        v_filled, v_read = sem("v_filled"), sem("v_read")
        a_filled, a_read = sem("a_filled"), sem("a_read")
        s_filled, s_read = sem("s_filled"), sem("s_read")
        norm_sq, norm_ms, norm_rt, norm_xn = sem("norm_sq"), sem("norm_ms"), sem("norm_rt"), sem("norm_xn")
        norm_h, root_done = sem("norm_h"), sem("root_done")
        xr_ready, ri_ready, la_ready, a_ready = sem("xr_ready"), sem("ri_ready"), sem("la_ready"), sem("a_ready")
        lam_abs, lam_exp = sem("lam_abs"), sem("lam_exp")
        th_ready, t2_ready, sq_ready, yg_ready, yh_ready = (
            sem("th_ready"), sem("t2_ready"), sem("sq_ready"), sem("yg_ready"), sem("yh_ready"))
        kvn_ready, qn_ready, gate_ready, gated = sem("kvn_ready"), sem("qn_ready"), sem("gate_ready"), sem("gated")
        first_high, first_low = sem("first_high"), sem("first_low")
        pool_set, mh_ready, ml_ready, gates_on = sem("pool_set"), sem("mh_ready"), sem("ml_ready"), sem("gates_on")
        ms_ready, root_ready = sem("ms_ready"), sem("root_ready")
        k_ready, q_ready, kc_ready = sem("k_ready"), sem("q_ready"), sem("kc_ready")
        max_ready, diag_ready = sem("max_ready"), sem("diag_ready")
        lb_max, lb_exp, lb_clamped, lb_ln = sem("lb_max"), sem("lb_exp"), sem("lb_clamped"), sem("lb_ln")
        zabs_ready, zln_ready, zdif_ready, kk_ready = sem("zabs_ready"), sem("zln_ready"), sem("zdif_ready"), sem("kk_ready")
        fabs_ready, fln_ready, qh_ready = sem("fabs_ready"), sem("fln_ready"), sem("qh_ready")
        decay_ready, decay_exp, level_ready = sem("decay_ready"), sem("decay_exp"), sem("level_ready")
        oms_ready, ort_ready, oa_ready = sem("oms_ready"), sem("ort_ready"), sem("oa_ready")
        ln_ready, sp_ready, y_ready = sem("ln_ready"), sem("sp_ready"), sem("y_ready")
        sel_ready, lmax_ready, lexp_ready = sem("sel_ready"), sem("lmax_ready"), sem("lexp_ready")
        wh_full = [sem(f"wh_full{s}") for s in range(3)]
        wl_full = [sem(f"wl_full{s}") for s in range(3)]
        g_done, u_done, t_done, d_done = sem("g_done"), sem("u_done"), sem("t_done"), sem("d_done")
        sg_ready, h_ready, hh_ready, hl_ready, d_added = (
            sem("sg_ready"), sem("h_ready"), sem("hh_ready"), sem("hl_ready"), sem("d_added"))
        pick_ready, picked, xh_ready, xl_ready = sem("pick_ready"), sem("picked"), sem("xh_ready"), sem("xl_ready")
        pickT_done, pickT_ready, put_done, put_added = sem("pickT_done"), sem("pickT_ready"), sem("put_done"), sem("put_added")
        items_ready = sem("items_ready")
        out_ready, out_sent = sem("out_ready"), sem("out_sent")

        block = ctx.enter_context(nc.Block())

        marks = {}
        half_used = {}
        freed = {}

        class Side:

            def __init__(self, eng):
                self.eng, self.n, self.counts, self.norms = eng, 0, {}, 0
                self.v = Ring([0, 1, 2], v_filled, v_read)
                self.a = Ring([3, 4, 5], a_filled, a_read)
                self.s = Ring([6, 7], s_filled, s_read)
                self.sc = Ring([6, 0], s_filled, s_read)
                self.o = Ring([2], o_filled, o_read)
                self.v2 = Ring([0, 1], v_filled, v_read)

            def scores_begin(self):
                self.sc.n, self.sc.base = self.s.n, self.s.n

            def scores_end(self):
                self.s.n = self.sc.n

            def barrier(self, name):
                self.n += 1
                marks[name] = self.n
                self.eng.drain().then_inc(stage, 1)
                self.eng.wait_ge(stage, 3 * self.n)

            def see(self, s, by=1):
                self.counts[s.name] = self.counts.get(s.name, 0) + by
                self.eng.wait_ge(s, self.counts[s.name])

            def link(self, ins, order):
                self.counts["order"] = self.counts.get("order", 0) + 1
                ins.then_inc(order, 1)
                self.eng.wait_ge(order, self.counts["order"])

        def tile_view(key, k, w):
            return raw[:, plan[key][0], 0:k * w].rearrange("p (k n) -> p k n", k=k)

        def half_key(layer, q):
            return ("mix_in", layer, IN_ORDER[q // 2]) if q < Q_OUT else ("mix_out", layer, (q - Q_OUT) // 2)

        def half_view(layer, q, store=raw):
            s = plan[half_key(layer, q)][0]
            return store[:, s, :].rearrange("p (k n) -> p k n", k=KD)[:, :, (q % 2) * HW:(q % 2 + 1) * HW]

        def arrived(eng, key):
            s, f = plan[key]
            eng.wait_ge(slot_full[s], 16 * (f + 1))

        FFN = {"ffn0": (6, 256, 0, 0), "ffn1": (6, 256, 6, 12), "ffn2": (NBB, FB, 12, 24)}
        MOE_B, MOE_U = 12 + NBB, 24 + 2 * NBB

        def flat_view(a):
            names = " ".join("abcd"[:len(a.shape)])
            return a if len(a.shape) == 1 else a.rearrange(f"{names} -> ({names})")

        def load_rows(eng, g):
            at = 0
            for name, r in ROWS[g]:
                eng.dma_start(rowbuf[at:at + r, g, :], flat_view(A[name]).rearrange("(r q) -> r q", q=P)).then_inc(rows_in[g], 16)
                at += r

        @block.tensor
        def _(pe):
            me = Side(pe)
            mm, tr = nc.tensor.matmul, nc.tensor.transpose
            pe.wait_ge(const_in, 16)
            ident = C("ident")

            def columns(g):
                pe.wait_ge(rows_in[g], 16 * len(ROWS[g]))
                b = me.v.claim(pe)
                r = ROWS_USED[g]
                tr(ps[:, b, 0:r], rowbuf[0:r, g, :], const[0:r, 0:r]).then_inc(v_filled, 1)

            columns(0)

            def drained(ring):
                pe.wait_ge(ring.read, ring.n)

            def norm(split=False):
                src = x if split == "raw" else xn
                if src is xn:
                    me.see(norm_xn, M)
                for j in range(4):
                    ring = me.s if split else (me.v, me.a)[j % 2]
                    b = ring.claim(pe)
                    for kk in range(2):
                        for m in range(M):
                            t = tr(ps[:, b, (kk * M + m) * P:(kk * M + m + 1) * P],
                                   src[:, m, (2 * j + kk) * P:(2 * j + kk + 1) * P], ident)
                    t.then_inc(ring.filled, 1)
                for ring in ((me.s,) if split else (me.v, me.a)):
                    drained(ring)

            def released(key, ring):
                freed[key] = (ring.filled, ring.n)

            def product_T(ring, key, c, src):
                w = tile_view(key, KD, 512)
                b = ring.claim(pe)
                for k in range(KD):
                    t = mm(ps[:, b, 0:S], w[:, k, c * P:(c + 1) * P], src[:, k, :], start=(k == 0), stop=(k == KD - 1))
                t.then_inc(ring.filled, 1)

            def product(ring, key, m, src, w=512, kc=KD, c0=0):
                wv = tile_view(key, kc, max(w, D) if kc == 4 else w)
                b = ring.claim(pe)
                for k in range(kc):
                    t = mm(ps[:, b, 0:w], src[:, k, m * P:(m + 1) * P], wv[:, k, c0:c0 + w], start=(k == 0), stop=(k == kc - 1))
                t.then_inc(ring.filled, 1)

            norm()
            columns(1)
            for t in (2, 3):
                arrived(pe, ("a_in", t))
                for c in range(4):
                    product_T(me.v, ("a_in", t), c, uT)
                released(("a_in", t), me.v)
            arrived(pe, ("a_gate",))
            gw = tile_view(("a_gate",), 16, P)
            for f in range(KD):
                me.see(xr_ready)
                b = me.a.claim(pe)
                for i in range(2):
                    t = mm(ps[:, b, i * S:(i + 1) * S], gw[:, i * KD + f, :], xr[:, f, :], start=True, stop=True)
                t.then_inc(a_filled, 1)
            released(("a_gate",), me.a)
            for t in (0, 1):
                arrived(pe, ("a_in", t))
                for c in range(4):
                    product_T(me.a, ("a_in", t), c, uT)
                released(("a_in", t), me.a)
            me.see(yh_ready)
            for t in range(2):
                arrived(pe, ("a_out", t))
                for m in range(M):
                    product(me.v, ("a_out", t), m, rg)
                released(("a_out", t), me.v)
            drained(me.v)

            def ffn_steps(ns):
                def wait(s, v):
                    if not (isinstance(v, int) and v <= 0):
                        pe.wait_ge(s, v)

                def split_product(bank, kind, xa, xb, k, B, w, last, c0=0, n=None):
                    a = wh[:, kind, k * w + c0:k * w + c0 + n]
                    l = wl[:, kind, k * w + c0:k * w + c0 + n]
                    mm(ps[:, bank, 0:n], xa, a, start=(k == 0), stop=False)
                    mm(ps[:, bank, 0:n], xa, l, start=False, stop=False)
                    return mm(ps[:, bank, 0:n], xb, a, start=False, stop=(k == last))

                def gate_up(kind, B, u, m, w, parts=False):
                    if parts:
                        me.see(first_low)
                    else:
                        pe.wait_ge(wh_full[kind], B + 1)
                        pe.wait_ge(wl_full[kind], B + 1)
                    wait(sg_ready if kind == 0 else h_ready, u)
                    for k in range(KD):
                        if parts and k == KD // 2:
                            pe.wait_ge(wh_full[kind], B + 1)
                            pe.wait_ge(wl_full[kind], B + 1)
                        t = split_product(kind, kind, xh[:, k, m * P:(m + 1) * P], xl[:, k, m * P:(m + 1) * P],
                                          k, B, w, KD - 1, 0, w)
                    t.then_inc(g_done if kind == 0 else u_done, 1)

                def turn(u, w):
                    pe.wait_ge(h_ready, u + 1)
                    wait(hl_ready, u)
                    for c in range(w // P):
                        t = tr(ps[:, 2, c * P:(c + 1) * P], hb[:, c * P:(c + 1) * P], ident)
                    t.then_inc(t_done, 1)

                def down(B, u, w):
                    pe.wait_ge(wh_full[2], B + 1)
                    pe.wait_ge(wl_full[2], B + 1)
                    pe.wait_ge(hh_ready, u + 1)
                    pe.wait_ge(hl_ready, u + 1)
                    wait(d_added, u)
                    for half in range(2):
                        for c in range(w // P):
                            t = split_product(3 + half, 2, hh[:, c * P:(c + 1) * P], hl[:, c * P:(c + 1) * P],
                                              c, B, D, w // P - 1, half * FB, FB)
                    t.then_inc(d_done, 1)
                return gate_up, turn, down

            gate_up, turn, down = ffn_steps(None)

            def ffn(name):
                nb, wlast, B0, U0 = FFN[name]
                norm(split="raw")

                def body(b, w, first=False):
                    for m in range(M):
                        u = b * M + (U0 + m)
                        gate_up(0, b + B0, u, m, w, parts=first and m == 0)
                        if not (first and m == 0):
                            turn(u - 1, w if m else FB)
                        gate_up(1, b + B0, u, m, w)
                        if not (first and m == 0):
                            down(b + (B0 if m else B0 - 1), u - 1, w if m else FB)

                body(0, FB, first=True)
                with pe.Fori(1, nb - 1) as b:
                    body(b, FB)
                body(nb - 1, wlast)
                u = U0 + nb * M - 1
                turn(u, wlast)
                down(B0 + nb - 1, u, wlast)
                pe.wait_ge(d_added, u + 1)

            me.barrier("ffn0")
            ffn("ffn0")

            me.barrier("nsa")
            norm()
            for t in range(3):
                arrived(pe, ("kv", t))
                product(me.v, ("kv", t), 0, uT)
                product(me.a, ("kv", t), 1, uT)
                released(("kv", t), me.a)
            for t in range(2):
                arrived(pe, ("b_in", t))
                product(me.v, ("b_in", t), 0, ubT)
                product(me.a, ("b_in", t), 1, ubT)
                released(("b_in", t), me.a)
            arrived(pe, ("b_in", 2))
            for m in range(M):
                product(me.v, ("b_in", 2), m, ubT, w=3 * NH)
            released(("b_in", 2), me.v)
            pe.wait_ge(kvc_in, 16 * 2 * 2 * NG)
            R = 2 * NG * NCMP
            for j in range(4):
                b = me.v.claim(pe)
                for i in range(4):
                    t = tr(ps[:, b, i * R:(i + 1) * R], xc[0:R, (4 * j + i) * P:(4 * j + i + 1) * P], const[0:R, 0:R])
                t.then_inc(v_filled, 1)
            drained(me.v)
            b = me.a.claim(pe)
            for kv in range(2):
                arrived(pe, ("cmp", kv))
                w1 = tile_view(("cmp", kv), 16, CH)
                for l in range(16):
                    t = mm(ps[0:NG * NCMP, b, kv * CH:(kv + 1) * CH], xcT[:, kv, l, :], w1[:, l, :],
                           start=(l == 0), stop=(l == 15))
            t.then_inc(a_filled, 1)
            released(("cmp", 0), me.a)
            released(("cmp", 1), me.a)
            hidden_at = me.a.n
            me.see(k_ready)
            for m in range(M):
                for w in range(2):
                    b = me.a.claim(pe)
                    for g in range(NG):
                        t = tr(ps[:, b, g * P:(g + 1) * P], kdup[:, m, w, g, :, :].rearrange("p a d -> p (a d)"), ident)
                    t.then_inc(a_filled, 1)
            pe.wait_ge(a_read, hidden_at)
            b = me.a.claim(pe)
            for j in range(4):
                t = tr(ps[:, b, j * 64:j * 64 + NG * NCMP], hidden_n[:, j * P:(j + 1) * P], const[0:NG * NCMP, 0:NG * NCMP])
            t.then_inc(a_filled, 1)
            drained(me.a)
            pe.wait_ge(w2_in, 16)
            b = me.v.claim(pe)
            for kv in range(2):
                for g in range(NG):
                    for hc in range(2):
                        t = mm(ps[0:NCMP, b, (kv * NG + g) * HD:(kv * NG + g + 1) * HD],
                               h1T[:, kv * 2 + hc, g * NCMP:(g + 1) * NCMP], w2[:, kv, hc, :], start=(hc == 0), stop=(hc == 1))
            t.then_inc(v_filled, 1)
            for m in range(M):
                me.see(q_ready)
                for j in range(2):
                    b = me.a.claim(pe)
                    for i in range(4):
                        t = tr(ps[:, b, i * P:(i + 1) * P], qn[:, m, (4 * j + i) * P:(4 * j + i + 1) * P], ident)
                    t.then_inc(a_filled, 1)
            me.see(kc_ready)
            b = me.v.claim(pe)
            for g in range(NG):
                t = tr(ps[:, b, g * 16:g * 16 + NCMP], kcdup[0:NCMP, g, :, :].rearrange("p a d -> p (a d)"),
                       const[0:NCMP, 0:NCMP])
            t.then_inc(v_filled, 1)
            drained(me.v)
            drained(me.a)

            def scores(m, h):
                g, nk = h // HPG, P * (m + 1)
                q = qT[:, h, m * P:(m + 1) * P]
                b = me.sc.claim(pe)
                mm(ps[:, b, 0:NCMP + nk], q, kT[:, g, 0:NCMP + nk], start=True, stop=False)
                mm(ps[:, b, 0:NCMP + nk], ident, C(f"neg_keys{m}"), start=False, stop=True)
                mm(ps[:, b + 1, 0:nk], q, kT[:, g, NCMP + S:NCMP + S + nk], start=True, stop=False)
                mm(ps[:, b + 1, m * P:nk], ident, C("neg_causal"), start=False, stop=True).then_inc(s_filled, 1)

            turned_at = {}

            def turn_probs(i, m, h):
                nb = m + 1
                me.see(diag_ready)
                b = me.a.claim(pe)
                for w in range(2):
                    for kb in range(nb):
                        c0 = NCMP + w * S + kb * P
                        t = mm(ps[:, b, (w * nb + kb) * P:(w * nb + kb + 1) * P], pr[:, i % 2, c0:c0 + P],
                               diag[:, i % 2, 1 + w, :], start=True, stop=True)
                t.then_inc(a_filled, 1)
                b = me.a.claim(pe)
                mm(ps[0:NCMP, b, 0:P], pr[:, i % 2, 0:NCMP], diag[:, i % 2, 0, :], start=True, stop=True).then_inc(a_filled, 1)
                turned_at[i] = me.a.n

            def values(i, m, h):
                g, nb, p0 = h // HPG, m + 1, HD * (h % 2)
                pe.wait_ge(a_read, turned_at[i])
                b = me.o.claim(pe) if h % 2 == 0 else me.o.banks[0]
                o = ps[p0:p0 + HD, b, 0:P]
                for w in range(2):
                    for kb in range(nb):
                        mm(o, kvn[:, kb, (2 * w + 3) * 256 + g * HD:(2 * w + 3) * 256 + (g + 1) * HD],
                           pT[:, i % 2, (w * nb + kb) * P:(w * nb + kb + 1) * P], start=(w == 0 and kb == 0), stop=False)
                t = mm(o, cmpn[0:NCMP, 1, g, :], pcT[0:NCMP, i % 2, :], start=False, stop=True)
                if h % 2:
                    t.then_inc(o_filled, 1)

            me.scores_begin()
            pe.wait_ge(q_zeroed, 1)
            pairs = [(m, h) for m in range(M) for h in range(NH)]
            scores(*pairs[0])
            for i, pair in enumerate(pairs):
                if i + 1 < len(pairs):
                    scores(*pairs[i + 1])
                turn_probs(i, *pair)
                if i:
                    values(i - 1, *pairs[i - 1])
            values(i, *pair)
            drained(me.o)
            me.scores_end()
            for t in range(2):
                arrived(pe, ("b_out", t))
                for m in range(M):
                    product(me.v, ("b_out", t), m, oT)
                released(("b_out", t), me.v)
            drained(me.v)

            me.barrier("ffn1")
            ffn("ffn1")

            def level_product(lv):
                me.see(level_ready)
                if lv == 128:
                    b = me.v2.claim(pe)
                    for h in range(HH):
                        t = mm(ps[:, b, h * P:(h + 1) * P], t2[:, h, 0:P], t2[:, h, P:S], start=True, stop=True)
                    t.then_inc(v_filled, 1)
                    return
                ks, qs = (kk, qh) if lv == 0 else (t2, t2)
                for hp in range(2):
                    b = me.v2.claim(pe)
                    for a in range(2):
                        for m in range(M):
                            t = mm(ps[:, b, (a * M + m) * P:(a * M + m + 1) * P], ks[:, 2 * hp + a, m * P:(m + 1) * P],
                                   qs[:, 2 * hp + a, m * P:(m + 1) * P], start=True, stop=True)
                    t.then_inc(v_filled, 1)

            def sb_z(b, h, stop=True):
                p0, hp = HD * (h % 2), h // 2
                mm(ps[:, b, 0:S], skT[p0:p0 + HD, hp, 0:P], sqT[p0:p0 + HD, hp, :], start=True, stop=stop)

            def sb_z1(b, h, stop=True):
                p0, hp = HD * (h % 2), h // 2
                return mm(ps[:, b, S:S + P], skT[p0:p0 + HD, hp, P:S], sqT[p0:p0 + HD, hp, P:S], start=True, stop=stop)

            def mixer(layer):
                norm(split="normalised")
                tiles = {t: ("mix_in", layer, t) for t in range(11)}

                def parts(q):
                    me.see(mh_ready)
                    me.see(ml_ready)
                    return wmh[:, q % 2], half_view(layer, q, raw_low)

                def half_T(ring, q):
                    wh_, wl_ = parts(q)
                    for c in range(HW // P):
                        b = ring.claim(pe)
                        for k in range(KD):
                            o, cs = ps[:, b, 0:S], slice(c * P, (c + 1) * P)
                            mm(o, wh_[:, k, cs], uh[:, k, :], start=(k == 0), stop=False)
                            mm(o, wh_[:, k, cs], ul[:, k, :], start=False, stop=False)
                            t = mm(o, wl_[:, k, cs], uh[:, k, :], start=False, stop=(k == KD - 1))
                        t.then_inc(ring.filled, 1)
                    half_used[layer, q] = (ring.filled, ring.n)

                def half_natural(ring, q):
                    wh_, wl_ = parts(q)
                    b = ring.claim(pe)
                    for m in range(M):
                        for k in range(KD):
                            o, ms = ps[:, b, m * HW:(m + 1) * HW], slice(m * P, (m + 1) * P)
                            mm(o, uh[:, k, ms], wh_[:, k, :], start=(k == 0), stop=False)
                            mm(o, uh[:, k, ms], wl_[:, k, :], start=False, stop=False)
                            t = mm(o, ul[:, k, ms], wh_[:, k, :], start=False, stop=(k == KD - 1))
                    t.then_inc(ring.filled, 1)
                    half_used[layer, q] = (ring.filled, ring.n)

                q = 0
                for t, ring in ((1, me.v), (0, me.a), (5, me.v), (4, me.a)):
                    for _ in range(2):
                        half_T(ring, q)
                        q += 1
                    released(tiles[t], ring)
                drained(me.v)
                me.v2.n = me.v.n

                def sb_scores(h):
                    b = me.s.claim(pe)
                    sb_z(b, h)
                    sb_z1(b, h).then_inc(s_filled, 1)

                kept_at = {}

                def sb_keep(h):
                    me.see(sp_ready)
                    spb = sp[:, h % 2, :]
                    b = me.a.claim(pe)
                    sb_z(b, h, stop=False)
                    mm(ps[:, b, 0:S], C("minus_from"), spb[:, 0:S], start=False, stop=False)
                    mm(ps[:, b, P:S], C("minus_one"), spb[:, S:S + P], start=False, stop=False)
                    mm(ps[:, b, 0:P], ident, C("neg_not_before"), start=False, stop=True)
                    sb_z1(b, h, stop=False)
                    mm(ps[:, b, S:S + P], C("minus_from"), spb[:, S:S + P], start=False, stop=False)
                    mm(ps[:, b, S:S + P], ident, C("neg_not_before"), start=False, stop=True).then_inc(a_filled, 1)
                    kept_at[h] = me.a.n

                def sb_values(h):
                    pe.wait_ge(a_read, kept_at[h])
                    b = me.o.claim(pe) if h % 2 == 0 else me.o.banks[0]
                    p0 = HD * (h % 2)
                    mm(ps[p0:p0 + HD, b, 0:S], sv[:, 0, h * HD:(h + 1) * HD], wt[:, h % 2, 0:S], start=True, stop=False)
                    t = mm(ps[p0:p0 + HD, b, P:S], sv[:, 1, h * HD:(h + 1) * HD], wt[:, h % 2, S:S + P], start=False, stop=True)
                    if h % 2:
                        t.then_inc(o_filled, 1)

                for i in range(HALVES):
                    j, c = divmod(i, 2)
                    half_natural(me.a, 8 + i)
                    if c == 1:
                        released(tiles[REST[j]], me.a)
                    h = HEAD_AT.get(i, SH if i > 11 else -1)
                    if i == min(HEAD_AT) - 1:
                        drained(me.a)
                        sb_scores(0)
                    if h >= 0 and i <= max(HEAD_AT) + 1:
                        if h + 1 < SH:
                            sb_scores(h + 1)
                        if h < SH:
                            sb_keep(h)
                        if h:
                            sb_values(h - 1)
                    if i in LEVEL_AT:
                        level_product(LEVEL_AT[i])
                drained(me.v2)
                drained(me.a)
                drained(me.o)
                me.v.n = me.v2.n
                arrived(pe, ("branch", layer, 1))

                def branch_b(m, half):
                    product(me.v, ("branch", layer, 1), m, obT, w=512, kc=4, c0=half * 512)

                branch_b(0, 0)
                for m in range(M):
                    b = me.v.claim(pe)
                    for h in range(HH):
                        o = ps[:, b, h * P:(h + 1) * P]
                        t = mm(o, sd[:, h, m, :], hv[:, m, h * P:(h + 1) * P], start=True, stop=(m == 0))
                        if m:
                            t = mm(o, sx[:, h, :], hv[:, 0, h * P:(h + 1) * P], start=False, stop=True)
                    t.then_inc(v_filled, 1)
                branch_b(0, 1)
                branch_b(1, 0)
                branch_b(1, 1)
                released(("branch", layer, 1), me.v)
                me.see(oa_ready)
                for m in range(M):
                    b = me.a.claim(pe)
                    for k in range(4):
                        t = tr(ps[:, b, k * P:(k + 1) * P], oa[:, m, k * P:(k + 1) * P], ident)
                    t.then_inc(a_filled, 1)
                drained(me.a)
                arrived(pe, ("branch", layer, 0))

                def turn_sum(half):
                    me.see(y_ready, M)
                    for j in (2 * half, 2 * half + 1):
                        b = me.s.claim(pe)
                        for kk_ in range(2):
                            for m in range(M):
                                k = 2 * j + kk_
                                t = tr(ps[:, b, (kk_ * M + m) * P:(kk_ * M + m + 1) * P], sga[:, m, k * P:(k + 1) * P], ident)
                        t.then_inc(s_filled, 1)

                for half in range(2):
                    for m in range(M):
                        product(me.v, ("branch", layer, 0), m, oaT, w=512, kc=4, c0=half * 512)
                        if (half, m) == (1, 0):
                            turn_sum(0)
                released(("branch", layer, 0), me.v)
                turn_sum(1)
                drained(me.s)
                for t in range(2):
                    for c in range(2):
                        half_natural(me.v, Q_OUT + 2 * t + c)
                    released(("mix_out", layer, t), me.v)
                drained(me.v)

            me.barrier("mix0")
            mixer(0)
            me.barrier("ffn2")
            ffn("ffn2")
            me.barrier("mix1")
            mixer(1)

            me.barrier("moe")
            norm()
            marks["moe_turned"] = me.a.n
            pe.wait_ge(wr_in, 16)
            b = me.v.claim(pe)
            for m in range(M):
                for k in range(KD):
                    t = mm(ps[:, b, m * E:(m + 1) * E], uT[:, k, m * P:(m + 1) * P], wr[:, k * E:(k + 1) * E],
                           start=(k == 0), stop=(k == KD - 1))
            t.then_inc(v_filled, 1)
            me.see(sel_ready)
            b = me.v.claim(pe)
            mm(ps[:, b, 0:E], C("before"), sel[:, 0, :], start=True, stop=True)
            mm(ps[:, b, E:2 * E], C("before"), sel[:, 1, :], start=True, stop=False)
            mm(ps[:, b, E:2 * E], C("one"), sel[:, 0, :], start=False, stop=True)
            mm(ps[:, b, 2 * E:3 * E], C("one"), sel[:, 0, :], start=True, stop=False)
            mm(ps[:, b, 2 * E:3 * E], C("one"), sel[:, 1, :], start=False, stop=True).then_inc(v_filled, 1)
            pe.wait_ge(items_ready, 1)
            n = pe.value_load(rti[0:1, 0:1], min_val=MIN_ITEMS, max_val=ITEMS)

            def gather():
                for k in range(KD):
                    o = ps[:, 5 + k // 4, (k % 4) * P:(k % 4 + 1) * P]
                    mm(o, xn[:, 0, k * P:(k + 1) * P], pick[:, 0, :], start=True, stop=False)
                    t = mm(o, xn[:, 1, k * P:(k + 1) * P], pick[:, 1, :], start=False, stop=True)
                t.then_inc(picked, 1)

            def turn_weighted():
                for m in range(M):
                    t = tr(ps[:, 7, m * P:(m + 1) * P], pickw[:, m, :], ident)
                t.then_inc(pickT_done, 1)

            def give_back(it, u):
                pe.wait_ge(pickT_ready, it + 1)
                pe.wait_ge(d_added, u)
                pe.wait_ge(hl_ready, u + 1)
                for m in range(M):
                    for half in range(2):
                        t = mm(ps[:, GIVE_BANKS[2 * m + half], :], pickT[:, m * P:(m + 1) * P],
                               ye[:, half * FB:(half + 1) * FB], start=True, stop=True)
                t.then_inc(put_done, 1)

            def step(B, u, before_turn=None, mid=None, before_down=None):
                gate_up(0, B, u, 0, FB)
                if before_turn:
                    before_turn()
                turn(u - 1, FB)
                if mid:
                    mid()
                gate_up(1, B, u, 0, FB)
                if before_down:
                    before_down()
                down(B - 1, u - 1, FB)

            def item(it, last=False):
                B, U = it * NBB + MOE_B, it * NBB + MOE_U
                step(B + 1, U + 1, before_down=lambda: give_back(it, U))
                with pe.Fori(2, NBB - 1) as b:
                    step(B + b, U + b, before_turn=lambda: pe.wait_ge(put_added, it + 1))

                def pass_on():
                    pe.wait_ge(pick_ready, it + 2)
                    turn_weighted()
                    if not last:
                        gather()

                step(B + (NBB - 1), U + (NBB - 1), mid=pass_on)
                if last:
                    turn(U + (NBB - 1), FB)
                    down(B + (NBB - 1), U + (NBB - 1), FB)
                    pe.wait_ge(d_added, U + NBB)
                    give_back(it + 1, U + (NBB - 1))
                else:
                    pe.wait_ge(xh_ready, it + 2)
                    pe.wait_ge(xl_ready, it + 2)
                    step(B + NBB, U + NBB)

            pe.wait_ge(pick_ready, 1)
            gather()
            pe.wait_ge(xh_ready, 1)
            pe.wait_ge(xl_ready, 1)
            gate_up(0, MOE_B, MOE_U, 0, FB)
            gate_up(1, MOE_B, MOE_U, 0, FB)
            with pe.Fori(0, n - 1) as it:
                item(it)
            item(n - 1, last=True)
            me.barrier("final")

        @block.scalar
        def _(act):
            me = Side(act)
            fn = nc.scalar.activation
            link = lambda ins: me.link(ins, act_order)
            load_rows(act, 0)
            act.wait_ge(x_in, 16)

            def high_parts(g, off):
                for j in range(4):
                    b = me.s.take(act)
                    for kk_ in range(2):
                        k = 2 * j + kk_
                        dst = xh[:, k, :] if g != "mix_norm_2" else uh[:, k, :]
                        t = fn(dst, ps[:, b, kk_ * S:(kk_ + 1) * S], ACT.Copy, scale=col(g, off + k))
                    t.then_inc(norm_h, 1)

            def norm(g=None, ready=None):
                for m in range(M):
                    fn(xn[:, m, :], x[:, m, :], ACT.Square, accum_out=small[:, m:m + 1]).then_inc(norm_sq, 1)
                me.see(norm_ms)
                fn(small[:, 4:6], small[:, 2:4], ACT.Sqrt).then_inc(norm_rt, 1)
                if g is None:
                    return
                if ready:
                    ready()
                for j in (1, 3):
                    b = me.a.take(act)
                    for kk_ in range(2):
                        k = 2 * j + kk_
                        for dst, name, off in g:
                            t = fn(dst[:, k, :], ps[:, b, kk_ * S:(kk_ + 1) * S], ACT.Copy, scale=col(name, off + k))
                    t.then_inc(a_read, 1)

            norm([(uT, "a_norm", 0)], ready=lambda: act.wait_ge(v_read, 1))
            me.see(lam_abs)
            fn(lam[:, 1, :], lam[:, 0, :], ACT.Exp, scale=-1.0).then_inc(lam_exp, 1)
            for f in range(KD):
                b = me.a.take(act)
                fn(rg[:, f, :], ps[:, b, 0:S], ACT.Sigmoid, bias=col("a_gate_b", f))
                link(fn(ig[:, f, :], ps[:, b, S:2 * S], ACT.Sigmoid, bias=col("a_gate_b", KD + f)))
                act.nop().then_inc(a_read, 1)
            act.nop().then_inc(ri_ready, 1)
            me.see(la_ready)
            fn(aa[:], rg[:], ACT.Exp).then_inc(a_ready, 1)
            fn(th[:], rg[:], ACT.Tanh).then_inc(th_ready, 1)
            me.see(t2_ready)
            fn(th[:], th[:], ACT.Sqrt, scale=-1.0).then_inc(sq_ready, 1)
            for f in range(KD):
                b = me.a.take(act)
                fn(yg[:, f, :], ps[:, b, 0:S], ACT.Gelu_apprx_tanh).then_inc(a_read, 1)
            act.wait_ge(a_read, me.a.n)
            act.nop().then_inc(yg_ready, 1)

            def wait(s, v):
                if not (isinstance(v, int) and v <= 0):
                    act.wait_ge(s, v)

            users = [g_done, u_done, d_done]

            def high(name, kind, b, U, n):
                s, f = plan[name][kind]
                act.wait_ge(slot_full[s], (b + (f + 1)) * 16)
                wait(users[kind], U)
                fn(wh[:, kind, 0:n], raw[:, s, 0:n], ACT.Copy).then_inc(wh_full[kind], 1)

            def arrived_first(name, kind):
                s, f = plan[name][kind]
                act.wait_ge(slot_full[s], 16 * (f + 1))

            def silu(u, w, root=1.0):
                act.wait_ge(g_done, u + 1)
                wait(h_ready, u)
                fn(sg[:, 0:w], ps[:, 0, 0:w], ACT.Silu, scale=root).then_inc(sg_ready, 1)

            def high_h(u, w):
                act.wait_ge(t_done, u + 1)
                wait(d_done, u)
                fn(hh[:, 0:w], ps[:, 2, 0:w], ACT.Copy).then_inc(hh_ready, 1)

            def ffn(name, g, off):
                nb, wlast, B0, U0 = FFN[name]
                high_parts(g, off)
                arrived_first(name, 0)
                wait(users[0], U0)
                n = SLOT // 2
                fn(wh[:, 0, 0:n], raw[:, plan[name][0][0], 0:n], ACT.Copy).then_inc(first_high, 1)
                fn(wh[:, 0, n:], raw[:, plan[name][0][0], n:], ACT.Copy).then_inc(wh_full[0], 1)
                high(name, 1, 0, U0, SLOT)
                for m in range(M):
                    fn(xn[:, m, :], x[:, m, :], ACT.Square, accum_out=small[:, m:m + 1]).then_inc(norm_sq, 1)
                me.see(norm_ms)
                fn(small[:, 4:6], small[:, 2:4], ACT.Sqrt).then_inc(norm_rt, 1)
                me.see(root_done)

                def body(b, w, first=False, last=False, wn=FB):
                    u = b * M + U0
                    silu(u, w, small[:, 6:7])
                    if not first:
                        high_h(u - 1, FB)
                    high(name, 2, b, u, w // P * D)
                    silu(u + 1, w, small[:, 7:8])
                    high_h(u, w)
                    if not last:
                        high(name, 0, b + 1, u + 2, KD * wn)
                        high(name, 1, b + 1, u + 2, KD * wn)

                body(0, FB, first=True)
                with act.Fori(1, nb - 2) as b:
                    body(b, FB)
                body(nb - 2, FB, wn=wlast)
                body(nb - 1, wlast, last=True)
                high_h(U0 + nb * M - 1, wlast)

            me.barrier("ffn0")
            ffn("ffn0", "f_norm", 0)

            me.barrier("nsa")
            norm([(uT, "kv_norm", 0), (ubT, "b_norm", 0)])
            for t in range(3):
                b = me.a.take(act)
                fn(kvn[:, 1, t * 512:(t + 1) * 512], ps[:, b, :], ACT.Copy).then_inc(a_read, 1)
                if t == 0:
                    marks["kvc_a"] = me.a.n
                if t == 2:
                    act.wait_ge(a_read, me.a.n)
                    act.nop().then_inc(kvn_ready, 1)
            def root(n, rows=P):
                me.see(ms_ready)
                fn(stat[0:rows, 1, 0:n], stat[0:rows, 0, 0:n], ACT.Sqrt).then_inc(root_ready, 1)
            for _ in range(2 * M):
                root(NG)
            for t in range(2):
                b = me.a.take(act)
                fn(qn[:, 1, t * 512:(t + 1) * 512], ps[:, b, :], ACT.Copy).then_inc(a_read, 1)
            act.wait_ge(a_read, me.a.n)
            act.nop().then_inc(qn_ready, 1)
            for m in range(M):
                root(NH)
            b = me.a.take(act)
            fn(hidden_n, ps[0:NG * NCMP, b, :], ACT.Copy).then_inc(a_read, 1)
            me.see(gate_ready)
            fn(gate[:], gate[:], ACT.Sigmoid).then_inc(gated, 1)
            act.wait_ge(q_zeroed, 1)
            for m in range(M):
                for w in range(2):
                    b = me.a.take(act)
                    c0 = NCMP + w * S + m * P
                    fn(kT[:, :, c0:c0 + P], ps[:, b, :].rearrange("p (g t) -> p g t", g=NG), ACT.Copy).then_inc(a_read, 1)
            b = me.a.take(act)
            for j in range(4):
                t = fn(h1T[:, j, 0:NG * NCMP], ps[:, b, j * 64:j * 64 + NG * NCMP], ACT.Gelu_apprx_tanh, bias=col("cmp_b1", j))
            t.then_inc(a_read, 1)
            for m in range(M):
                for j in range(2):
                    b = me.a.take(act)
                    for p0 in (0, HD):
                        heads = qT[p0:p0 + HD, 8 * j:8 * j + 8, m * P:(m + 1) * P].rearrange("p (c a) t -> p c a t", a=2)
                        t = fn(heads[:, :, p0 // HD, :], ps[p0:p0 + HD, b, :].rearrange("p (c t) -> p c t", c=4), ACT.Copy)
                    t.then_inc(a_read, 1)
                    if m == 0 and j == 0:
                        root(NG, NCMP)

            def probs(i, m, h):
                nk, st_ = P * (m + 1), stat[:, i % 3, :]
                b = me.sc.take(act)
                me.see(max_ready)
                for j, (bank, c0, n, d0) in enumerate([(b, 0, NCMP, 0), (b, NCMP, nk, NCMP), (b + 1, 0, nk, NCMP + S)]):
                    t = fn(pr[:, i % 2, d0:d0 + n], ps[:, bank, c0:c0 + n], ACT.Exp, bias=st_[:, 3 + j:4 + j], scale=SCALE,
                           accum_out=st_[:, 6 + j:7 + j])
                t.then_inc(s_read, 1)

            def turned(i, m):
                b = me.a.take(act)
                n = 2 * (m + 1) * P
                fn(pT[:, i % 2, 0:n], ps[:, b, 0:n], ACT.Copy).then_inc(a_read, 1)
                b = me.a.take(act)
                fn(pcT[0:NCMP, i % 2, :], ps[0:NCMP, b, 0:P], ACT.Copy).then_inc(a_read, 1)

            pairs = [(m, h) for m in range(M) for h in range(NH)]
            me.scores_begin()
            probs(0, *pairs[0])
            for i, (m, h) in enumerate(pairs):
                if i + 1 < len(pairs):
                    probs(i + 1, *pairs[i + 1])
                turned(i, m)
            me.scores_end()

            me.barrier("ffn1")
            ffn("ffn1", "f_norm", KD)

            def mixer(layer):
                def high_half(q):
                    arrived(act, half_key(layer, q))
                    if q >= 2:
                        act.wait_ge(*half_used[layer, q - 2])
                    fn(wmh[:, q % 2], half_view(layer, q), ACT.Copy).then_inc(mh_ready, 1)

                norm()
                high_half(0)
                high_parts("mix_norm_2", layer * KD)
                high_half(1)
                me.see(lb_max)
                fn(lbt[:, 1:3, :], lbt[:, 1:3, :], ACT.Exp).then_inc(lb_exp, 1)
                me.see(lb_clamped)
                fn(lbt[:, 5:7, :], lbt[:, 5:7, :], ACT.Ln).then_inc(lb_ln, 1)
                high_half(2)
                high_half(3)
                for c in range(4):
                    b = me.a.take(act)
                    fn(qh[:, c, :], ps[:, b, 0:S], ACT.Silu).then_inc(a_read, 1)
                    if c % 2:
                        high_half(4 + c // 2)
                act.wait_ge(a_read, me.a.n)
                act.nop().then_inc(qh_ready, 1)
                me.see(zabs_ready)
                link(fn(t1[:], t1[:], ACT.Exp))
                fn(t2[:], t1[:], ACT.Ln, bias=1.0).then_inc(zln_ready, 1)
                high_half(6)
                me.see(zdif_ready)
                fn(kk[:], t1[:], ACT.Exp).then_inc(kk_ready, 1)
                high_half(7)
                me.see(fabs_ready)
                link(fn(t2[:], t2[:], ACT.Exp))
                fn(t2[:], t2[:], ACT.Ln, bias=1.0).then_inc(fln_ready, 1)
                for c in range(4):
                    b = me.a.take(act)
                    fn(sqT[:, c, :], ps[:, b, 0:S], ACT.Copy, scale=HD ** -0.5).then_inc(a_read, 1)
                    if c % 2:
                        high_half(8 + c // 2)
                dests = [(hv, 0), (sv, 0), (hog, 0), (sga, 0), (sga, 512), (sgb, 0), (sgb, 512)]

                def soft(h):
                    b = me.s.take(act)
                    link(fn(e1[:, h % 2, :], ps[:, b, 0:384], ACT.Abs))
                    link(fn(e1[:, h % 2, :], e1[:, h % 2, :], ACT.Exp, scale=-1.0))
                    fn(e1[:, h % 2, :], e1[:, h % 2, :], ACT.Ln, bias=1.0).then_inc(ln_ready, 1)

                def weights(h):
                    b = me.a.take(act)
                    fn(wt[:, h % 2, :], ps[:, b, 0:384], ACT.Exp).then_inc(a_read, 1)

                for i in range(HALVES):
                    j, c = divmod(i, 2)
                    if LEVEL_AT.get(i):
                        me.see(decay_ready)
                        fn(t1[:], t1[:], ACT.Exp).then_inc(decay_exp, 1)
                    dst, c0 = dests[j]
                    b = me.a.take(act)
                    fn(dst[:, :, c0 + c * HW:c0 + (c + 1) * HW], ps[:, b, :].rearrange("p (m n) -> p m n", m=M),
                       ACT.Copy).then_inc(a_read, 1)
                    if 10 + i < Q_OUT:
                        high_half(10 + i)
                    if i == min(HEAD_AT) - 1:
                        soft(0)
                    if i in HEAD_AT:
                        h = HEAD_AT[i]
                        if h + 1 < SH:
                            soft(h + 1)
                        weights(h)
                act.wait_ge(a_read, me.a.n)
                for gate_, f in ((sgb, ACT.Sigmoid), (sga, ACT.Sigmoid), (hog, ACT.Silu)):
                    fn(gate_[:], gate_[:], f).then_inc(gates_on, 1)
                me.see(oms_ready)
                fn(small[:, 24:32], small[:, 16:24], ACT.Sqrt).then_inc(ort_ready, 1)
                high_half(Q_OUT)
                high_half(Q_OUT + 1)
                for m in range(M):
                    b = me.a.take(act)
                    fn(oaT[:, :, m * P:(m + 1) * P], ps[:, b, :].rearrange("p (k t) -> p k t", k=4), ACT.Copy).then_inc(a_read, 1)
                for j in range(4):
                    b = me.s.take(act)
                    fn(uh[:, 2 * j:2 * j + 2, :].rearrange("p k t -> p (k t)"), ps[:, b, :], ACT.Copy).then_inc(norm_h, 1)
                high_half(Q_OUT + 2)
                high_half(Q_OUT + 3)

            me.barrier("mix0")
            mixer(0)
            me.barrier("ffn2")
            ffn("ffn2", "ffn_norm_2", 0)
            me.barrier("mix1")
            mixer(1)

            me.barrier("moe")
            norm([(uT, "ffn_norm_2", KD)])
            high("moe", 0, 0, MOE_U, SLOT)
            high("moe", 1, 0, MOE_U, SLOT)
            me.see(lmax_ready)
            for m in range(M):
                t = fn(R_["exp"][:, m * E:(m + 1) * E], R_["logit"][:, m * E:(m + 1) * E], ACT.Exp, bias=R_["neg_max"][:, m:m + 1])
            t.then_inc(lexp_ready, 1)
            act.wait_ge(items_ready, 1)
            n = act.value_load(rti[0:1, 0:1], min_val=MIN_ITEMS, max_val=ITEMS)

            def take_tokens(count, u):
                act.wait_ge(picked, count)
                act.wait_ge(u_done, u)
                for j in range(2):
                    t = fn(xh[:, 4 * j:4 * j + 4, 0:P], ps[:, 5 + j, :].rearrange("p (k t) -> p k t", k=4), ACT.Copy)
                t.then_inc(xh_ready, 1)

            def item(it, last=False):
                U = it * NBB + MOE_U

                def step(b):
                    u = U + b
                    silu(u, FB)
                    high_h(u - 1, FB)
                    high("moe", 0, it * NBB + b + 1, u + 1, SLOT)
                    high("moe", 1, it * NBB + b + 1, u + 1, SLOT)
                    high("moe", 2, it * NBB + b, u, SLOT)

                with act.Fori(1, NBB - 1) as b:
                    step(b)
                u = U + (NBB - 1)
                silu(u, FB)
                high_h(u - 1, FB)
                if not last:
                    high("moe", 0, it * NBB + NBB, u + 1, SLOT)
                    take_tokens(it + 2, u + 1)
                    high("moe", 1, it * NBB + NBB, u + 1, SLOT)
                high("moe", 2, it * NBB + (NBB - 1), u, SLOT)
                act.wait_ge(pickT_done, it + 1)
                fn(pickT, ps[:, 7, 0:S], ACT.Copy).then_inc(pickT_ready, 1)
                if last:
                    high_h(u, FB)
                else:
                    step(NBB)

            take_tokens(1, MOE_U)
            high("moe", 2, 0, MOE_U, SLOT)
            silu(MOE_U, FB)
            high("moe", 0, 1, MOE_U + 1, SLOT)
            high("moe", 1, 1, MOE_U + 1, SLOT)
            with act.Fori(0, n - 1) as it:
                item(it)
            item(n - 1, last=True)
            me.barrier("final")
            norm()

        @block.vector
        def _(dve):
            me = Side(dve)
            v = nc.vector
            link = lambda ins: me.link(ins, dve_order)

            def norm(g=None):
                me.norms += 1
                me.see(norm_sq, M)
                v.tensor_scalar(small[:, 2:4], small[:, 0:2], 1.0 / D, EPS, ALU.mult, ALU.add).then_inc(norm_ms, 1)
                me.see(norm_rt)
                link(v.reciprocal(small[:, 6:8], small[:, 4:6]))
                for m in range(M):
                    v.tensor_scalar(xn[:, m, :], x[:, m, :], small[:, 6 + m:7 + m], None, ALU.mult).then_inc(norm_xn, 1)
                if g is None:
                    return
                for j in (0, 2):
                    b = me.v.take(dve)
                    for kk_ in range(2):
                        k = 2 * j + kk_
                        for dst, name, off in g:
                            t = v.tensor_scalar(dst[:, k, :], ps[:, b, kk_ * S:(kk_ + 1) * S], col(name, off + k), None, ALU.mult)
                    t.then_inc(v_read, 1)

            def low_parts(g, off, hi, lo):
                for j in range(4):
                    b = me.s.take(dve)
                    me.see(norm_h)
                    for kk_ in range(2):
                        k = 2 * j + kk_
                        t = v.scalar_tensor_tensor(lo[:, k, :], ps[:, b, kk_ * S:(kk_ + 1) * S], col(g, off + k),
                                                   hi[:, k, :], ALU.mult, ALU.subtract)
                    t.then_inc(s_read, 1)

            def residual(t, m):
                b = me.v.take(dve)
                xs = x[:, m, t * 512:(t + 1) * 512]
                v.tensor_tensor(xs, xs, ps[:, b, :], ALU.add).then_inc(v_read, 1)

            def columns(g):
                b = me.v.take(dve)
                v.tensor_copy(cols[:, g * P:g * P + ROWS_USED[g]], ps[:, b, 0:ROWS_USED[g]]).then_inc(v_read, 1)

            columns(0)
            dve.wait_ge(v_read, me.v.n)
            dve.wait_ge(x_in, 16)

            norm([(uT, "a_norm", 0)])
            columns(1)
            link(v.memset(zp[:, :, 0:CONV - 1], 0.0))
            la = col("a_lambda", 0, KD)
            link(v.tensor_scalar(lam[:, 2, :], la, -1.0, None, ALU.mult))
            v.tensor_tensor(lam[:, 0, :], lam[:, 2, :], la, ALU.max).then_inc(lam_abs, 1)
            me.see(lam_exp)
            link(v.tensor_scalar(lam[:, 3, :], lam[:, 1, :], 2.0, None, ALU.add))
            link(v.reciprocal(lam[:, 3, :], lam[:, 3, :]))
            link(v.tensor_tensor(lam[:, 3, :], lam[:, 1, :], lam[:, 3, :], ALU.mult))
            link(v.tensor_tensor(lam[:, 4, :], lam[:, 3, :], lam[:, 3, :], ALU.mult))
            link(v.tensor_scalar(lam[:, 5, :], lam[:, 4, :], 1.0 / 17, 1.0 / 15, ALU.mult, ALU.add))
            for d in (13, 11, 9, 7, 5, 3, 1):
                link(v.tensor_tensor(lam[:, 5, :], lam[:, 5, :], lam[:, 4, :], ALU.mult))
                link(v.tensor_scalar(lam[:, 5, :], lam[:, 5, :], 1.0 / d, None, ALU.add))
            link(v.tensor_tensor(lam[:, 5, :], lam[:, 5, :], lam[:, 3, :], ALU.mult))
            link(v.tensor_scalar(lam[:, 6, :], lam[:, 2, :], 0.0, None, ALU.max))
            link(v.scalar_tensor_tensor(lam[:, 6, :], lam[:, 5, :], 2.0, lam[:, 6, :], ALU.mult, ALU.add))
            link(v.tensor_scalar(lam[:, 7, :], lam[:, 6, :], -LRU_C, None, ALU.mult))
            for f in range(KD):
                b = me.v.take(dve)
                v.tensor_copy(zp[:, f, CONV - 1:], ps[:, b, 0:S]).then_inc(v_read, 1)
                dve.wait_ge(v_read, me.v.n)
                link(v.tensor_scalar(xr[:, f, :], zp[:, f, 0:S], col("a_conv_w", f), col("a_conv_b", f), ALU.mult, ALU.add))
                for k in range(1, CONV):
                    t = v.scalar_tensor_tensor(xr[:, f, :], zp[:, f, k:k + S], col("a_conv_w", k * KD + f), xr[:, f, :],
                                               ALU.mult, ALU.add)
                    if k < CONV - 1:
                        link(t)
                t.then_inc(xr_ready, 1)
            me.see(ri_ready)
            v.tensor_tensor(rg[:], rg[:], lam[:, 7, :].unsqueeze(2).to_broadcast([P, KD, S]), ALU.mult).then_inc(la_ready, 1)
            link(v.tensor_tensor(ig[:], ig[:], xr[:], ALU.mult))
            me.see(a_ready)
            link(v.tensor_tensor(xr[:], aa[:], aa[:], ALU.mult))
            link(v.memset(aa[:, :, 0:1], 0.0))
            me.see(th_ready)
            v.scalar_tensor_tensor(th[:], xr[:], 1.0, th[:], ALU.add, ALU.mult).then_inc(t2_ready, 1)
            me.see(sq_ready)
            link(v.tensor_tensor(ig[:], ig[:], th[:], ALU.mult))
            link(v.tensor_tensor_scan(rg[:].rearrange("p k t -> p (k t)"), aa[:].rearrange("p k t -> p (k t)"),
                                      ig[:].rearrange("p k t -> p (k t)"), 0.0, ALU.mult, ALU.add))
            me.see(yg_ready)
            v.tensor_tensor(rg[:], rg[:], yg[:], ALU.mult).then_inc(yh_ready, 1)
            for t in range(2):
                for m in range(M):
                    residual(t, m)

            def wait(s, val):
                if not (isinstance(val, int) and val <= 0):
                    dve.wait_ge(s, val)

            def low(name, kind, B, n):
                dve.wait_ge(wh_full[kind], B + 1)
                v.tensor_tensor(wl[:, kind, 0:n], raw[:, plan[name][kind][0], 0:n], wh[:, kind, 0:n].bitcast(F32),
                                ALU.subtract).then_inc(wl_full[kind], 1)

            def hidden(u, w, root=None):
                dve.wait_ge(sg_ready, u + 1)
                dve.wait_ge(u_done, u + 1)
                wait(t_done, u)
                if root is None:
                    t = v.tensor_tensor(hb[:, 0:w], ps[:, 1, 0:w], sg[:, 0:w], ALU.mult)
                else:
                    t = v.scalar_tensor_tensor(hb[:, 0:w], ps[:, 1, 0:w], root, sg[:, 0:w], ALU.mult, ALU.mult)
                t.then_inc(h_ready, 1)

            def low_h(u, w):
                dve.wait_ge(hh_ready, u + 1)
                v.tensor_tensor(hl[:, 0:w], ps[:, 2, 0:w], hh[:, 0:w].bitcast(F32), ALU.subtract).then_inc(hl_ready, 1)

            def add_down(u, dst):
                dve.wait_ge(d_done, u + 1)
                for half in range(2):
                    o = dst[:, half * FB:(half + 1) * FB]
                    t = v.tensor_tensor(o, o, ps[:, 3 + half, :], ALU.add)
                t.then_inc(d_added, 1)

            def ffn(name, g, off):
                nb, wlast, B0, U0 = FFN[name]
                low_parts(g, off, xh[:].bitcast(F32), xl)
                me.see(first_high)
                n = SLOT // 2
                v.tensor_tensor(wl[:, 0, 0:n], raw[:, plan[name][0][0], 0:n], wh[:, 0, 0:n].bitcast(F32),
                                ALU.subtract).then_inc(first_low, 1)
                dve.wait_ge(wh_full[0], B0 + 1)
                v.tensor_tensor(wl[:, 0, n:], raw[:, plan[name][0][0], n:], wh[:, 0, n:].bitcast(F32),
                                ALU.subtract).then_inc(wl_full[0], 1)
                low(name, 1, B0, SLOT)
                me.see(norm_sq, M)
                v.tensor_scalar(small[:, 2:4], small[:, 0:2], 1.0 / D, EPS, ALU.mult, ALU.add).then_inc(norm_ms, 1)
                me.see(norm_rt)
                v.reciprocal(small[:, 6:8], small[:, 4:6]).then_inc(root_done, 1)
                me.see(root_done)

                def body(b, w, first=False, last=False, wn=FB):
                    u, B = b * M + U0, b + B0
                    if not first:
                        low_h(u - 1, FB)
                    hidden(u, w, small[:, 6:7])
                    if not first:
                        add_down(u - 1, x[:, 1, :])
                    low(name, 2, B, w // P * D)
                    low_h(u, w)
                    if not last:
                        low(name, 0, B + 1, KD * wn)
                    hidden(u + 1, w, small[:, 7:8])
                    if not last:
                        low(name, 1, B + 1, KD * wn)
                    add_down(u, x[:, 0, :])

                body(0, FB, first=True)
                with dve.Fori(1, nb - 2) as b:
                    body(b, FB)
                body(nb - 2, FB, wn=wlast)
                body(nb - 1, wlast, last=True)
                low_h(U0 + nb * M - 1, wlast)
                add_down(U0 + nb * M - 1, x[:, 1, :])

            me.barrier("ffn0")
            ffn("ffn0", "f_norm", 0)

            me.barrier("nsa")
            norm([(uT, "kv_norm", 0), (ubT, "b_norm", 0)])
            for t in range(3):
                b = me.v.take(dve)
                v.tensor_copy(kvn[:, 0, t * 512:(t + 1) * 512], ps[:, b, :]).then_inc(v_read, 1)
                if t == 0:
                    marks["kvc_v"] = me.v.n
            dve.wait_ge(bc_in, 16 * len(BC))
            def tables(dst, cos, sin, g, rows=P):
                v.tensor_tensor(dst[0:rows, 0, :], C(cos, rows), g[0:rows], ALU.mult)
                link(v.tensor_tensor(dst[0:rows, 1, :], C(sin, rows), g[0:rows], ALU.mult))

            gq, gk = bc[:, 0:HD], [bc[:, 64 + i * HD:64 + (i + 1) * HD] for i in range(3)]
            for m in range(M):
                tables(rope_g[:, m], f"cos{m}", f"sin{m}", gq)
                for w in range(2):
                    tables(rope_k[:, m, w], f"cos{m}", f"sin{m}", gk[1 + w])
            tables(rope_g[:, 2], "cosc", "sinc", gk[0], NCMP)

            def rope_norm(src, out, table, n, rows=P):
                a = tmp_a[0:rows, 0:n * HD].rearrange("p (h d) -> p h d", d=HD)
                b2 = tmp_b[0:rows, 0:n * HD].rearrange("p (h d) -> p h d", d=HD)
                link(v.tensor_tensor(a, src, src, ALU.mult))
                link(v.tensor_reduce(stat[0:rows, 0, 0:n], a, AX.X, ALU.add))
                link(v.tensor_scalar(stat[0:rows, 0, 0:n], stat[0:rows, 0, 0:n], 1.0 / HD, EPS, ALU.mult, ALU.add))
                dve.nop().then_inc(ms_ready, 1)
                me.see(root_ready)
                link(v.reciprocal(stat[0:rows, 1, 0:n], stat[0:rows, 1, 0:n]))
                link(v.tensor_tensor(a, src, stat[0:rows, 1, 0:n].unsqueeze(2).to_broadcast([rows, n, HD]), ALU.mult))
                link(v.tensor_tensor(b2, a, table[0:rows, 1, :].unsqueeze(1).to_broadcast([rows, n, HD]), ALU.mult))
                link(v.tensor_tensor(a, a, table[0:rows, 0, :].unsqueeze(1).to_broadcast([rows, n, HD]), ALU.mult))
                hf = HD // 2
                v.tensor_tensor(out[:, :, 0:hf], a[:, :, 0:hf], b2[:, :, hf:], ALU.subtract)
                link(v.tensor_tensor(out[:, :, hf:], a[:, :, hf:], b2[:, :, 0:hf], ALU.add))

            me.see(kvn_ready)
            for m in range(M):
                for w in range(2):
                    o = 512 + w * 512
                    kd = kdup[:, m, w]
                    rope_norm(kvn[:, m, o:o + NG * HD].rearrange("p (g d) -> p g d", d=HD), kd[:, :, 0, :],
                              rope_k[:, m, w], NG)
                    link(v.tensor_copy(kd[:, :, 1, :], kd[:, :, 0, :]))
            dve.nop().then_inc(k_ready, 1)
            for t in range(2):
                b = me.v.take(dve)
                v.tensor_copy(qn[:, 0, t * 512:(t + 1) * 512], ps[:, b, :]).then_inc(v_read, 1)
            for m in range(M):
                b = me.v.take(dve)
                v.tensor_tensor(gate[:, m, :, :].rearrange("p b h -> p (b h)"), ps[:, b, 0:3 * NH], bc[:, 384:384 + 3 * NH],
                                ALU.add).then_inc(v_read, 1)
            dve.wait_ge(v_read, me.v.n)
            dve.nop().then_inc(gate_ready, 1)
            R = NG * NCMP
            for j in range(4):
                b = me.v.take(dve)
                src = ps[:, b, 0:8 * R].rearrange("p (i k c) -> p i k c", i=4, k=2)
                for kv in range(2):
                    t = v.tensor_tensor(xcT[:, kv, 4 * j:4 * j + 4, :], src[:, :, kv, :],
                                        col("cmp_pos", kv * 16 + 4 * j, 4).unsqueeze(2).to_broadcast([P, 4, R]), ALU.add)
                t.then_inc(v_read, 1)
            me.see(qn_ready)
            for m in range(M):
                qh_ = qn[:, m, :].rearrange("p (h d) -> p h d", d=HD)
                rope_norm(qh_, qh_, rope_g[:, m], NH)
                dve.nop().then_inc(q_ready, 1)
            b = me.v.take(dve)
            b2v = bc[0:NCMP, 256:256 + 2 * HD].rearrange("p (k d) -> p k d", k=2)
            for kv in range(2):
                t = v.tensor_tensor(cmpn[0:NCMP, kv], ps[0:NCMP, b, kv * 256:(kv + 1) * 256].rearrange("p (g d) -> p g d", g=NG),
                                    b2v[:, kv, :].unsqueeze(1).to_broadcast([NCMP, NG, HD]), ALU.add)
            t.then_inc(v_read, 1)
            dve.wait_ge(v_read, me.v.n)
            rope_norm(cmpn[0:NCMP, 0], kcdup[0:NCMP, :, 0, :], rope_g[:, 2], NG, NCMP)
            link(v.tensor_copy(kcdup[0:NCMP, :, 1, :], kcdup[0:NCMP, :, 0, :]))
            dve.nop().then_inc(kc_ready, 1)
            b = me.v.take(dve)
            v.tensor_copy(kT[:, :, 0:NCMP], ps[:, b, 0:64].rearrange("p (g c) -> p g c", g=NG)[:, :, 0:NCMP]).then_inc(v_read, 1)
            me.see(gated)
            link(v.tensor_scalar(gate[:, 0, 0, :], gate[:, 0, 0, :], C("row_valid"), None, ALU.mult))

            def maxima(i, m, h):
                nk, st_ = P * (m + 1), stat[:, i % 3, :]
                b = me.sc.take(dve)
                v.tensor_reduce(st_[:, 0:1], ps[:, b, 0:NCMP], AX.X, ALU.max)
                v.tensor_reduce(st_[:, 1:2], ps[:, b, NCMP:NCMP + nk], AX.X, ALU.max)
                link(v.tensor_reduce(st_[:, 2:3], ps[:, b + 1, 0:nk], AX.X, ALU.max))
                v.tensor_scalar(st_[:, 3:6], st_[:, 0:3], -SCALE, None, ALU.mult).then_inc(max_ready, 1)

            def diagonals(i, m, h):
                st_ = stat[:, i % 3, :]
                dve.wait_ge(s_read, me.sc.base + i + 1)
                link(v.reciprocal(st_[:, 9:12], st_[:, 6:9]))
                link(v.tensor_tensor(st_[:, 12:15], st_[:, 9:12], gate[:, m, :, h], ALU.mult))
                v.tensor_tensor(diag[:, i % 2], C("ident").unsqueeze(1).to_broadcast([P, 3, P]),
                                st_[:, 12:15].unsqueeze(2).to_broadcast([P, 3, P]), ALU.mult).then_inc(diag_ready, 1)

            def outputs(m, h):
                if h % 2:
                    b = me.o.take(dve)
                    v.tensor_copy(oT[:, h // 2, m * P:(m + 1) * P], ps[:, b, 0:P]).then_inc(o_read, 1)

            pairs = [(m, h) for m in range(M) for h in range(NH)]
            me.scores_begin()
            maxima(0, *pairs[0])
            for i, pair in enumerate(pairs):
                diagonals(i, *pair)
                if i + 1 < len(pairs):
                    maxima(i + 1, *pairs[i + 1])
                if i:
                    outputs(*pairs[i - 1])
            outputs(*pair)
            me.scores_end()
            for t in range(2):
                for m in range(M):
                    residual(t, m)

            me.barrier("ffn1")
            ffn("ffn1", "f_norm", KD)

            def mixer(layer):
                def low_half(q):
                    me.see(mh_ready)
                    v.tensor_tensor(half_view(layer, q, raw_low), half_view(layer, q), wmh[:, q % 2].bitcast(F32),
                                    ALU.subtract).then_inc(ml_ready, 1)

                norm()
                low_half(0)
                low_parts("mix_norm_2", layer * KD, uh[:].bitcast(F32), ul)
                low_half(1)
                lg = [col("hgrn_lb_logits_2", i * HH, HH) for i in range(2)]
                link(v.tensor_copy(lbt[:, 7, :], lg[0]))
                link(v.tensor_tensor(lbt[:, 0, :], lbt[:, 7, :], lg[1], ALU.max))
                for i in range(2):
                    link(v.tensor_tensor(lbt[:, 1 + i, :], lg[i], lbt[:, 0, :], ALU.subtract))
                dve.nop().then_inc(lb_max, 1)
                me.see(lb_exp)
                link(v.tensor_tensor(lbt[:, 7, :], lbt[:, 1, :], lbt[:, 2, :], ALU.add))
                link(v.reciprocal(lbt[:, 7, :], lbt[:, 7, :]))
                for i in range(2):
                    link(v.tensor_tensor(lbt[:, 1 + i, :], lbt[:, 1 + i, :], lbt[:, 7, :], ALU.mult))
                link(v.tensor_copy(lbt[:, 3, :], lbt[:, 1, :]))
                if layer:
                    link(v.tensor_tensor(lbt[:, 3, :], lbt[:, 1, :], lbt[:, 2, :], ALU.add))
                link(v.tensor_tensor(lbt[:, 3, :], lbt[:, 3, :], lbt[:, 1, :], ALU.subtract))
                link(v.tensor_scalar(lbt[:, 4, :], lbt[:, 3, :], -1.0, 1.0, ALU.mult, ALU.add))
                link(v.tensor_scalar(lbt[:, 5:7, :], lbt[:, 3:5, :], 1e-12, None, ALU.max))
                dve.nop().then_inc(lb_clamped, 1)
                me.see(lb_ln)
                link(v.tensor_scalar(lbt[:, 1:3, :], lbt[:, 3:5, :], 1e-12, NEG, ALU.is_lt, ALU.mult))
                link(v.tensor_tensor(lbt[:, 5:7, :], lbt[:, 5:7, :], lbt[:, 1:3, :], ALU.add))

                def per_head(i):
                    return lbt[:, i, :].unsqueeze(2).to_broadcast([P, HH, S])

                for c in range(4):
                    b = me.v.take(dve)
                    v.tensor_copy(zf[:, c, :], ps[:, b, 0:S]).then_inc(v_read, 1)
                    if c == 1:
                        low_half(2)
                low_half(3)
                dve.wait_ge(v_read, me.v.n)
                link(v.scalar_tensor_tensor(t1[:], zf[:], -1.0, zf[:], ALU.mult, ALU.min))
                dve.nop().then_inc(zabs_ready, 1)
                low_half(4)
                dve.wait_ge(masks_in, 16 * (layer + 1))
                dve.wait_ge(pool_set, 3 * (layer + 1))
                link(v.tensor_copy(lmask[:], t3[:].rearrange("p h t -> p (h t)")))
                low_half(5)
                me.see(zln_ready)
                link(v.scalar_tensor_tensor(t3[:], zf[:], 0.0, t2[:], ALU.min, ALU.subtract))
                link(v.tensor_tensor(t1[:], t3[:], zf[:], ALU.subtract))
                dve.nop().then_inc(zdif_ready, 1)
                low_half(6)

                def stick_keys(c0):
                    for c in (c0, c0 + 1):
                        b = me.v.take(dve)
                        v.tensor_copy(skT[:, c, :], ps[:, b, 0:S]).then_inc(v_read, 1)

                stick_keys(0)
                link(v.tensor_tensor(t3[:], t3[:], per_head(6), ALU.add))
                link(v.tensor_tensor(t2[:], t3[:], per_head(5), ALU.subtract))
                link(v.scalar_tensor_tensor(t2[:], t2[:], -1.0, t2[:], ALU.mult, ALU.min))
                dve.nop().then_inc(fabs_ready, 1)
                low_half(7)
                link(v.tensor_tensor(t3[:], t3[:], per_head(5), ALU.max))
                me.see(kk_ready)
                link(v.tensor_tensor(kk[:], kk[:], per_head(4), ALU.mult))
                stick_keys(2)
                me.see(fln_ready)
                link(v.tensor_tensor(t3[:], t3[:], t2[:], ALU.add))
                flat = lambda a: a[:].rearrange("p h t -> p (h t)")
                link(v.tensor_tensor_scan(flat(bb), flat(keep), flat(t3), 0.0, ALU.mult, ALU.add))
                me.see(qh_ready)

                def exponents(lv):
                    if lv <= 32:
                        bv = flat(bb).rearrange("p (n s) -> p n s", s=2 * lv)
                        tv = flat(t1).rearrange("p (n s) -> p n s", s=2 * lv)
                        mid = bv[:, :, lv - 1:lv].to_broadcast([P, HH * S // (2 * lv), lv])
                        v.tensor_tensor(tv[:, :, 0:lv], mid, bv[:, :, 0:lv], ALU.subtract)
                        link(v.tensor_tensor(tv[:, :, lv:], bv[:, :, lv:], mid, ALU.subtract))
                        return
                    chunk = lambda a, c: a[:, :, c * HC:(c + 1) * HC]
                    last = lambda c: bb[:, :, c * HC + HC - 1:c * HC + HC].to_broadcast([P, HH, HC])
                    if lv == 64:
                        for c in (0, 2):
                            v.tensor_tensor(chunk(t1, c), last(c), chunk(bb, c), ALU.subtract)
                        for c in (1, 3):
                            t = v.tensor_copy(chunk(t1, c), chunk(bb, c))
                        link(t)
                        return
                    v.tensor_tensor(chunk(t1, 1), last(1), chunk(bb, 1), ALU.subtract)
                    v.tensor_copy(chunk(t1, 2), chunk(bb, 2))
                    v.tensor_tensor(chunk(t1, 3), chunk(bb, 3), last(2), ALU.add)
                    link(v.tensor_tensor(chunk(t1, 0), last(0), chunk(bb, 0), ALU.subtract))
                    link(v.tensor_tensor(chunk(t1, 0), chunk(t1, 0), last(1), ALU.add))

                def factors(lv):
                    sz = 2 * lv
                    view = lambda a: flat(a).rearrange("p (n s) -> p n s", s=sz)
                    v.tensor_tensor(view(t2)[:, :, 0:lv], view(kk)[:, :, 0:lv], view(t1)[:, :, 0:lv], ALU.mult)
                    link(v.tensor_tensor(view(t2)[:, :, lv:], view(qh)[:, :, lv:], view(t1)[:, :, lv:], ALU.mult))

                def collect(j, lv):
                    if lv == 128:
                        b = me.v2.take(dve)
                        v.tensor_copy(sx[:].rearrange("p h t -> p (h t)"), ps[:, b, :]).then_inc(v_read, 1)
                        dve.wait_ge(v_read, me.v2.n)
                        return
                    mask = lmask[:, j * P:(j + 1) * P].unsqueeze(1).to_broadcast([P, 4, P])
                    for hp in range(2):
                        b = me.v2.take(dve)
                        v.copy_predicated(sd[:, 2 * hp:2 * hp + 2].rearrange("p a m t -> p (a m) t"), mask,
                                          ps[:, b, :].rearrange("p (n t) -> p n t", n=4)).then_inc(v_read, 1)
                    dve.wait_ge(v_read, me.v2.n)

                me.v2.n = me.v.n
                levels = [0] + LEVELS + [64, 128]

                def softplus(h):
                    b = me.s.take(dve)
                    me.see(ln_ready)
                    s_ = sp[:, h % 2, :]
                    v.scalar_tensor_tensor(s_, ps[:, b, 0:384], 0.0, e1[:, h % 2, :], ALU.max, ALU.add).then_inc(s_read, 1)
                    dve.wait_ge(s_read, me.s.n)
                    diag = s_.rearrange("p (a t) -> p a t", t=P)[:, 0:3:2, :]
                    v.tensor_tensor(diag, diag, C("before").unsqueeze(1).to_broadcast([P, 2, P]), ALU.mult).then_inc(sp_ready, 1)

                k = 0
                low_half(8)
                for i in range(HALVES):
                    if 9 + i < Q_OUT:
                        low_half(9 + i)
                    if i in LEVEL_AT:
                        if k:
                            collect(k - 1, levels[k - 1])
                            me.see(decay_exp)
                            factors(levels[k])
                        dve.nop().then_inc(level_ready, 1)
                        k += 1
                        if k < len(levels):
                            exponents(levels[k])
                            dve.nop().then_inc(decay_ready, 1)
                    if i == min(HEAD_AT) - 1:
                        softplus(0)
                    h = HEAD_AT.get(i, SH if i == max(HEAD_AT) + 1 else -1)
                    if 0 <= h and h + 1 < SH:
                        softplus(h + 1)
                    if h > 0 and h % 2 == 0:
                        b = me.o.take(dve)
                        v.tensor_copy(obT[:, h // 2 - 1, :], ps[:, b, 0:S]).then_inc(o_read, 1)
                collect(len(levels) - 1, 128)
                me.v.n = me.v2.n

                def gated_branch(dst, m, half):
                    cs = slice(half * 512, half * 512 + 512)
                    b = me.v.take(dve)
                    return v.tensor_tensor(dst[:, m, cs], ps[:, b, :], dst[:, m, cs], ALU.mult).then_inc(v_read, 1)

                me.see(gates_on)
                gated_branch(sgb, 0, 0)
                for m in range(M):
                    b = me.v.take(dve)
                    v.tensor_copy(oa[:, m, :], ps[:, b, :]).then_inc(v_read, 1)
                dve.wait_ge(v_read, me.v.n)
                o8 = oa[:].rearrange("p m (h d) -> p (m h) d", d=P)
                t8 = flat(t1).rearrange("p (n d) -> p n d", d=P)
                link(v.tensor_tensor(t8, o8, o8, ALU.mult))
                link(v.tensor_reduce(small[:, 16:24], t8, AX.X, ALU.add))
                link(v.tensor_scalar(small[:, 16:24], small[:, 16:24], 1.0 / P, EPS, ALU.mult, ALU.add))
                dve.nop().then_inc(oms_ready, 1)
                g = bc[:, 432 + layer * P:432 + (layer + 1) * P].unsqueeze(1).to_broadcast([P, 8, P])
                link(v.tensor_tensor(o8, o8, g, ALU.mult))
                me.see(gates_on, 2)
                link(v.tensor_tensor(oa[:], oa[:], hog[:], ALU.mult))
                gated_branch(sgb, 0, 1)
                me.see(ort_ready)
                link(v.reciprocal(small[:, 32:40], small[:, 24:32]))
                v.tensor_tensor(o8, o8, small[:, 32:40].unsqueeze(2).to_broadcast([P, 8, P]), ALU.mult).then_inc(oa_ready, 1)
                gated_branch(sgb, 1, 0)
                gated_branch(sgb, 1, 1)
                low_half(Q_OUT)
                low_half(Q_OUT + 1)

                def low_sum(half):
                    for j in (2 * half, 2 * half + 1):
                        b = me.s.take(dve)
                        me.see(norm_h)
                        two = lambda a: a[:, 2 * j:2 * j + 2, :].rearrange("p k t -> p (k t)")
                        v.tensor_tensor(two(ul), ps[:, b, :], two(uh).bitcast(F32), ALU.subtract).then_inc(s_read, 1)

                for half in range(2):
                    for m in range(M):
                        gated_branch(sga, m, half)
                        dve.wait_ge(v_read, me.v.n)
                        cs = slice(half * 512, half * 512 + 512)
                        v.tensor_tensor(sga[:, m, cs], sga[:, m, cs], sgb[:, m, cs], ALU.add).then_inc(y_ready, 1)
                        if (half, m) == (1, 0):
                            low_sum(0)
                low_sum(1)
                for q in range(4):
                    b = me.v.take(dve)
                    xs = x[:, :, q * HW:(q + 1) * HW]
                    v.tensor_tensor(xs, xs, ps[:, b, :].rearrange("p (m n) -> p m n", m=M), ALU.add).then_inc(v_read, 1)
                    if q < 2:
                        low_half(Q_OUT + 2 + q)

            me.barrier("mix0")
            mixer(0)
            me.barrier("ffn2")
            ffn("ffn2", "ffn_norm_2", 0)
            me.barrier("mix1")
            mixer(1)

            me.barrier("moe")
            norm([(uT, "ffn_norm_2", KD)])
            dve.wait_ge(ye_in, 16)
            dve.wait_ge(a_filled, marks["moe_turned"])
            for m in range(M):
                link(v.tensor_tensor(xn[:, m, :], xn[:, m, :], ye[:], ALU.mult))
            v.memset(ye[:], 0.0)
            low("moe", 0, MOE_B, SLOT)
            b = me.v.take(dve)
            v.tensor_copy(R_["logit"], ps[:, b, 0:M * E]).then_inc(v_read, 1)
            dve.wait_ge(v_read, me.v.n)
            for m in range(M):
                lm = R_["logit"][:, m * E:(m + 1) * E]
                ge8 = R_["a64"].rearrange("p (e f) -> p e f", e=E)
                eq8 = R_["b64"].rearrange("p (e f) -> p e f", e=E)
                mine, other = lm.unsqueeze(2).to_broadcast([P, E, E]), lm.unsqueeze(1).to_broadcast([P, E, E])
                link(v.tensor_tensor(ge8, other, mine, ALU.is_gt))
                link(v.tensor_tensor(eq8, other, mine, ALU.is_equal))
                link(v.tensor_tensor(R_["b64"], R_["b64"], C("lower_e"), ALU.mult))
                link(v.tensor_tensor(R_["a64"], R_["a64"], R_["b64"], ALU.add))
                link(v.tensor_reduce(R_["rank"], ge8, AX.X, ALU.add))
                link(v.tensor_scalar(sel[:, m, :], R_["rank"], 1.5, None, ALU.is_lt))
                link(v.tensor_reduce(R_["neg_max"][:, m:m + 1], lm, AX.X, ALU.max))
            link(v.tensor_scalar(R_["neg_max"], R_["neg_max"], -1.0, None, ALU.mult))
            dve.nop().then_inc(sel_ready, 1)
            dve.nop().then_inc(lmax_ready, 1)
            me.see(lexp_ready)
            for m in range(M):
                wm = R_["weight"][:, m * E:(m + 1) * E]
                link(v.tensor_tensor(wm, R_["exp"][:, m * E:(m + 1) * E], sel[:, m, :], ALU.mult))
                link(v.tensor_reduce(R_["sum"][:, m:m + 1], wm, AX.X, ALU.add))
                link(v.reciprocal(R_["sum"][:, m:m + 1], R_["sum"][:, m:m + 1]))
                link(v.tensor_scalar(wm, wm, R_["sum"][:, m:m + 1], None, ALU.mult))
            b = me.v.take(dve)
            v.tensor_copy(R_["pos"], ps[:, b, 0:3 * E]).then_inc(v_read, 1)
            dve.wait_ge(v_read, me.v.n)
            count = R_["pos"][:, 2 * E:3 * E]
            link(v.tensor_scalar(R_["tiles"], count, 0.5, None, ALU.is_gt))
            link(v.memset(R_["tiles"][:, 0:1], 1.0))
            link(v.tensor_scalar(R_["ones"], count, P + 0.5, None, ALU.is_gt))
            link(v.tensor_tensor(R_["tiles"], R_["tiles"], R_["ones"], ALU.add))
            link(v.memset(R_["ones"], 1.0))
            link(v.tensor_tensor_scan(R_["upto"], R_["ones"], R_["tiles"], 0.0, ALU.mult, ALU.add))
            link(v.tensor_tensor(R_["before"], R_["upto"], R_["tiles"], ALU.subtract))
            shape = [P, ITEMS, E]
            own = R_["owner"].rearrange("p (i e) -> p i e", i=ITEMS)
            tmp = R_["tmp"].rearrange("p (i e) -> p i e", i=ITEMS)
            iota_i = C("iota_i").unsqueeze(2).to_broadcast(shape)
            over_e = lambda a: a.unsqueeze(1).to_broadcast(shape)
            link(v.tensor_tensor(own, iota_i, over_e(R_["before"]), ALU.is_ge))
            link(v.tensor_tensor(tmp, iota_i, over_e(R_["upto"]), ALU.is_lt))
            link(v.tensor_tensor(own, own, tmp, ALU.mult))

            def of_item(dst, a):
                link(v.tensor_tensor(tmp, own, over_e(a), ALU.mult))
                link(v.tensor_reduce(dst, tmp, AX.X, ALU.add))

            of_item(R_["expert"], C("iota_e"))
            of_item(R_["first"], R_["before"])
            link(v.tensor_tensor(R_["first"], C("iota_i"), R_["first"], ALU.subtract))
            link(v.tensor_scalar(R_["first"], R_["first"], float(P), None, ALU.mult))
            for m in range(M):
                sl, wi = slot_of[:, m, :], weight_of[:, m, :]
                of_item(wi, R_["weight"][:, m * E:(m + 1) * E])
                of_item(sl, R_["pos"][:, m * E:(m + 1) * E])
                of_item(R_["there"], sel[:, m, :])
                link(v.tensor_tensor(sl, sl, R_["first"], ALU.subtract))
                link(v.tensor_scalar(sl, sl, 1.0, None, ALU.add))
                link(v.tensor_tensor(sl, sl, R_["there"], ALU.mult))
                link(v.tensor_scalar(sl, sl, -1.0, None, ALU.add))
            link(v.tensor_copy(rti[0:1, 0:1], R_["upto"][0:1, E - 1:E]))
            link(v.tensor_copy(rti[0:1, 1:1 + ITEMS], R_["expert"][0:1, :]))
            dve.nop().then_inc(items_ready, 1)
            n = dve.value_load(rti[0:1, 0:1], min_val=MIN_ITEMS, max_val=ITEMS)

            def add_up(u, first=False):
                if not first:
                    return add_down(u, ye)
                dve.wait_ge(d_done, u + 1)
                for half in range(2):
                    t = v.tensor_copy(ye[:, half * FB:(half + 1) * FB], ps[:, 3 + half, :])
                t.then_inc(d_added, 1)

            def pick_tokens(i):
                for m in range(M):
                    t = v.tensor_scalar(pick[:, m, :], C("iota_slot"), slot_of[:, m, bass.ds(i, 1)], None, ALU.is_equal)
                return t

            def weigh_tokens(i):
                for m in range(M):
                    t = v.tensor_scalar(pickw[:, m, :], C("iota_slot"), slot_of[:, m, bass.ds(i, 1)],
                                        weight_of[:, m, bass.ds(i, 1)], ALU.is_equal, ALU.mult)
                return t

            def low_tokens(count):
                dve.wait_ge(xh_ready, count)
                for j in range(2):
                    t = v.tensor_tensor(xl[:, 4 * j:4 * j + 4, 0:P], ps[:, 5 + j, :].rearrange("p (k t) -> p k t", k=4),
                                        xh[:, 4 * j:4 * j + 4, 0:P].bitcast(F32), ALU.subtract)
                t.then_inc(xl_ready, 1)

            def item(it, last=False):
                B, U = it * NBB + MOE_B, it * NBB + MOE_U

                def add_given(count):
                    dve.wait_ge(put_done, count)
                    for m in range(M):
                        for half in range(2):
                            xs = x[:, m, half * FB:(half + 1) * FB]
                            t = v.tensor_tensor(xs, xs, ps[:, GIVE_BANKS[2 * m + half], :], ALU.add)
                    t.then_inc(put_added, 1)

                def step(b, first=False):
                    low_h(U + b - 1, FB)
                    low("moe", 0, B + b + 1, SLOT)
                    hidden(U + b, FB)
                    low("moe", 1, B + b + 1, SLOT)
                    if first:
                        add_given(it + 1)
                    add_up(U + b - 1, first)
                    low("moe", 2, B + b, SLOT)

                step(1, first=True)
                dve.wait_ge(picked, it + 1)
                t = weigh_tokens(it)
                if not last:
                    t = pick_tokens(it + 1)
                t.then_inc(pick_ready, 1)
                with dve.Fori(2, NBB - 1) as b:
                    step(b)
                u = U + (NBB - 1)
                low_h(u - 1, FB)
                if not last:
                    low("moe", 0, B + NBB, SLOT)
                hidden(u, FB)
                if not last:
                    low_tokens(it + 2)
                    low("moe", 1, B + NBB, SLOT)
                add_up(u - 1)
                low("moe", 2, B + (NBB - 1), SLOT)
                if last:
                    low_h(u, FB)
                    add_up(u)
                else:
                    step(NBB)
                if last:
                    add_given(it + 2)

            pick_tokens(0).then_inc(pick_ready, 1)
            v.memset(pickT, 0.0).then_inc(pickT_ready, 1)
            low("moe", 1, MOE_B, SLOT)
            low_tokens(1)
            low("moe", 2, MOE_B, SLOT)
            low("moe", 0, MOE_B + 1, SLOT)
            hidden(MOE_U, FB)
            low("moe", 1, MOE_B + 1, SLOT)
            with dve.Fori(0, n - 1) as it:
                item(it)
            item(n - 1, last=True)
            me.barrier("final")
            norm()
            dve.wait_ge(final_in, 16)
            for m in range(M):
                dve.wait_ge(norm_xn, M * me.norms)
                v.tensor_tensor(xn[:, m, :], xn[:, m, :], uT[:, 0:4, :].rearrange("p a b -> p (a b)"), ALU.mult).then_inc(out_ready, 1)

        @block.sync
        def _(sp_eng):
            sy = sp_eng
            sy.dma_start(x[:], A["x"].rearrange("a (m p) d -> p (a m) d", p=P)).then_inc(x_in, 16)
            sy.dma_start(const[:], A["const_f32"]).then_inc(const_in, 16)
            sy.wait_ge(rows_in[0], 16 * len(ROWS[0]))

            def kp(w):
                return w.rearrange("(k p) n -> p k n", p=P)

            held = [None, None, None]

            def fill(s, src, k, w, free=None):
                if free or held[s]:
                    sy.wait_ge(*(free or held[s]))
                sy.dma_start(raw[:, s, 0:k * w].rearrange("p (k n) -> p k n", k=k), src).then_inc(slot_full[s], 16)

            def ffn_tiles(name, win_g, win_u, wdn):
                nb, wlast = FFN[name][:2]
                B0 = FFN[name][2]

                slot = [s for s, _ in plan[name]]

                def gu(b, w=FB, st=False, free=True):
                    cs = slice(b * FB, b * FB + w) if st else bass.ds(b * FB, FB)
                    fill(slot[0], kp(win_g)[:, :, cs], KD, w, (wl_full[0], b + B0) if free else None)
                    fill(slot[1], kp(win_u)[:, :, cs], KD, w, (wl_full[1], b + B0) if free else None)

                def dn(b, w=FB, st=False, free=True):
                    cs = slice(b * 4, b * 4 + w // P) if st else bass.ds(b * 4, 4)
                    fill(slot[2], kp(wdn)[:, cs, :], w // P, D, (wl_full[2], b + B0) if free else None)

                gu(0, FB, True, free=False)
                dn(0, FB, True, free=False)
                gu(1, FB, True)
                with sy.Fori(1, nb - 2) as b:
                    dn(b)
                    gu(b + 1)
                dn(nb - 2, FB, True)
                gu(nb - 1, wlast, True)
                dn(nb - 1, wlast, True)
                for kind in range(3):
                    held[slot[kind]] = (wl_full[kind], B0 + nb)

            for key in order:
                if len(key) == 1 and key[0] in FFN:
                    if key[0] == "ffn2":
                        ffn_tiles("ffn2", A["dense_w_gate_2"][0], A["dense_w_up_2"][0], A["dense_w_down_2"][0])
                    else:
                        i = int(key[0][3])
                        ffn_tiles(key[0], A["f_w_in"][i, :, 0:F_A], A["f_w_in"][i, :, F_A:2 * F_A], A["f_w_out"][i])
                    continue
                if key == ("moe",):
                    continue
                s, f = plan[key]
                kind = key[0]
                t = key[-1]
                if kind == "a_in":
                    fill(s, kp(A["a_w_in"][0])[:, :, t * 512:t * 512 + 512], KD, 512)
                elif kind == "a_gate":
                    fill(s, A["a_gate_w"][0].rearrange("g h i j -> i (g h) j"), 16, P)
                elif kind == "a_out":
                    fill(s, kp(A["a_w_out"][0])[:, :, t * 512:t * 512 + 512], KD, 512)
                elif kind == "kv":
                    fill(s, kp(A["kv_w"])[:, :, t * 512:t * 512 + 512], KD, 512)
                elif kind == "cmp":
                    fill(s, kp(A["cmp_w1"][t]), 16, CH)
                elif kind == "b_in":
                    w = 512 if t < 2 else 3 * NH
                    fill(s, kp(A["b_w_in"][0])[:, :, t * 512:t * 512 + w], KD, w)
                elif kind == "b_out":
                    fill(s, kp(A["b_w_out"][0])[:, :, t * 512:t * 512 + 512], KD, 512)
                elif kind == "mix_in":
                    fill(s, kp(A["w_in_2"][key[1]])[:, :, t * 512:t * 512 + 512], KD, 512)
                elif kind == "branch":
                    w = A["w_branch_hgrn_2"] if t == 0 else A["w_branch_sb_2"]
                    fill(s, kp(w[key[1]]), 4, D)
                elif kind == "mix_out":
                    fill(s, kp(A["w_out_2"][key[1]])[:, :, t * 512:t * 512 + 512], KD, 512)
                held[s] = freed[key]

            wg = A["moe_w_gate_2"][0].rearrange("e (k p) n -> e p k n", p=P)
            wu = A["moe_w_up_2"][0].rearrange("e (k p) n -> e p k n", p=P)
            wd = A["moe_w_down_2"][0].rearrange("e (k p) n -> e p k n", p=P)
            slot = [s for s, _ in plan["moe"]]

            def expert_of(it):
                return sy.value_load(rti[0:1, bass.ds(it + 1, 1)], min_val=0, max_val=E - 1)

            def one(kind, w, e, B, cs):
                src = w[bass.ds(e, 1), :, cs, :] if kind == 2 else w[bass.ds(e, 1), :, :, cs]
                sy.wait_ge(wl_full[kind], B)
                k = 4 if kind == 2 else KD
                sy.dma_start(raw[:, slot[kind], :].rearrange("p (k n) -> p k n", k=k),
                             src.rearrange("e p k n -> (e p) k n")).then_inc(slot_full[slot[kind]], 16)

            for kind, w, b in ((0, wg, 0), (1, wu, 0), (2, wd, 0), (0, wg, 1), (1, wu, 1)):
                src = w[0, :, 0:4, :] if kind == 2 else w[0, :, :, b * FB:(b + 1) * FB]
                fill(slot[kind], src, 4 if kind == 2 else KD, D if kind == 2 else FB, (wl_full[kind], MOE_B + 1) if b else None)
            sy.wait_ge(items_ready, 1)
            n = sy.value_load(rti[0:1, 0:1], min_val=MIN_ITEMS, max_val=ITEMS)

            def item(it, last=False):
                B = it * NBB + MOE_B
                e = expert_of(it)
                with sy.Fori(1, NBB - 1) as b:
                    one(0, wg, e, B + b + 1, bass.ds(b * FB + FB, FB))
                    one(1, wu, e, B + b + 1, bass.ds(b * FB + FB, FB))
                    one(2, wd, e, B + b, bass.ds(b * 4, 4))
                if not last:
                    e_next = expert_of(it + 1)
                    one(0, wg, e_next, B + NBB, slice(0, FB))
                    one(1, wu, e_next, B + NBB, slice(0, FB))
                one(2, wd, e, B + (NBB - 1), slice((NBB - 1) * 4, NBB * 4))
                if not last:
                    one(0, wg, e_next, B + (NBB + 1), slice(FB, 2 * FB))
                    one(1, wu, e_next, B + (NBB + 1), slice(FB, 2 * FB))
                    one(2, wd, e_next, B + NBB, slice(0, 4))

            with sy.Fori(0, n - 1) as it:
                item(it)
            item(n - 1, last=True)
            sy.wait_ge(out_ready, 2)
            sy.dma_start(out.rearrange("a (m p) d -> p (a m) d", p=P), xn[:]).then_inc(out_sent, 16)
            sy.wait_ge(out_sent, 16)

        @block.gpsimd
        def _(po):
            load_rows(po, 1)
            for name, (at, w) in BC.items():
                po.dma_start(bc[:, at:at + w], flat_view(A[name]).partition_broadcast(P)).then_inc(bc_in, 16)
            po.wait_ge(stage, 3 * marks["nsa"])
            po.dma_start(w2[:].rearrange("p k c d -> p (k c) d"),
                         A["cmp_w2"].rearrange("k (c p) d -> p (k c) d", p=P)).then_inc(w2_in, 16)
            nc.gpsimd.memset(qT[:], 0.0).then_inc(q_zeroed, 1)
            po.wait_ge(v_read, marks["kvc_v"])
            po.wait_ge(a_read, marks["kvc_a"])
            po.dma_start(kv_scratch.rearrange("(m p) n -> p m n", p=P), kvn[:, :, 0:512]).then_inc(kvc_out, 16)
            po.wait_ge(kvc_out, 16)
            for kv in range(2):
                for g in range(NG):
                    r = (kv * NG + g) * NCMP
                    for half in range(2):
                        src = kv_scratch[half * CS:half * CS + NCMP * CS, kv * 256 + g * HD:kv * 256 + g * HD + HD]
                        po.dma_start(xc[r:r + NCMP, half * CS * HD:(half + 1) * CS * HD].rearrange(
                            "c (l d) -> c l d", d=HD), src.rearrange("(c l) d -> c l d", l=CS)).then_inc(kvc_in, 16)
            for layer in range(2):
                po.wait_ge(stage, 3 * marks[f"mix{layer}"])
                po.dma_start(t3[:].rearrange("p h t -> p (h t)"), A["const_masks"]).then_inc(masks_in, 16)
                nc.gpsimd.memset(keep[:], 1.0).then_inc(pool_set, 1)
                nc.gpsimd.memset(sd[:], 0.0).then_inc(pool_set, 1)
                po.wait_ge(pool_set, 3 * layer + 2)
                nc.gpsimd.memset(keep[:].rearrange("p h (c s) -> p (h c) s", s=HC)[:, :, 0:1], 0.0).then_inc(pool_set, 1)
            po.wait_ge(stage, 3 * marks["moe"])
            po.dma_start(ye[:], A["ffn_norm_2"][1, :].partition_broadcast(P)).then_inc(ye_in, 16)
            po.dma_start(wr[:].rearrange("p (k e) -> p k e", e=E),
                         A["moe_router_2"][0].rearrange("(k p) e -> p k e", p=P)).then_inc(wr_in, 16)
            po.wait_ge(stage, 3 * marks["final"])
            po.dma_start(uT[:, 0:4, :].rearrange("p a b -> p (a b)"), A["final_norm_2"].partition_broadcast(P)).then_inc(final_in, 16)


_INS = ["x", "a_norm", "a_w_in", "a_conv_w", "a_conv_b", "a_gate_w", "a_gate_b", "a_lambda", "a_w_out", "kv_norm",
        "kv_w", "k_norm", "cmp_pos", "cmp_w1", "cmp_b1", "cmp_w2", "cmp_b2", "b_norm", "b_w_in", "b_gate_b", "q_norm",
        "b_w_out", "f_norm", "f_w_in", "f_w_out", "mix_norm_2", "w_in_2", "hgrn_lb_logits_2", "hgrn_out_norm_2",
        "w_branch_hgrn_2", "w_branch_sb_2", "w_out_2", "ffn_norm_2", "dense_w_gate_2", "dense_w_up_2",
        "dense_w_down_2", "moe_router_2", "moe_w_gate_2", "moe_w_up_2", "moe_w_down_2", "final_norm_2"]


def kernel(**inputs):
    import concourse.bacc as bacc
    from concourse.bass_utils import run_bass_kernel_spmd

    nc = bacc.Bacc("TRN2", target_bir_lowering=False, num_devices=1)
    arrays = {name: np.ascontiguousarray(inputs[name]) for name in _INS}
    arrays["const_f32"], arrays["const_masks"] = CONST_F32, CONST_MASKS
    aps = {name: nc.dram_tensor(f"in_{name}", a.shape, mybir.dt.from_np(a.dtype), kind="ExternalInput").ap()
           for name, a in arrays.items()}
    out = nc.dram_tensor("out", (1, S, D), F32, kind="ExternalOutput").ap()
    build(nc, aps, out)
    r = run_bass_kernel_spmd(nc, [{f"in_{name}": a for name, a in arrays.items()}], core_ids=[0])
    return r.results[0]["out"]
```
